# Optimizing a Trainium2 kernel written in Bass

```python
import jax, jax.numpy as jnp
from jax import lax
import numpy as np
import math

D_MODEL = 1024
BATCH = 1
SEQ = 512
DEPTH = 1

CHUNK = 64
D_MIX = D_MODEL
SSD_HEADS = 8
SSD_HEAD_DIM = 64
SSD_INNER = SSD_HEADS * SSD_HEAD_DIM
SSD_GROUPS = 2
SSD_STATE = 128
CONV_WIDTH = 4
SSD_CONV_DIM = SSD_INNER + 2 * SSD_GROUPS * SSD_STATE
ATT_HEADS = 8
ATT_HEAD_DIM = 64
ATT_INNER = ATT_HEADS * ATT_HEAD_DIM
Q_BLOCK = 128
N_EXPERT_GROUPS = 4
EXPERTS_PER_GROUP = 4
N_EXPERTS = N_EXPERT_GROUPS * EXPERTS_PER_GROUP
TOP_K = 2
D_FF_EXPERT = 512
DEEPNORM_ALPHA = (2.0 * DEPTH) ** 0.25
DEEPNORM_BETA = (8.0 * DEPTH) ** -0.25
LN_EPS = 1e-5
RMS_EPS = 1e-5
IN_SIZES = (SSD_INNER, SSD_CONV_DIM, SSD_HEADS, ATT_INNER, ATT_INNER, ATT_INNER, ATT_HEADS)
D_IN_PROJ = SSD_INNER + SSD_CONV_DIM + SSD_HEADS + 3 * ATT_INNER + ATT_HEADS


def _split_cols(u, sizes):
    idx = np.cumsum(np.array(sizes))[:-1].tolist()
    return jnp.split(u, idx, axis=-1)

def _layer_norm(u, g, b):
    uf = u.astype(jnp.float32)
    mu = jnp.mean(uf, axis=-1, keepdims=True)
    var = jnp.mean(jnp.square(uf - mu), axis=-1, keepdims=True)
    return ((uf - mu) * lax.rsqrt(var + LN_EPS) * g + b).astype(u.dtype)

def _causal_dwconv(u, w, b):
    s = u.shape[1]
    up = jnp.pad(u, ((0, 0), (CONV_WIDTH - 1, 0), (0, 0)))
    out = b
    for k in range(CONV_WIDTH):
        out = out + up[:, k:k + s, :] * w[k]
    return out

def _ssd_scan(xs, dt, a, bm, cm, d_skip):
    f32 = jnp.float32
    xs, dt, bm, cm = xs.astype(f32), dt.astype(f32), bm.astype(f32), cm.astype(f32)
    b, s, h, p = xs.shape
    nc = s // CHUNK
    r = h // SSD_GROUPS
    xdt = (xs * dt[..., None]).reshape(b, nc, CHUNK, SSD_GROUPS, r, p)
    da = (dt * a.astype(f32)).reshape(b, nc, CHUNK, SSD_GROUPS, r)
    bc = bm.reshape(b, nc, CHUNK, SSD_GROUPS, SSD_STATE)
    cc = cm.reshape(b, nc, CHUNK, SSD_GROUPS, SSD_STATE)
    a_cum = jnp.cumsum(da, axis=2)
    seg = a_cum[:, :, :, None] - a_cum[:, :, None, :]
    tri = jnp.tril(jnp.ones((CHUNK, CHUNK), dtype=bool))[None, None, :, :, None, None]
    lmat = jnp.exp(jnp.where(tri, seg, -jnp.inf))
    cb = jnp.einsum('bclgn,bcsgn->bclsg', cc, bc)
    y_diag = jnp.einsum('bclsg,bclsgr,bcsgrp->bclgrp', cb, lmat, xdt)
    decay_to_end = jnp.exp(a_cum[:, :, -1:] - a_cum)
    chunk_states = jnp.einsum('bclgn,bclgr,bclgrp->bcgrpn', bc, decay_to_end, xdt)
    chunk_decay = jnp.exp(a_cum[:, :, -1])

    def step(state, inp):
        st, dec = inp
        return state * dec[..., None, None] + st, state

    init = jnp.zeros((b, SSD_GROUPS, r, p, SSD_STATE), f32)
    _, states_in = lax.scan(step, init, (jnp.moveaxis(chunk_states, 1, 0),
                                         jnp.moveaxis(chunk_decay, 1, 0)))
    states_in = jnp.moveaxis(states_in, 0, 1)
    y_off = jnp.einsum('bclgn,bcgrpn,bclgr->bclgrp', cc, states_in, jnp.exp(a_cum))
    y = (y_diag + y_off).reshape(b, s, h, p)
    return y + xs * d_skip.astype(f32)[:, None]

def _forgetting_attention(q, k, v, log_f):
    b, s, h, d = q.shape
    fcum = jnp.transpose(jnp.cumsum(log_f, axis=1), (0, 2, 1))
    scale = d ** -0.5
    outs = []
    for blk in range(s // Q_BLOCK):
        q0, q1 = blk * Q_BLOCK, (blk + 1) * Q_BLOCK
        logits = jnp.einsum('bqhd,bkhd->bhqk', q[:, q0:q1], k[:, :q1]).astype(jnp.float32) * scale
        logits = logits + fcum[:, :, q0:q1, None] - fcum[:, :, None, :q1]
        qpos = jnp.arange(q0, q1)[:, None]
        kpos = jnp.arange(q1)[None, :]
        logits = jnp.where(qpos >= kpos, logits, -jnp.inf)
        probs = jax.nn.softmax(logits, axis=-1)
        outs.append(jnp.einsum('bhqk,bkhd->bqhd', probs.astype(v.dtype), v[:, :q1]))
    return jnp.concatenate(outs, axis=1)

def _hybrid_mixer(h, w_in, b_in, conv_w, conv_b, a_log, d_skip, ssd_norm_g, w_out):
    bsz, s, _ = h.shape
    proj = jnp.einsum('bsd,de->bse', h, w_in) + b_in
    z, xbc, dt_raw, q, k, v, f_raw = _split_cols(proj, IN_SIZES)
    xbc = jax.nn.silu(_causal_dwconv(xbc, conv_w, conv_b))
    xs, bm, cm = _split_cols(xbc, (SSD_INNER, SSD_GROUPS * SSD_STATE, SSD_GROUPS * SSD_STATE))
    xs = xs.reshape(bsz, s, SSD_HEADS, SSD_HEAD_DIM)
    bm = bm.reshape(bsz, s, SSD_GROUPS, SSD_STATE)
    cm = cm.reshape(bsz, s, SSD_GROUPS, SSD_STATE)
    dt = jax.nn.softplus(dt_raw.astype(jnp.float32))
    a = -jnp.exp(a_log.astype(jnp.float32))
    y = _ssd_scan(xs, dt, a, bm, cm, d_skip).reshape(bsz, s, SSD_INNER)
    y = (y * jax.nn.silu(z.astype(jnp.float32))).reshape(bsz, s, SSD_GROUPS, SSD_INNER // SSD_GROUPS)
    y = y * lax.rsqrt(jnp.mean(jnp.square(y), axis=-1, keepdims=True) + RMS_EPS)
    y_ssd = (y.reshape(bsz, s, SSD_INNER) * ssd_norm_g).astype(h.dtype)
    q = q.reshape(bsz, s, ATT_HEADS, ATT_HEAD_DIM)
    k = k.reshape(bsz, s, ATT_HEADS, ATT_HEAD_DIM)
    v = v.reshape(bsz, s, ATT_HEADS, ATT_HEAD_DIM)
    log_f = jax.nn.log_sigmoid(f_raw.astype(jnp.float32))
    y_att = _forgetting_attention(q, k, v, log_f).reshape(bsz, s, ATT_INNER)
    merged = jnp.concatenate([y_ssd, y_att.astype(h.dtype)], axis=-1)
    return jnp.einsum('bse,ed->bsd', merged, w_out)

def _hier_moe(h, rg_w, rg_b, re_w, re_b, w_gate, w_up, w_down):
    bsz, s, d = h.shape
    hf = h.reshape(bsz * s, d)
    g_logits = (hf @ rg_w + rg_b).astype(jnp.float32)
    g_val, g_idx = lax.top_k(jax.nn.softmax(g_logits, axis=-1), 1)
    g_val, g_idx = g_val[:, 0], g_idx[:, 0]
    e_all = (jnp.einsum('td,gde->tge', hf, re_w) + re_b).astype(jnp.float32)
    e_logits = jnp.take_along_axis(e_all, g_idx[:, None, None], axis=1)[:, 0]
    e_val, e_idx = lax.top_k(jax.nn.softmax(e_logits, axis=-1), TOP_K)
    e_val = e_val / jnp.sum(e_val, axis=-1, keepdims=True)
    weights = g_val[:, None] * e_val
    expert_id = g_idx[:, None] * EXPERTS_PER_GROUP + e_idx
    combine = jnp.sum(jax.nn.one_hot(expert_id, N_EXPERTS, dtype=jnp.float32) * weights[..., None], axis=1)
    out = jnp.zeros((bsz * s, d), jnp.float32)
    for e in range(N_EXPERTS):
        act = jax.nn.silu(hf @ w_gate[e]) * (hf @ w_up[e])
        out = out + combine[:, e:e + 1] * (act @ w_down[e]).astype(jnp.float32)
    return out.astype(h.dtype).reshape(bsz, s, d)

def first_inputs(seed: int = 0) -> dict:
    key = jax.random.key(seed)
    ks = jax.random.split(key, 20)
    f32 = jnp.float32
    x = jax.random.normal(ks[0], (BATCH, SEQ, D_MODEL), f32)
    col_scale = np.concatenate([
        np.ones(SSD_INNER + SSD_CONV_DIM), np.full(SSD_HEADS, 0.1),
        np.ones(2 * ATT_INNER), np.full(ATT_INNER, DEEPNORM_BETA), np.full(ATT_HEADS, 0.1)]).astype(np.float32)
    w_in = jax.random.normal(ks[1], (DEPTH, D_MODEL, D_IN_PROJ), f32) * (D_MODEL ** -0.5) * jnp.asarray(col_scale)
    b_in = 0.01 * jax.random.normal(ks[2], (DEPTH, D_IN_PROJ), f32)
    dt0 = jnp.exp(jax.random.uniform(ks[3], (DEPTH, SSD_HEADS), f32, np.log(1e-3), np.log(1e-1)))
    dt_bias = dt0 + jnp.log(-jnp.expm1(-dt0))
    off_dt = SSD_INNER + SSD_CONV_DIM
    b_in = b_in.at[:, off_dt:off_dt + SSD_HEADS].set(dt_bias)
    f_bias = jax.random.uniform(ks[4], (DEPTH, ATT_HEADS), f32, 1.0, 5.0)
    b_in = b_in.at[:, D_IN_PROJ - ATT_HEADS:].set(f_bias)
    conv_w = jax.random.normal(ks[5], (DEPTH, CONV_WIDTH, SSD_CONV_DIM), f32) * (CONV_WIDTH ** -0.5)
    conv_b = 0.01 * jax.random.normal(ks[6], (DEPTH, SSD_CONV_DIM), f32)
    a_log = jnp.log(jax.random.uniform(ks[7], (DEPTH, SSD_HEADS), f32, 1.0, 16.0))
    d_skip = 1.0 + 0.1 * jax.random.normal(ks[8], (DEPTH, SSD_HEADS), f32)
    ssd_norm_g = 1.0 + 0.05 * jax.random.normal(ks[9], (DEPTH, SSD_INNER), f32)
    w_out = jax.random.normal(ks[10], (DEPTH, D_MIX, D_MODEL), f32) * (D_MIX ** -0.5) * DEEPNORM_BETA
    ln1_g = 1.0 + 0.05 * jax.random.normal(ks[11], (DEPTH, D_MODEL), f32)
    ln1_b = 0.02 * jax.random.normal(ks[12], (DEPTH, D_MODEL), f32)
    router_group_w = jax.random.normal(ks[13], (DEPTH, D_MODEL, N_EXPERT_GROUPS), f32) * (D_MODEL ** -0.5)
    router_group_b = 0.01 * jax.random.normal(ks[14], (DEPTH, N_EXPERT_GROUPS), f32)
    router_expert_w = jax.random.normal(ks[15], (DEPTH, N_EXPERT_GROUPS, D_MODEL, EXPERTS_PER_GROUP), f32) * (D_MODEL ** -0.5)
    router_expert_b = 0.01 * jax.random.normal(ks[16], (DEPTH, N_EXPERT_GROUPS, EXPERTS_PER_GROUP), f32)
    kw = jax.random.split(ks[17], 3)
    w_gate = jax.random.normal(kw[0], (DEPTH, N_EXPERTS, D_MODEL, D_FF_EXPERT), f32) * (D_MODEL ** -0.5)
    w_up = jax.random.normal(kw[1], (DEPTH, N_EXPERTS, D_MODEL, D_FF_EXPERT), f32) * (D_MODEL ** -0.5)
    w_down = jax.random.normal(kw[2], (DEPTH, N_EXPERTS, D_FF_EXPERT, D_MODEL), f32) * (D_FF_EXPERT ** -0.5) * DEEPNORM_BETA
    ln2_g = 1.0 + 0.05 * jax.random.normal(ks[18], (DEPTH, D_MODEL), f32)
    ln2_b = 0.02 * jax.random.normal(ks[19], (DEPTH, D_MODEL), f32)
    return {"x": x, "w_in": w_in, "b_in": b_in, "conv_w": conv_w, "conv_b": conv_b,
            "a_log": a_log, "d_skip": d_skip, "ssd_norm_g": ssd_norm_g, "w_out": w_out,
            "ln1_g": ln1_g, "ln1_b": ln1_b, "router_group_w": router_group_w,
            "router_group_b": router_group_b, "router_expert_w": router_expert_w,
            "router_expert_b": router_expert_b, "w_gate": w_gate, "w_up": w_up,
            "w_down": w_down, "ln2_g": ln2_g, "ln2_b": ln2_b}

def first_block(x, w_in, b_in, conv_w, conv_b, a_log, d_skip, ssd_norm_g, w_out,
              ln1_g, ln1_b, router_group_w, router_group_b, router_expert_w,
              router_expert_b, w_gate, w_up, w_down, ln2_g, ln2_b):
    h = x
    for l in range(DEPTH):
        mix = _hybrid_mixer(h, w_in[l], b_in[l], conv_w[l], conv_b[l], a_log[l],
                            d_skip[l], ssd_norm_g[l], w_out[l])
        h = _layer_norm(DEEPNORM_ALPHA * h + mix, ln1_g[l], ln1_b[l])
        ffn = _hier_moe(h, router_group_w[l], router_group_b[l], router_expert_w[l],
                        router_expert_b[l], w_gate[l], w_up[l], w_down[l])
        h = _layer_norm(DEEPNORM_ALPHA * h + ffn, ln2_g[l], ln2_b[l])
    return h


DEPTH_2 = 2

N_MIXERS = 2
N_ATTN_LAYERS = (DEPTH_2 + 1) // 2
N_RWKV_LAYERS = DEPTH_2 // 2
DA_HEADS = 8
DA_HEAD_DIM = D_MODEL // (2 * DA_HEADS)
DA_QBLOCK = 128
RW_HEAD = 64
RW_HEADS = D_MODEL // RW_HEAD
RW_DECAY_LORA = max(32, int(round(1.8 * D_MODEL ** 0.5 / 32)) * 32)
RW_AAA_LORA = max(32, int(round(1.8 * D_MODEL ** 0.5 / 32)) * 32)
RW_MV_LORA = max(32, int(round(1.3 * D_MODEL ** 0.5 / 32)) * 32)
RW_GATE_LORA = max(32, int(round(0.6 * D_MODEL ** 0.8 / 32)) * 32)
RW_GN_EPS = 64e-5
MOE_GROUPS = 4
MOE_EPG = 8
MOE_EXPERTS = MOE_GROUPS * MOE_EPG
MOE_TOPK = 2
MOE_HIDDEN = D_MODEL // 2
MOE_BLOCK = 128
DEEPNORM_ALPHA_2 = (2 * DEPTH_2) ** 0.25
DEEPNORM_BETA_2 = (8 * DEPTH_2) ** -0.25


def layer_norm(x, g, b):
    xf = x.astype(jnp.float32)
    mu = jnp.mean(xf, -1, keepdims=True)
    var = jnp.mean(jnp.square(xf - mu), -1, keepdims=True)
    return ((xf - mu) * lax.rsqrt(var + LN_EPS) * g + b).astype(x.dtype)

def diff_attention(x, w_qkv, w_o, lam, subln_g, lambda_init):
    B, S, _ = x.shape
    q, k, v = jnp.split(x @ w_qkv, 3, axis=-1)
    q = q.reshape(B, S, DA_HEADS, 2, DA_HEAD_DIM)
    k = k.reshape(B, S, DA_HEADS, 2, DA_HEAD_DIM)
    v = v.reshape(B, S, DA_HEADS, 2 * DA_HEAD_DIM)
    lamf = lam.astype(jnp.float32)
    lam_full = jnp.exp(jnp.sum(lamf[0] * lamf[1])) - jnp.exp(jnp.sum(lamf[2] * lamf[3])) + lambda_init
    n_blk = S // DA_QBLOCK
    q_blocks = jnp.moveaxis(q.reshape(B, n_blk, DA_QBLOCK, DA_HEADS, 2, DA_HEAD_DIM), 1, 0)
    k_pos = jnp.arange(S)
    scale = DA_HEAD_DIM ** -0.5

    def one_block(args):
        q_blk, blk = args
        s = jnp.einsum('bqhcd,bkhcd->bhcqk', q_blk, k).astype(jnp.float32) * scale
        q_pos = blk * DA_QBLOCK + jnp.arange(DA_QBLOCK)
        causal = k_pos[None, :] <= q_pos[:, None]
        p = jax.nn.softmax(jnp.where(causal, s, -jnp.inf), axis=-1)
        attn = p[:, :, 0] - lam_full * p[:, :, 1]
        return jnp.einsum('bhqk,bkhe->bqhe', attn.astype(v.dtype), v)

    o = lax.map(one_block, (q_blocks, jnp.arange(n_blk)))
    o = jnp.moveaxis(o, 0, 1).reshape(B, S, DA_HEADS, 2 * DA_HEAD_DIM).astype(jnp.float32)
    o = o * lax.rsqrt(jnp.mean(o * o, -1, keepdims=True) + RMS_EPS) * subln_g * (1.0 - lambda_init)
    return o.reshape(B, S, D_MODEL).astype(x.dtype) @ w_o

def wkv7_scan(r, decay, k, v, a_vec, b_vec):
    B, S, H, N = r.shape

    def step(state, inp):
        r_t, w_t, k_t, v_t, a_t, b_t = inp
        sa = jnp.einsum('bhij,bhj->bhi', state, a_t)
        state = (state * w_t[:, :, None, :] + sa[..., None] * b_t[:, :, None, :]
                 + v_t[..., None] * k_t[:, :, None, :])
        return state, jnp.einsum('bhij,bhj->bhi', state, r_t)

    xs = tuple(jnp.moveaxis(t, 1, 0) for t in (r, decay, k, v, a_vec, b_vec))
    _, ys = lax.scan(step, jnp.zeros((B, H, N, N), jnp.float32), xs)
    return jnp.moveaxis(ys, 0, 1)

def rwkv7_time_mix(x, mu, w_rkv, w_o, w0, w1, w2, a0, a1, a2, g1, g2, k_k, k_a, r_k,
                   lnx_g, lnx_b, v_first, value_mix):
    B, S, D = x.shape
    H, N = RW_HEADS, RW_HEAD
    xx = jnp.pad(x, ((0, 0), (1, 0), (0, 0)))[:, :-1] - x
    xm = x[None] + xx[None] * mu[:, None, None, :]
    r, k, v = jnp.einsum('nbsd,nde->nbse', xm[:3], w_rkv)
    xv, xw, xa, xg = xm[2], xm[3], xm[4], xm[5]
    w = -jax.nn.softplus(-(w0 + jnp.tanh(xw @ w1) @ w2)) - 0.5
    if value_mix is None:
        v_first = v
    else:
        v0, v1, v2 = value_mix
        v = v + (v_first - v) * jax.nn.sigmoid(v0 + (xv @ v1) @ v2)
    a = jax.nn.sigmoid(a0 + (xa @ a1) @ a2)
    g = jax.nn.sigmoid(xg @ g1) @ g2
    kk = (k * k_k).reshape(B, S, H, N).astype(jnp.float32)
    kk = kk / jnp.maximum(jnp.sqrt(jnp.sum(kk * kk, -1, keepdims=True)), 1e-12)
    k = k * (1.0 + (a - 1.0) * k_a)
    rh, kh, vh, ah = [t.reshape(B, S, H, N).astype(jnp.float32) for t in (r, k, v, a)]
    decay = jnp.exp(-jnp.exp(w.reshape(B, S, H, N).astype(jnp.float32)))
    y = wkv7_scan(rh, decay, kh, vh, -kk, kk * ah)
    ym = jnp.mean(y, -1, keepdims=True)
    yv = jnp.mean(jnp.square(y - ym), -1, keepdims=True)
    y = (y - ym) * lax.rsqrt(yv + RW_GN_EPS) * lnx_g.reshape(H, N) + lnx_b.reshape(H, N)
    y = y + jnp.sum(rh * kh * r_k, -1, keepdims=True) * vh
    out = (y.reshape(B, S, D).astype(x.dtype) * g) @ w_o
    return out, v_first

def hier_moe(x, rg_w, rg_b, re_w, re_b, w_gu, w_down):
    B, S, D = x.shape
    n_tok = B * S
    t = x.reshape(n_tok, D)
    g_prob = jax.nn.softmax((t @ rg_w + rg_b).astype(jnp.float32), axis=-1)
    g_p, g_idx = lax.top_k(g_prob, 1)
    e_logits = (t @ re_w + re_b).astype(jnp.float32).reshape(n_tok, MOE_GROUPS, MOE_EPG)
    e_logits = jnp.take_along_axis(e_logits, g_idx[:, :, None], axis=1)[:, 0]
    e_p, e_idx = lax.top_k(jax.nn.softmax(e_logits, axis=-1), MOE_TOPK)
    e_p = e_p / jnp.sum(e_p, -1, keepdims=True)
    gate = (g_p * e_p).reshape(-1)
    expert = (g_idx * MOE_EPG + e_idx).reshape(-1).astype(jnp.int32)
    tok = jnp.repeat(jnp.arange(n_tok, dtype=jnp.int32), MOE_TOPK)
    n_assign = n_tok * MOE_TOPK
    order = jnp.argsort(expert)
    e_sorted, tok_sorted, gate_sorted = expert[order], tok[order], gate[order]
    counts = jnp.bincount(expert, length=MOE_EXPERTS).astype(jnp.int32)
    padded = (counts + MOE_BLOCK - 1) // MOE_BLOCK * MOE_BLOCK
    pad_end = jnp.cumsum(padded)
    pad_start = pad_end - padded
    start = jnp.cumsum(counts) - counts
    dest = pad_start[e_sorted] + jnp.arange(n_assign, dtype=jnp.int32) - start[e_sorted]
    n_blocks = -(-n_assign // MOE_BLOCK) + MOE_EXPERTS
    n_rows = n_blocks * MOE_BLOCK
    tok_buf = jnp.full((n_rows,), n_tok, jnp.int32).at[dest].set(tok_sorted)
    gate_buf = jnp.zeros((n_rows,), jnp.float32).at[dest].set(gate_sorted)
    t_pad = jnp.concatenate([t, jnp.zeros((1, D), t.dtype)], axis=0)
    x_buf = t_pad[tok_buf].reshape(n_blocks, MOE_BLOCK, D)
    block_e = jnp.minimum(jnp.searchsorted(pad_end, jnp.arange(n_blocks) * MOE_BLOCK, side='right'),
                          MOE_EXPERTS - 1)

    def expert_block(args):
        xb, e = args
        hg, hu = jnp.split(xb @ w_gu[e], 2, axis=-1)
        return (jax.nn.silu(hg) * hu) @ w_down[e]

    y = lax.map(expert_block, (x_buf, block_e)).reshape(n_rows, D)
    y = y * gate_buf[:, None].astype(y.dtype)
    out = jax.ops.segment_sum(y, tok_buf, num_segments=n_tok + 1)[:n_tok]
    return out.reshape(B, S, D)

def second_inputs(seed: int = 0) -> dict:
    key = jax.random.key(seed)
    k = jax.random.split(key, 34)
    D, L, NA, NR = D_MODEL, DEPTH_2, N_ATTN_LAYERS, N_RWKV_LAYERS
    H, N = RW_HEADS, RW_HEAD
    f32 = jnp.float32

    def nrm(i, shape, scale):
        return scale * jax.random.normal(k[i], shape, f32)

    def unif(i, shape, lo, hi):
        return jax.random.uniform(k[i], shape, f32, lo, hi)

    return {
        'x': nrm(0, (BATCH, SEQ, D), 1.0),
        'ln1_g': 1.0 + nrm(1, (L, D), 0.02),
        'ln1_b': nrm(2, (L, D), 0.02),
        'ln2_g': 1.0 + nrm(3, (L, D), 0.02),
        'ln2_b': nrm(4, (L, D), 0.02),
        'attn_w_qkv': nrm(5, (NA, D, 3 * D), D ** -0.5),
        'attn_w_o': nrm(6, (NA, D, D), DEEPNORM_BETA_2 * D ** -0.5),
        'attn_lambda': nrm(7, (NA, 4, DA_HEAD_DIM), 0.1),
        'attn_subln_g': 1.0 + nrm(8, (NA, 2 * DA_HEAD_DIM), 0.02),
        'rw_mu': unif(9, (NR, 6, D), 0.0, 1.0),
        'rw_w_rkv': nrm(10, (NR, 3, D, D), D ** -0.5),
        'rw_w_o': nrm(11, (NR, D, D), DEEPNORM_BETA_2 * D ** -0.5),
        'rw_w0': unif(12, (NR, D), -6.0, -1.0),
        'rw_w1': nrm(13, (NR, D, RW_DECAY_LORA), D ** -0.5),
        'rw_w2': nrm(14, (NR, RW_DECAY_LORA, D), 0.1 * RW_DECAY_LORA ** -0.5),
        'rw_a0': nrm(15, (NR, D), 0.1),
        'rw_a1': nrm(16, (NR, D, RW_AAA_LORA), D ** -0.5),
        'rw_a2': nrm(17, (NR, RW_AAA_LORA, D), 0.5 * RW_AAA_LORA ** -0.5),
        'rw_g1': nrm(18, (NR, D, RW_GATE_LORA), D ** -0.5),
        'rw_g2': nrm(19, (NR, RW_GATE_LORA, D), RW_GATE_LORA ** -0.5),
        'rw_k_k': 0.85 + nrm(20, (NR, D), 0.02),
        'rw_k_a': 1.0 + nrm(21, (NR, D), 0.02),
        'rw_r_k': nrm(22, (NR, H, N), 0.1),
        'rw_lnx_g': 1.0 + nrm(23, (NR, D), 0.02),
        'rw_lnx_b': nrm(24, (NR, D), 0.02),
        'rw_v0': 1.0 + nrm(25, (NR - 1, D), 0.1),
        'rw_v1': nrm(26, (NR - 1, D, RW_MV_LORA), D ** -0.5),
        'rw_v2': nrm(27, (NR - 1, RW_MV_LORA, D), 0.5 * RW_MV_LORA ** -0.5),
        'moe_rg_w': nrm(28, (L, D, MOE_GROUPS), D ** -0.5),
        'moe_rg_b': nrm(29, (L, MOE_GROUPS), 0.01),
        'moe_re_w': nrm(30, (L, D, MOE_EXPERTS), D ** -0.5),
        'moe_re_b': nrm(31, (L, MOE_EXPERTS), 0.01),
        'moe_w_gu': nrm(32, (L, MOE_EXPERTS, D, 2 * MOE_HIDDEN), D ** -0.5),
        'moe_w_down': nrm(33, (L, MOE_EXPERTS, MOE_HIDDEN, D), DEEPNORM_BETA_2 * MOE_HIDDEN ** -0.5),
    }

def second_block(x, ln1_g, ln1_b, ln2_g, ln2_b, attn_w_qkv, attn_w_o, attn_lambda, attn_subln_g,
              rw_mu, rw_w_rkv, rw_w_o, rw_w0, rw_w1, rw_w2, rw_a0, rw_a1, rw_a2, rw_g1, rw_g2,
              rw_k_k, rw_k_a, rw_r_k, rw_lnx_g, rw_lnx_b, rw_v0, rw_v1, rw_v2,
              moe_rg_w, moe_rg_b, moe_re_w, moe_re_b, moe_w_gu, moe_w_down):
    v_first = None
    for i in range(DEPTH_2):
        j = i // N_MIXERS
        if i % N_MIXERS == 0:
            lambda_init = 0.8 - 0.6 * math.exp(-0.3 * i)
            h = diff_attention(x, attn_w_qkv[j], attn_w_o[j], attn_lambda[j], attn_subln_g[j], lambda_init)
        else:
            value_mix = None if j == 0 else (rw_v0[j - 1], rw_v1[j - 1], rw_v2[j - 1])
            h, v_first = rwkv7_time_mix(x, rw_mu[j], rw_w_rkv[j], rw_w_o[j], rw_w0[j], rw_w1[j], rw_w2[j],
                                        rw_a0[j], rw_a1[j], rw_a2[j], rw_g1[j], rw_g2[j], rw_k_k[j],
                                        rw_k_a[j], rw_r_k[j], rw_lnx_g[j], rw_lnx_b[j], v_first, value_mix)
        x = layer_norm(DEEPNORM_ALPHA_2 * x + h, ln1_g[i], ln1_b[i])
        f = hier_moe(x, moe_rg_w[i], moe_rg_b[i], moe_re_w[i], moe_re_b[i], moe_w_gu[i], moe_w_down[i])
        x = layer_norm(DEEPNORM_ALPHA_2 * x + f, ln2_g[i], ln2_b[i])
    return x


def setup_inputs(seed=0):
    out = dict(first_inputs(seed))
    for name, value in second_inputs(seed + 1).items():
        if name != "x":
            out[name + "_2"] = value
    return out


def reference(
    x, w_in, b_in, conv_w, conv_b, a_log, d_skip, ssd_norm_g, w_out, ln1_g, ln1_b,
    router_group_w, router_group_b, router_expert_w, router_expert_b, w_gate, w_up, w_down,
    ln2_g, ln2_b, ln1_g_2, ln1_b_2, ln2_g_2, ln2_b_2, attn_w_qkv_2, attn_w_o_2, attn_lambda_2,
    attn_subln_g_2, rw_mu_2, rw_w_rkv_2, rw_w_o_2, rw_w0_2, rw_w1_2, rw_w2_2, rw_a0_2, rw_a1_2,
    rw_a2_2, rw_g1_2, rw_g2_2, rw_k_k_2, rw_k_a_2, rw_r_k_2, rw_lnx_g_2, rw_lnx_b_2, rw_v0_2,
    rw_v1_2, rw_v2_2, moe_rg_w_2, moe_rg_b_2, moe_re_w_2, moe_re_b_2, moe_w_gu_2, moe_w_down_2,
):
    x = first_block(
        x, w_in, b_in, conv_w, conv_b, a_log, d_skip, ssd_norm_g, w_out, ln1_g, ln1_b,
        router_group_w, router_group_b, router_expert_w, router_expert_b, w_gate, w_up, w_down,
        ln2_g, ln2_b,
    )
    return second_block(
        x, ln1_g_2, ln1_b_2, ln2_g_2, ln2_b_2, attn_w_qkv_2, attn_w_o_2, attn_lambda_2,
        attn_subln_g_2, rw_mu_2, rw_w_rkv_2, rw_w_o_2, rw_w0_2, rw_w1_2, rw_w2_2, rw_a0_2,
        rw_a1_2, rw_a2_2, rw_g1_2, rw_g2_2, rw_k_k_2, rw_k_a_2, rw_r_k_2, rw_lnx_g_2,
        rw_lnx_b_2, rw_v0_2, rw_v1_2, rw_v2_2, moe_rg_w_2, moe_rg_b_2, moe_re_w_2, moe_re_b_2,
        moe_w_gu_2, moe_w_down_2,
    )


_drawn_inputs = setup_inputs


def setup_inputs(seed=0):
    import zlib

    import numpy as np

    out = dict(_drawn_inputs(seed))
    spreads = {}
    factors = {'conv_b': 3.993,
     'router_group_b': 5.462,
     'router_expert_b': 5.397,
     'attn_subln_g_2': 6.278,
     'rw_w1_2': 8.0,
     'rw_w2_2': 8.0,
     'rw_a0_2': 5.613,
     'rw_k_k_2': 8.0,
     'rw_k_a_2': 8.0,
     'rw_lnx_g_2': 22.646,
     'rw_lnx_b_2': 23.475,
     'moe_rg_b_2': 6.131,
     'moe_re_b_2': 6.286}
    for name, (base, spread) in spreads.items():
        noise = np.random.default_rng([zlib.crc32(name.encode()), seed]).standard_normal(out[name].shape)
        drawn = base * np.exp(spread * noise) if base else spread * noise
        out[name] = __import__('jax').numpy.asarray(drawn.astype(out[name].dtype))
    for name, factor in factors.items():
        out[name] = (out[name] * factor).astype(out[name].dtype)
    return out
```

```python
from contextlib import ExitStack

import numpy as np

import concourse.bass as bass
from concourse import mybir

F32 = mybir.dt.float32
I32 = mybir.dt.int32
U32 = mybir.dt.uint32
ALU = mybir.AluOpType
ACT = mybir.ActivationFunctionType
AX = mybir.AxisListType.X

P = 128
T = 512
D = 1024
NT = T // P
NK = D // P
CH = 512
SLOTS = 6
LN_EPS = 1e-5
RMS_EPS = 1e-5
NEG = -1e30
BLK = 32

HEADS = 8
HD = 64
STATE = 128
GROUPS = 2
CONV_W = 4
O_Z, O_XS, O_BC, O_DT, O_Q, O_K, O_V, O_F = 0, 512, 1024, 1536, 1544, 2056, 2568, 3080
F_ROW = 32
ALPHA_1 = 2.0 ** 0.25
ALPHA_2 = 4.0 ** 0.25
SCALE = HD ** -0.5
LAMBDA_INIT = 0.8 - 0.6
DA_HEADS = 8

RC = 64
NC_R = T // RC
RB = 32
DECAY_LORA, AAA_LORA, GATE_LORA = 64, 64, 160
GN_EPS = 64e-5


class Signal:

    def __init__(self, sem):
        self.sem = sem
        self.total = 0

    def take(self, n):
        base = self.total
        self.total += n
        return base


class Chain:

    def __init__(self, eng, steps):
        self.eng, self.steps = eng, steps

    def __call__(self, ins):
        self.steps.total += 1
        ins.then_inc(self.steps.sem, 1)
        self.eng.wait_ge(self.steps.sem, self.steps.total)


def build(nc, a, out, stop=None):
    ctx = ExitStack()
    with ctx:
        def sb(name, cols, dt=F32):
            return ctx.enter_context(nc.sbuf_tensor(name, [P, cols], dt))

        def signal(name):
            return Signal(ctx.enter_context(nc.semaphore(name)))

        ring = sb("ring", SLOTS * NK * CH)
        x_tok = sb("x_tok", NT * D)[:, :].rearrange("p (j d) -> p j d", j=NT)
        xt_mem = sb("xt_mem", NK * T)
        xT = xt_mem[:, :].rearrange("p (k t) -> p k t", k=NK)
        arena = sb("arena", 16448)
        rows = sb("rows", 2 * D)
        cst = sb("cst", 8 * P + BLK + 64)
        small = sb("small", 760)
        ps = ctx.enter_context(nc.psum_tensor("ps", [P, 8, 512], F32))
        ybuf = nc.dram_tensor("ybuf", [(2 * T // BLK + 32) * BLK, D], F32).ap()

        def const(n, w=P):
            return cst[:, n * P:n * P + w]

        ident, mask_qk, mask_sq, before, ones, low_ts, low_st, upto_st = (const(n) for n in range(8))
        iota_f = cst[:, 8 * P:8 * P + BLK]
        cols = cst[:, 8 * P + BLK:8 * P + BLK + 64]
        eps_ln = cols[:, 0:1]
        one_col = cols[:, 1:2]
        eps_gn = cols[:, 2:3]

        def view(mem, at, *shape):
            n = int(np.prod(shape))
            v = mem[:, at:at + n]
            if len(shape) == 2:
                return v.rearrange("p (a b) -> p a b", a=shape[0])
            if len(shape) == 3:
                return v.rearrange("p (a b c) -> p a b c", a=shape[0], b=shape[1])
            return v

        def slot(n):
            return ring[:, n * NK * CH:(n + 1) * NK * CH]

        arrived = [signal(f"chunk_arrived{n}") for n in range(SLOTS)]
        loaded = signal("params_loaded")
        x_loaded = signal("x_loaded")
        zeroed = signal("ybuf_zeroed")
        consts = signal("consts_ready")
        mm = signal("matmuls_done")
        tr = signal("transposes_done")
        ev = signal("act_evacuated")
        dv = signal("dve_evacuated")
        dve_chain = signal("dve_chain")
        act_chain = signal("act_chain")
        pool_chain = signal("pool_chain")
        ln_done = signal("ln_done")
        stat = signal("variance_ready")
        sq = signal("deviation_ready")
        stored = signal("output_stored")
        pe_a = signal("pe_a_done")
        pe_b = signal("pe_b_done")
        pe_c = signal("pe_c_done")
        act_a = signal("act_a_done")
        act_b = signal("act_b_done")
        dve_a = signal("dve_a_done")
        dve_b = signal("dve_b_done")
        dve_c = signal("dve_c_done")

        def cols_of(w, c0):
            return w.rearrange("(k p) n -> p k n", p=P)[:, :, c0:c0 + CH]

        def layer_chunks(ws):
            return [cols_of(w, c) for w, cs in ws for c in cs]

        w_in, w_out = a["w_in"][0], a["w_out"][0]
        w_qkv, w_o2 = a["attn_w_qkv_2"][0], a["attn_w_o_2"][0]
        rkv, w_o3 = a["rw_w_rkv_2"][0], a["rw_w_o_2"][0]
        stream = []
        mixer_at, moe_at = [], []
        n_experts = [16, 32, 32]
        for n, ws in enumerate((
                [(w_in, (O_Z, O_XS, O_BC, O_Q, O_K, O_V)), (w_out, (0, CH))],
                [(w_qkv, range(0, 3 * D, CH)), (w_o2, (0, CH))],
                [(rkv[0], (0, CH)), (rkv[1], (0, CH)), (rkv[2], (0, CH)), (w_o3, (0, CH))])):
            mixer_at.append(len(stream))
            stream += layer_chunks(ws)
            moe_at.append(len(stream))
            stream += [None] * (3 * n_experts[n])

        def chunk_dst(src, n):
            return slot(n % SLOTS).rearrange("p (k n) -> p k n", k=src.shape[1])

        def load_chunk(eng, n):
            eng.dma_start(chunk_dst(stream[n], n), stream[n]).then_inc(arrived[n % SLOTS].sem, 16)

        def wait_chunk(eng, n):
            eng.wait_ge(arrived[n % SLOTS].sem, 16 * (n // SLOTS + 1))

        gu = a["moe_w_gu_2"]
        gate_src = [a["w_gate"][0], gu[0][:, :, 0:CH], gu[1][:, :, 0:CH]]
        up_src = [a["w_up"][0], gu[0][:, :, CH:D], gu[1][:, :, CH:D]]
        down_src = [a["w_down"][0], a["moe_w_down_2"][0], a["moe_w_down_2"][1]]

        def kinds(n):
            return (0, 1, 2) if n % SLOTS != SLOTS - 1 else (2, 0, 1)

        def load_expert_chunk(eng, l, e, j, n):
            src = (gate_src, up_src, down_src)[kinds(n - j)[j]][l][bass.ds(e, 1), :, :] \
                .rearrange("e (k p) n -> p (e k) n", p=P)
            eng.dma_start(chunk_dst(src, n), src).then_inc(arrived[n % SLOTS].sem, 16)

        used = {}

        def stream_mixer(sp, first, last):
            for n in range(first, last):
                if n - SLOTS in used:
                    sp.wait_ge(*used[n - SLOTS])
                if stream[n] is not None:
                    load_chunk(sp, n)
                else:
                    l = max(i for i in range(3) if moe_at[i] <= n)
                    load_expert_chunk(sp, l, (n - moe_at[l]) // 3, (n - moe_at[l]) % 3, n)

        def transpose_stage(src, dst):
            t0 = tr.take(NK)
            with nc.Block() as block:
                @block.tensor
                def _(pe):
                    for k in range(NK):
                        for j in range(NT):
                            ins = pe.transpose(ps[:, k, j * P:(j + 1) * P], src(j, k), ident)
                        ins.then_inc(tr.sem, 1)

                @block.scalar
                def _(act):
                    for k in range(0, NK, 2):
                        act.wait_ge(tr.sem, t0 + k + 1)
                        act.activation(dst[:, k, :], ps[:, k, :], ACT.Copy)

                @block.vector
                def _(dve):
                    for k in range(1, NK, 2):
                        dve.wait_ge(tr.sem, t0 + k + 1)
                        dve.tensor_copy(dst[:, k, :], ps[:, k, :])

        mean_var = view(small, 0, 32)
        g_row, b_row = view(rows, 0, D), view(rows, D, D)

        def normalise(dve, link, j, sq_at):
            xj = x_tok[:, j, :]
            st = mean_var[:, 16:28]
            for c in range(2):
                ins = dve.bn_stats(st[:, 6 * c:6 * c + 6], xj[:, c * CH:(c + 1) * CH])
            link(ins)
            dve.bn_aggr(mean_var[:, 0:2], st).then_inc(stat.sem, 1)
            dve.wait_ge(sq.sem, sq_at + j + 1)
            link(dve.reciprocal(mean_var[:, 3:4], mean_var[:, 2:3]))
            link(dve.tensor_scalar(xj, xj, mean_var[:, 0:1], mean_var[:, 3:4], ALU.subtract, ALU.mult))
            link(dve.tensor_tensor(xj, xj, g_row, ALU.mult))
            link(dve.tensor_tensor(xj, xj, b_row, ALU.add))

        def deviations(act, stat_at):
            for j in range(NT):
                act.wait_ge(stat.sem, stat_at + j + 1)
                act.activation(mean_var[:, 2:3], mean_var[:, 1:2], ACT.Sqrt, bias=eps_ln).then_inc(sq.sem, 1)

        def load_norm_rows(pool, g_src, b_src):
            pool.dma_start(g_row, g_src.partition_broadcast(P)).then_inc(loaded.sem, 16)
            pool.dma_start(b_row, b_src.partition_broadcast(P)).then_inc(loaded.sem, 16)

        def project_out_stage(l, alpha, mT, g_src, b_src):
            first = moe_at[l] - 2
            m0, s0, q0, l0 = mm.take(2 * NT), stat.take(NT), sq.take(NT), loaded.take(32)
            for c in range(2):
                used[first + c] = (mm.sem, m0 + 2 * NT - 1 + c)
            with nc.Block() as block:
                @block.sync
                def _(sp):
                    stream_mixer(sp, first + SLOTS, first + SLOTS + 2)

                @block.gpsimd
                def _(pool):
                    load_norm_rows(pool, g_src, b_src)

                @block.tensor
                def _(pe):
                    for j in range(NT):
                        for c in range(2):
                            if j == 0:
                                wait_chunk(pe, first + c)
                            w = slot((first + c) % SLOTS).rearrange("p (k n) -> p k n", k=NK)
                            for k in range(NK):
                                ins = pe.matmul(ps[:, 2 * j + c, :], mT[:, k, j * P:(j + 1) * P], w[:, k, :],
                                                start=(k == 0), stop=(k == NK - 1))
                            ins.then_inc(mm.sem, 1)

                @block.scalar
                def _(act):
                    deviations(act, s0)

                @block.vector
                def _(dve):
                    link = Chain(dve, dve_chain)
                    for j in range(NT):
                        for c in range(2):
                            dve.wait_ge(mm.sem, m0 + 2 * j + c + 1)
                            xc = x_tok[:, j, c * CH:(c + 1) * CH]
                            ins = dve.scalar_tensor_tensor(xc, xc, alpha, ps[:, 2 * j + c, :],
                                                           ALU.mult, ALU.add)
                        link(ins)
                        if j == 0:
                            dve.wait_ge(loaded.sem, l0 + 32)
                        normalise(dve, link, j, q0)
            transpose_stage(lambda j, k: x_tok[:, j, k * P:(k + 1) * P], xT)

        zeros = view(arena, 14368, D)

        def start_stage():
            l0, z0 = x_loaded.take(16), consts.take(1)
            zeroed.take(16)
            with nc.Block() as block:
                @block.sync
                def _(sp):
                    sp.dma_start(x_tok, a["x"][0].rearrange("(j p) d -> p j d", p=P)).then_inc(x_loaded.sem, 16)
                    stream_mixer(sp, 0, SLOTS)
                    sp.wait_ge(x_loaded.sem, l0 + 16)

                @block.scalar
                def _(act):
                    act.wait_ge(consts.sem, z0 + 1)
                    act.dma_start(ybuf.rearrange("(r p) d -> p r d", p=P),
                                  zeros.unsqueeze(1).to_broadcast([P, ybuf.shape[0] // P, D])).then_inc(zeroed.sem, 16)

                @block.gpsimd
                def _(pool):
                    link = Chain(pool, pool_chain)
                    pool.memset(zeros, 0.0).then_inc(consts.sem, 1)

                    def select(m, fill, op, base, step, mult):
                        link(pool.affine_select(out=m, in_=m, pattern=[[step, P]], compare_op=op, fill=fill,
                                                base=base, channel_multiplier=mult))

                    for m, v in ((ident, 0.0), (mask_qk, 0.0), (mask_sq, 0.0), (before, 1.0), (ones, 1.0),
                                 (low_ts, 1.0), (low_st, 1.0), (upto_st, 1.0)):
                        pool.memset(m, v)
                    pool.memset(eps_ln, LN_EPS)
                    pool.memset(one_col, 1.0)
                    pool.memset(eps_gn, GN_EPS)
                    link(pool.iota(iota_f, pattern=[[1, BLK]], base=0, channel_multiplier=0,
                                   allow_small_or_imprecise_dtypes=True))
                    select(ident, 1.0, ALU.not_equal, 0, -1, 1)
                    select(mask_qk, NEG, ALU.is_ge, 0, -1, 1)
                    select(mask_sq, NEG, ALU.is_ge, 0, 1, -1)
                    select(before, 0.0, ALU.is_gt, 0, 1, -1)
                    select(low_ts, 0.0, ALU.is_gt, 0, -1, 1)
                    select(low_st, 0.0, ALU.is_gt, 0, 1, -1)
                    select(upto_st, 0.0, ALU.is_ge, 0, 1, -1)
                    for m in (low_st, upto_st):
                        link(pool.memset(m[0:RC, RC:P], 0.0))
                    for r in range(1, P // RB):
                        link(pool.memset(low_ts[r * RB:(r + 1) * RB, 0:r * RB], 0.0))
            transpose_stage(lambda j, k: x_tok[:, j, k * P:(k + 1) * P], xT)

        xbc = view(arena, 0, 8, 516)
        xbc_a = view(arena, 4128, 8, T)
        z_s = view(arena, 8224, NT, T)
        v_tok = view(arena, 10272, NT, T)
        qT = view(arena, 12320, 4, T)
        kT = view(arena, 14368, 4, T)
        gate_u = rows[0:64, 1024:1536]
        gate_c = rows[0:64, 1536:2048]

        def in_proj_stage():
            wsmall = view(arena, 4128, NK, 64)
            brow = rows[0:1, 0:2 * T]
            bcol = view(small, 32, 16)
            convw = view(small, 48, 8, CONV_W)
            convb = view(small, 80, 8)
            sign, bgate = small[0:64, 88:89], small[0:64, 89:90]
            b_in = a["b_in"][0]
            l0, c0, m0, e0, z0 = loaded.take(16 * 13), consts.take(1), mm.take(25), ev.take(25), dve_a.take(32)
            first = mixer_at[0]
            for c in range(6):
                used[first + c] = (mm.sem, m0 + 1 + 4 * (c + 1))
            with nc.Block() as block:
                @block.sync
                def _(sp):
                    stream_mixer(sp, first + SLOTS, first + 12)

                @block.gpsimd
                def _(pool):
                    link = Chain(pool, pool_chain)
                    pool.memset(wsmall, 0.0)
                    pool.memset(sign, -1.0)
                    pool.memset(bgate, 0.0)
                    link(pool.memset(xbc[:, :, 0:CONV_W - 1], 0.0))
                    link(pool.memset(sign[0:32, :], 1.0))

                    def load(dst, src):
                        pool.dma_start(dst, src).then_inc(loaded.sem, 16)

                    wk = w_in.rearrange("(k p) n -> p k n", p=P)
                    with nc.allow_non_contiguous_dma("bias columns"):
                        load(wsmall[:, :, 0:HEADS], wk[:, :, O_DT:O_DT + HEADS])
                        load(wsmall[:, :, F_ROW:F_ROW + HEADS], wk[:, :, O_F:O_F + HEADS])
                        load(bgate[0:HEADS, :], b_in[O_DT:O_DT + HEADS].unsqueeze(1))
                        load(bgate[F_ROW:F_ROW + HEADS, :], b_in[O_F:O_F + HEADS].unsqueeze(1))
                        load(brow[:, 0:T], b_in[O_Z:O_Z + T].unsqueeze(0))
                        load(brow[:, T:2 * T], b_in[O_V:O_V + T].unsqueeze(0))
                        load(bcol[:, 0:8], b_in[O_XS:O_XS + 8 * P].rearrange("(c p) -> p c", p=P))
                        load(bcol[:, 8:16], b_in[O_Q:O_Q + 8 * P].rearrange("(c p) -> p c", p=P))
                        for k in range(CONV_W):
                            load(convw[:, :, k], a["conv_w"][0][k].rearrange("(c p) -> p c", p=P))
                        load(convb, a["conv_b"][0].rearrange("(c p) -> p c", p=P))
                    pool.wait_ge(loaded.sem, l0 + 16 * 13)
                    pool.tensor_tensor(bgate, bgate, sign, ALU.mult).then_inc(consts.sem, 1)

                def is_tok(c):
                    return c in (0, 5)

                @block.tensor
                def _(pe):
                    pe.wait_ge(loaded.sem, l0 + 16 * 13)
                    for n in range(25):
                        if n >= 8:
                            pe.wait_ge(ev.sem, e0 + n - 7)
                        bank = ps[:, n % 8, :]
                        if n == 0:
                            for k in range(NK):
                                ins = pe.matmul(bank[0:64, :], wsmall[:, k, :], xT[:, k, :],
                                                start=(k == 0), stop=(k == NK - 1))
                            ins.then_inc(mm.sem, 1)
                            continue
                        c, j = (n - 1) // 4, (n - 1) % 4
                        if j == 0:
                            wait_chunk(pe, first + c)
                        w = slot((first + c) % SLOTS).rearrange("p (k n) -> p k n", k=NK)
                        if is_tok(c):
                            pe.matmul(bank, ones[0:1, :], brow[:, (c // 5) * T:(c // 5 + 1) * T], start=True, stop=False)
                        for k in range(NK):
                            if is_tok(c):
                                ins = pe.matmul(bank, xT[:, k, j * P:(j + 1) * P], w[:, k, :],
                                                start=False, stop=(k == NK - 1))
                            else:
                                ins = pe.matmul(bank, w[:, k, j * P:(j + 1) * P], xT[:, k, :],
                                                start=(k == 0), stop=(k == NK - 1))
                        ins.then_inc(mm.sem, 1)

                @block.scalar
                def _(act):
                    act.wait_ge(consts.sem, c0 + 1)
                    for n in range(25):
                        act.wait_ge(mm.sem, m0 + n + 1)
                        bank = ps[:, n % 8, :]
                        c, j = (n - 1) // 4, (n - 1) % 4
                        if (c, j) == (4, 0):
                            act.wait_ge(zeroed.sem, 16)
                        if n == 0:
                            ins = act.activation(gate_u, bank[0:64, :], ACT.Identity, bias=bgate, scale=sign)
                        elif c == 0:
                            ins = act.activation(z_s[:, j, :], bank, ACT.Silu)
                        elif c == 5:
                            ins = act.activation(v_tok[:, j, :], bank, ACT.Copy)
                        else:
                            dst = (xbc[:, j, 3:515], xbc[:, 4 + j, 3:515], qT[:, j, :], kT[:, j, :])[c - 1]
                            ins = act.activation(dst, bank, ACT.Identity, bias=bcol[:, 4 * (c - 1) + j:4 * (c - 1) + j + 1])
                        ins.then_inc(ev.sem, 1)
                    for c in range(8):
                        act.wait_ge(dve_a.sem, z0 + 25 + c)
                        act.activation(xbc_a[:, c, :], xbc_a[:, c, :], ACT.Silu)

                @block.vector
                def _(dve):
                    dve.wait_ge(consts.sem, c0 + 1)
                    dve.wait_ge(mm.sem, m0 + 1)
                    for k in range(CONV_W):
                        tap = CONV_W - 1 - k
                        for c in range(8):
                            if k == 0:
                                dve.wait_ge(ev.sem, e0 + 5 + c + 1)
                            else:
                                dve.wait_ge(dve_a.sem, z0 + 8 * (k - 1) + c + 1)
                            shifted = xbc[:, c, tap:tap + T]
                            if k == 0:
                                ins = dve.tensor_scalar(xbc_a[:, c, :], shifted, convw[:, c, tap:tap + 1],
                                                        convb[:, c:c + 1], ALU.mult, ALU.add)
                            else:
                                ins = dve.scalar_tensor_tensor(xbc_a[:, c, :], shifted, convw[:, c, tap:tap + 1],
                                                               xbc_a[:, c, :], ALU.mult, ALU.add)
                            ins.then_inc(dve_a.sem, 1)

        xs_tok = view(arena, 0, NT, T)
        xdt = view(arena, 2048, NT, T)
        merged_s = view(arena, 4128, NT, T)
        merged_a = view(arena, 4128 + 2048, NT, T)
        CB_AT = (0, 512, 896, 1152)
        TRI = 1280
        cb = view(xt_mem, 0, GROUPS, TRI)
        sel = view(rows, 0, HEADS, P)
        gate_c_tok = view(small, 96, NT, 64)
        gate_u_tok = view(small, 96 + 256, NT, 64)
        dskip = view(small, 620, HEADS)
        coef = small[0:64, 628:629]
        neg_c = view(small, 630, NT, HEADS)
        sumsq = view(small, 664, 32)

        def decay_stage():
            tmp = xt_mem[0:64, 3072:3584]
            l0, a0, d0 = loaded.take(32), act_a.take(6), dve_a.take(1)
            t0, b0, e0 = tr.take(5), pe_a.take(8), dve_b.take(8)
            with nc.Block() as block:
                @block.gpsimd
                def _(pool):
                    with nc.allow_non_contiguous_dma("one value per partition"):
                        pool.dma_start(coef[0:HEADS, :], a["a_log"][0].unsqueeze(1)).then_inc(loaded.sem, 16)
                    pool.dma_start(dskip, a["d_skip"][0].partition_broadcast(P)).then_inc(loaded.sem, 16)
                    pool.wait_ge(loaded.sem, l0 + 32)

                @block.scalar
                def _(act):
                    link = Chain(act, act_chain)
                    act.wait_ge(loaded.sem, l0 + 32)
                    act.activation(coef[0:HEADS, :], coef[0:HEADS, :], ACT.Exp).then_inc(act_a.sem, 1)
                    link(act.activation(tmp, gate_u, ACT.Abs))
                    link(act.activation(tmp, tmp, ACT.Exp, scale=-1.0))
                    act.activation(tmp, tmp, ACT.Ln, bias=one_col[0:64, :]).then_inc(act_a.sem, 1)
                    for j in range(NT):
                        act.wait_ge(tr.sem, t0 + j + 1)
                        act.activation(xs_tok[:, j, :], ps[:, j, :], ACT.Copy).then_inc(act_a.sem, 1)

                @block.vector
                def _(dve):
                    link = Chain(dve, dve_chain)
                    dve.wait_ge(act_a.sem, a0 + 2)
                    link(dve.tensor_scalar(gate_u, gate_u, 0.0, None, ALU.max))
                    link(dve.tensor_tensor(gate_u, gate_u, tmp, ALU.add))
                    dve.tensor_scalar(tmp[32:64, :], gate_u[32:64, :], -1.0, None, ALU.mult)
                    link(dve.tensor_scalar(tmp[0:32, :], gate_u[0:32, :], -1.0, None, ALU.mult))
                    link(dve.tensor_scalar(tmp[0:HEADS, :], tmp[0:HEADS, :], coef[0:HEADS, :], None, ALU.mult))
                    dve.tensor_tensor_scan(gate_c, ones[0:64, 0:1].to_broadcast([64, T]), tmp, 0.0,
                                           ALU.mult, ALU.add).then_inc(dve_a.sem, 1)
                    link(dve.tensor_copy(sel[0:64, :, :],
                                         ident[0:64, 0:HEADS].unsqueeze(2).to_broadcast([64, HEADS, P])))
                    dve.tensor_scalar(sel[32:64, :, :],
                                      ident[32:64, F_ROW:F_ROW + HEADS].unsqueeze(2).to_broadcast([32, HEADS, P]),
                                      -1.0 / SCALE, None, ALU.mult)
                    dve.wait_ge(tr.sem, t0 + 5)
                    dve.tensor_copy(gate_c_tok, ps[:, 4, 0:256].rearrange("p (j r) -> p j r", j=NT))
                    link(dve.tensor_copy(gate_u_tok, ps[:, 4, 256:512].rearrange("p (j r) -> p j r", j=NT)))
                    dve.tensor_scalar(neg_c, gate_c_tok[:, :, 0:HEADS], -1.0, None, ALU.mult)
                    for j in range(NT):
                        dve.wait_ge(act_a.sem, a0 + 3 + j)
                        dve.tensor_tensor(xdt[:, j, :].rearrange("p (h d) -> p h d", h=HEADS),
                                          xs_tok[:, j, :].rearrange("p (h d) -> p h d", h=HEADS),
                                          gate_u_tok[:, j, 0:HEADS].unsqueeze(2).to_broadcast([P, HEADS, HD]),
                                          ALU.mult)
                    for n in range(8):
                        g, i = n // 4, n % 4
                        dve.wait_ge(pe_a.sem, b0 + n + 1)
                        dve.tensor_copy(cb[:, g, CB_AT[i]:CB_AT[i] + T - i * P], ps[:, 5 + n % 3, 0:T - i * P])\
                           .then_inc(dve_b.sem, 1)

                @block.tensor
                def _(pe):
                    for j in range(NT):
                        for c in range(4):
                            ins = pe.transpose(ps[:, j, c * P:(c + 1) * P], xbc_a[:, c, j * P:(j + 1) * P], ident)
                        ins.then_inc(tr.sem, 1)
                    pe.wait_ge(dve_a.sem, d0 + 1)
                    for j in range(NT):
                        pe.transpose(ps[:, 4, j * 64:(j + 1) * 64], gate_c[:, j * P:(j + 1) * P], ident[0:64, 0:64])
                        ins = pe.transpose(ps[:, 4, 256 + j * 64:256 + (j + 1) * 64], gate_u[:, j * P:(j + 1) * P],
                                           ident[0:64, 0:64])
                    ins.then_inc(tr.sem, 1)
                    for n in range(8):
                        g, i = n // 4, n % 4
                        if n >= 3:
                            pe.wait_ge(dve_b.sem, e0 + n - 2)
                        pe.matmul(ps[:, 5 + n % 3, 0:T - i * P], xbc_a[:, 4 + g, i * P:(i + 1) * P],
                                  xbc_a[:, 6 + g, i * P:T], start=True, stop=True).then_inc(pe_a.sem, 1)

        def ssd_stage():
            eb = [view(xt_mem, 2 * TRI, TRI), view(arena, 4128 + 2048, TRI)]
            gnorm = rows[:, 2 * T:3 * T]
            l0 = loaded.take(16)
            m0, e0, g0 = pe_a.take(4 * HEADS), act_a.take(4 * HEADS + 2), dve_a.take(4 * HEADS)
            y0, d0 = pe_b.take(HEADS), dve_b.take(HEADS)
            k0 = dve_c.take(2)
            with nc.Block() as block:
                @block.gpsimd
                def _(pool):
                    pool.dma_start(gnorm, a["ssd_norm_g"][0].partition_broadcast(P)).then_inc(loaded.sem, 16)

                @block.tensor
                def _(pe):
                    def decays(h):
                        for i in range(NT):
                            n = 4 * h + i
                            if h >= 1:
                                pe.wait_ge(act_a.sem, e0 + n - 3)
                            w = T - i * P
                            d, row = sel[0:HEADS, h, :], gate_c[0:HEADS, :]
                            pe.matmul(ps[:, i, 0:P], ident, mask_sq, start=True, stop=False)
                            ins = pe.matmul(ps[:, i, 0:P], d, row[:, i * P:(i + 1) * P], start=False, stop=True)
                            if w > P:
                                ins = pe.matmul(ps[:, i, P:w], d, row[:, (i + 1) * P:T], start=True, stop=True)
                            ins.then_inc(pe_a.sem, 1)

                    decays(0)
                    for h in range(HEADS):
                        if h + 1 < HEADS:
                            decays(h + 1)
                        pe.wait_ge(dve_a.sem, g0 + 4 * h + 4)
                        if h >= 2:
                            pe.wait_ge(dve_b.sem, d0 + h - 1)
                        for j in range(NT):
                            for i in range(j + 1):
                                at = CB_AT[i] + (j - i) * P
                                ins = pe.matmul(ps[:, 4 + h % 2, j * HD:(j + 1) * HD], eb[h % 2][:, at:at + P],
                                                xdt[:, i, h * HD:(h + 1) * HD], start=(i == 0), stop=(i == j))
                        ins.then_inc(pe_b.sem, 1)

                @block.scalar
                def _(act):
                    for h in range(HEADS):
                        if h >= 2:
                            act.wait_ge(pe_b.sem, y0 + h - 1)
                        for i in range(NT):
                            w = T - i * P
                            act.wait_ge(pe_a.sem, m0 + 4 * h + i + 1)
                            act.activation(eb[h % 2][:, CB_AT[i]:CB_AT[i] + w], ps[:, i, 0:w], ACT.Exp,
                                           bias=neg_c[:, i, h:h + 1]).then_inc(act_a.sem, 1)
                    act.wait_ge(dve_c.sem, k0 + 1)
                    for j in range(NT):
                        for g in range(GROUPS):
                            ins = act.activation(xdt[:, j, g * 256:(g + 1) * 256], merged_s[:, j, g * 256:(g + 1) * 256],
                                                 ACT.Square, accum_out=sumsq[:, 2 * j + g:2 * j + g + 1])
                    ins.then_inc(act_a.sem, 1)
                    act.wait_ge(dve_c.sem, k0 + 2)
                    act.activation(sumsq[:, 16:24], sumsq[:, 8:16], ACT.Sqrt).then_inc(act_a.sem, 1)

                @block.vector
                def _(dve):
                    link = Chain(dve, dve_chain)

                    def take_y(h):
                        dve.wait_ge(pe_b.sem, y0 + h + 1)
                        dve.scalar_tensor_tensor(merged_s[:, :, h * HD:(h + 1) * HD], xs_tok[:, :, h * HD:(h + 1) * HD],
                                                 dskip[:, h:h + 1],
                                                 ps[:, 4 + h % 2, 0:4 * HD].rearrange("p (j d) -> p j d", j=NT),
                                                 ALU.mult, ALU.add).then_inc(dve_b.sem, 1)

                    for h in range(HEADS):
                        g = h // (HEADS // GROUPS)
                        for i in range(NT):
                            dve.wait_ge(act_a.sem, e0 + 4 * h + i + 1)
                            e = eb[h % 2][:, CB_AT[i]:CB_AT[i] + T - i * P]
                            dve.tensor_tensor(e, e, cb[:, g, CB_AT[i]:CB_AT[i] + T - i * P], ALU.mult)\
                               .then_inc(dve_a.sem, 1)
                        if h >= 1:
                            take_y(h - 1)
                    take_y(HEADS - 1)
                    dve.wait_ge(dve_b.sem, d0 + HEADS)
                    for j in range(NT):
                        ins = dve.tensor_tensor(merged_s[:, j, :], merged_s[:, j, :], z_s[:, j, :], ALU.mult)
                    ins.then_inc(dve_c.sem, 1)
                    dve.wait_ge(act_a.sem, e0 + 4 * HEADS + 1)
                    dve.tensor_scalar(sumsq[:, 8:16], sumsq[:, 0:8], 1.0 / 256, RMS_EPS, ALU.mult, ALU.add)\
                       .then_inc(dve_c.sem, 1)
                    dve.wait_ge(act_a.sem, e0 + 4 * HEADS + 2)
                    link(dve.reciprocal(sumsq[:, 24:32], sumsq[:, 16:24]))
                    dve.wait_ge(loaded.sem, l0 + 16)
                    for j in range(NT):
                        for g in range(GROUPS):
                            y = merged_s[:, j, g * 256:(g + 1) * 256]
                            dve.scalar_tensor_tensor(y, y, sumsq[:, 24 + 2 * j + g:25 + 2 * j + g],
                                                     gnorm[:, g * 256:(g + 1) * 256], ALU.mult, ALU.mult)

        def attention_stage(n_comp, q, k, v, dv_head, put, lam=None, forget=False):
            jobs = HEADS * NT
            prob = [[view(xt_mem, (2 * b + c) * T, T) for c in range(2)] for b in range(2)]
            turned = [view(xt_mem, (4 + b) * T, T) for b in range(2)]
            st = view(small, 696, 2, 8)
            m0, x0, e0, n0 = pe_a.take(jobs * n_comp), dve_a.take(jobs * n_comp), act_a.take(jobs * n_comp), dve_b.take(jobs)
            t0, c0, o0, d0 = tr.take(jobs), act_b.take(jobs), pe_b.take(jobs), dve_c.take(jobs)

            def width(n):
                return (n % NT + 1) * P

            def score(n, c):
                return ps[:, n_comp * (n % 2) + c, 0:width(n)]

            with nc.Block() as block:
                @block.tensor
                def _(pe):
                    def scores(n):
                        h, j = n // NT, n % NT
                        for c in range(n_comp):
                            if n >= 2:
                                pe.wait_ge(act_a.sem, e0 + n_comp * (n - 2) + c + 1)
                            qj = q(h, c)[:, j * P:(j + 1) * P]
                            for lo, hi in ((j * P, (j + 1) * P), (0, j * P))[0:1 + (j > 0)]:
                                part = score(n, c)[:, lo:hi]
                                if lo == j * P:
                                    pe.matmul(part, ident, mask_qk, start=True, stop=False)
                                if forget:
                                    pe.matmul(part, sel[F_ROW:F_ROW + HEADS, h, :], gate_c[F_ROW:F_ROW + HEADS, lo:hi],
                                              start=(lo != j * P), stop=False)
                                ins = pe.matmul(part, qj, k(h, c)[:, lo:hi], start=(lo != j * P and not forget), stop=True)
                            ins.then_inc(pe_a.sem, 1)

                    def turn(n):
                        pe.wait_ge(dve_b.sem, n0 + n + 1)
                        if n >= 2:
                            pe.wait_ge(act_b.sem, c0 + n - 1)
                        for i in range(n % NT + 1):
                            ins = pe.transpose(ps[:, 4 + n % 2, i * P:(i + 1) * P],
                                               prob[n % 2][0][:, i * P:(i + 1) * P], ident)
                        ins.then_inc(tr.sem, 1)

                    def product(n):
                        h = n // NT
                        pe.wait_ge(act_b.sem, c0 + n + 1)
                        if n >= 2:
                            pe.wait_ge(dve_c.sem, d0 + n - 1)
                        for i in range(n % NT + 1):
                            ins = pe.matmul(ps[:, 6 + n % 2, 0:dv_head], turned[n % 2][:, i * P:(i + 1) * P],
                                            v[:, i, h * dv_head:(h + 1) * dv_head],
                                            start=(i == 0), stop=(i == n % NT))
                        ins.then_inc(pe_b.sem, 1)

                    for s in range(jobs + 3):
                        if s < jobs:
                            scores(s)
                        if 0 <= s - 2 < jobs:
                            turn(s - 2)
                        if 0 <= s - 3 < jobs:
                            product(s - 3)

                @block.scalar
                def _(act):
                    for s in range(jobs + 2):
                        if s < jobs:
                            for c in range(n_comp):
                                act.wait_ge(dve_a.sem, x0 + n_comp * s + c + 1)
                                if s >= 2:
                                    act.wait_ge(tr.sem, t0 + s - 1)
                                act.activation(prob[s % 2][c][:, 0:width(s)], score(s, c), ACT.Exp,
                                               bias=st[:, s % 2, 2 + c:3 + c], scale=SCALE,
                                               accum_out=st[:, s % 2, 4 + c:5 + c]).then_inc(act_a.sem, 1)
                        n = s - 2
                        if 0 <= n:
                            act.wait_ge(tr.sem, t0 + n + 1)
                            if n >= 2:
                                act.wait_ge(pe_b.sem, o0 + n - 1)
                            act.activation(turned[n % 2][:, 0:width(n)], ps[:, 4 + n % 2, 0:width(n)], ACT.Copy)\
                               .then_inc(act_b.sem, 1)

                @block.vector
                def _(dve):
                    link = Chain(dve, dve_chain)

                    def maxima(n):
                        for c in range(n_comp):
                            dve.wait_ge(pe_a.sem, m0 + n_comp * n + c + 1)
                            link(dve.tensor_reduce(st[:, n % 2, c:c + 1], score(n, c), AX, ALU.max))
                            dve.tensor_scalar(st[:, n % 2, 2 + c:3 + c], st[:, n % 2, c:c + 1], -SCALE, None, ALU.mult)\
                               .then_inc(dve_a.sem, 1)

                    def divide(n):
                        p, r = prob[n % 2], st[:, n % 2, 6:8]
                        dve.wait_ge(act_a.sem, e0 + n_comp * (n + 1))
                        link(dve.reciprocal(r[:, 0:n_comp], st[:, n % 2, 4:4 + n_comp]))
                        p0 = p[0][:, 0:width(n)]
                        if n_comp == 1:
                            dve.tensor_scalar(p0, p0, r[:, 0:1], None, ALU.mult).then_inc(dve_b.sem, 1)
                        else:
                            p1 = p[1][:, 0:width(n)]
                            link(dve.tensor_scalar(p1, p1, r[:, 1:2], lam, ALU.mult, ALU.mult))
                            dve.scalar_tensor_tensor(p0, p0, r[:, 0:1], p1, ALU.mult, ALU.subtract).then_inc(dve_b.sem, 1)

                    for s in range(jobs + 4):
                        if s < jobs:
                            maxima(s)
                        if 0 <= s - 1 < jobs:
                            divide(s - 1)
                        n = s - 4
                        if 0 <= n:
                            dve.wait_ge(pe_b.sem, o0 + n + 1)
                            dve.tensor_copy(put(n // NT, n % NT), ps[:, 6 + n % 2, 0:dv_head]).then_inc(dve_c.sem, 1)

        def moe_stage(l, alpha, g_src, b_src, last):
            E, EPG = n_experts[l], n_experts[l] // 4
            G = 4
            NR = G + E
            MAXB = 2 * T // BLK + E
            wr = view(arena, 0, NK, NR)
            brow = arena[0:1, 300:300 + NR]
            at = [400]

            def take(*shape, dt=F32):
                v = view(arena, at[0], *shape)
                at[0] += int(np.prod(shape))
                return v.bitcast(dt) if dt != F32 else v

            logits, expo, pen = take(NT, NR), take(NT, G), take(NT, G)
            gmax, gsum, m1, m2 = take(NT), take(NT), take(NT), take(NT)
            iota_g, iota_e = take(G), take(E)
            first, pick_g = take(NT), take(NT, G)
            es, es2 = take(NT, E), take(NT, E)
            pick1, pick2, pick = take(NT, E), take(NT, E), take(NT, E)
            w1, w2, ratio = take(NT), take(NT), take(NT)
            count_i, count_s = take(E, dt=I32), take(E, dt=I32)
            nblk, ends, starts = take(E), take(E), take(E)
            table = take(E + 2, dt=I32)
            pos = take(NT, E)
            slots = take(2, NT)
            slots_i = take(2, NT, dt=U32)
            slots_now = take(2, NT)
            hit1, hit2, hit = take(NT, BLK), take(NT, BLK), take(NT, BLK)
            x_rows, xg = take(2, P), take(NK, BLK)
            silu_g, hidden, hT = take(P), take(P), take(P)
            y_sb = take(D // 4)
            y1, y2 = take(NT, D), take(NT, D)
            assert at[0] <= 16448

            def bc(v, n):
                return v.unsqueeze(2).to_broadcast([P, v.shape[1], n])

            def mid(v, n):
                return v.unsqueeze(1).to_broadcast([P, n, v.shape[1]])

            l0, m0, d0, a0 = loaded.total, mm.take(2), dve_a.take(3), act_a.take(2)
            p0 = pool_chain.take(0)
            router = ((a["router_group_w"][0], a["router_group_b"][0], None, a["router_expert_b"][0]),
                      (a["moe_rg_w_2"][0], a["moe_rg_b_2"][0], a["moe_re_w_2"][0], a["moe_re_b_2"][0]),
                      (a["moe_rg_w_2"][1], a["moe_rg_b_2"][1], a["moe_re_w_2"][1], a["moe_re_b_2"][1]))[l]
            n_w = 5 if l == 0 else 2
            loaded.total = l0 + 16 * (n_w + 2)
            ready = consts.take(1)
            with nc.Block() as block:
                @block.gpsimd
                def _(pool):
                    def load(dst, src):
                        pool.dma_start(dst, src).then_inc(loaded.sem, 16)

                    with nc.allow_non_contiguous_dma("router columns"):
                        load(wr[:, :, 0:G], router[0].rearrange("(k p) g -> p k g", p=P))
                        if l == 0:
                            for g in range(G):
                                load(wr[:, :, G + g * EPG:G + (g + 1) * EPG],
                                     a["router_expert_w"][0][g].rearrange("(k p) e -> p k e", p=P))
                        else:
                            load(wr[:, :, G:NR], router[2].rearrange("(k p) e -> p k e", p=P))
                        load(brow[:, 0:G], router[1].unsqueeze(0))
                        load(brow[:, G:NR], (router[3].rearrange("g e -> (g e)") if l == 0 else router[3]).unsqueeze(0))
                    pool.iota(iota_g, pattern=[[1, G]], base=0, channel_multiplier=0, allow_small_or_imprecise_dtypes=True)
                    pool.iota(iota_e, pattern=[[1, E]], base=0, channel_multiplier=0, allow_small_or_imprecise_dtypes=True)
                    pool.memset(table, 0).then_inc(consts.sem, 1)

                @block.tensor
                def _(pe):
                    pe.wait_ge(loaded.sem, l0 + 16 * (n_w + 2))
                    for j in range(NT):
                        pe.matmul(ps[:, j, 0:NR], ones[0:1, :], brow, start=True, stop=False)
                        for k in range(NK):
                            ins = pe.matmul(ps[:, j, 0:NR], xT[:, k, j * P:(j + 1) * P], wr[:, k, :],
                                            start=False, stop=(k == NK - 1))
                    ins.then_inc(mm.sem, 1)
                    pe.wait_ge(dve_a.sem, d0 + 3)
                    for j in range(NT):
                        for i in range(j + 1):
                            pe.matmul(ps[:, 4, j * E:(j + 1) * E], before if i == j else ones, pick[:, i, :],
                                      start=(i == 0), stop=(i == j))
                    for i in range(NT):
                        ins = pe.matmul(ps[:, 5, 0:E], ones, pick[:, i, :], start=(i == 0), stop=(i == NT - 1))
                    ins.then_inc(mm.sem, 1)

                @block.scalar
                def _(act):
                    act.wait_ge(dve_a.sem, d0 + 1)
                    act.activation(expo, expo, ACT.Exp).then_inc(act_a.sem, 1)
                    act.wait_ge(dve_a.sem, d0 + 2)
                    act.activation(ratio, ratio, ACT.Exp).then_inc(act_a.sem, 1)

                @block.vector
                def _(dve):
                    link = Chain(dve, dve_chain)

                    def pick_max(dst, tmp, x, m, iota, n):
                        link(dve.tensor_reduce(m, x, AX, ALU.max))
                        link(dve.tensor_tensor(tmp, x, bc(m, n), ALU.is_equal))
                        link(dve.scalar_tensor_tensor(tmp, tmp, -1000.0, mid(iota, NT), ALU.mult, ALU.add))
                        link(dve.tensor_reduce(first, tmp, AX, ALU.min))
                        link(dve.tensor_tensor(dst, tmp, bc(first, n), ALU.is_equal))

                    dve.wait_ge(consts.sem, ready + 1)
                    dve.wait_ge(mm.sem, m0 + 1)
                    link(dve.tensor_copy(logits, ps[:, 0:NT, 0:NR]))
                    gl, el = logits[:, :, 0:G], logits[:, :, G:NR]
                    pick_max(pick_g, pen, gl, gmax, iota_g, G)
                    dve.tensor_tensor(expo, gl, bc(gmax, G), ALU.subtract).then_inc(dve_a.sem, 1)
                    link(dve.tensor_scalar(pen, pick_g, -NEG, NEG, ALU.mult, ALU.add))
                    link(dve.tensor_tensor(es.rearrange("p j (g e) -> p j g e", g=G),
                                           el.rearrange("p j (g e) -> p j g e", g=G),
                                           pen.unsqueeze(3).to_broadcast([P, NT, G, EPG]), ALU.add))
                    pick_max(pick1, es2, es, m1, iota_e, E)
                    link(dve.scalar_tensor_tensor(es, pick1, 2 * NEG, es, ALU.mult, ALU.add))
                    pick_max(pick2, es2, es, m2, iota_e, E)
                    dve.tensor_tensor(ratio, m2, m1, ALU.subtract).then_inc(dve_a.sem, 1)
                    dve.tensor_tensor(pick, pick1, pick2, ALU.add).then_inc(dve_a.sem, 1)
                    dve.wait_ge(act_a.sem, a0 + 2)
                    link(dve.tensor_reduce(gsum, expo, AX, ALU.add))
                    link(dve.tensor_scalar(w2, ratio, 1.0, None, ALU.add))
                    link(dve.tensor_tensor(w1, gsum, w2, ALU.mult))
                    link(dve.reciprocal(w1, w1))
                    dve.tensor_tensor(w2, w1, ratio, ALU.mult)
                    dve.wait_ge(mm.sem, m0 + 2)
                    link(dve.tensor_scalar(count_i, ps[:, 5, 0:E], float(BLK - 1), None, ALU.add))
                    link(dve.tensor_scalar(count_s, count_i, BLK.bit_length() - 1, None, ALU.arith_shift_right))
                    link(dve.tensor_scalar(nblk, count_s, 1.0, None, ALU.max))
                    link(dve.tensor_tensor_scan(ends, ones[:, 0:E], nblk, 0.0, ALU.mult, ALU.add))
                    link(dve.tensor_tensor(starts, ends, nblk, ALU.subtract))
                    dve.tensor_copy(table[:, 1:E + 1], ends)
                    dve.tensor_copy(table[:, E + 1:E + 2], ends[:, E - 1:E])
                    link(dve.scalar_tensor_tensor(pos, mid(starts, NT), float(BLK),
                                                  ps[:, 4, 0:NT * E].rearrange("p (j e) -> p j e", j=NT),
                                                  ALU.mult, ALU.add))
                    for n, pk in enumerate((pick1, pick2)):
                        link(dve.tensor_tensor(es, pos, pk, ALU.mult))
                        link(dve.tensor_reduce(slots[:, n, :], es, AX, ALU.add))
                    dve.tensor_copy(slots_i, slots)
                    dve.tensor_copy(slots_now, slots)
                    dve.memset(y_sb, 0.0)

            s_hit, s_got, s_rows, s_turned, s_xg, s_gu, s_silu, s_h, s_hturned, s_hT, s_down, s_y, s_stored, s_slots = (
                signal(f"{n}{l}").sem for n in (
                    "selection_ready", "gathered", "rows_taken", "inputs_turned", "inputs_ready", "gate_up_done", "silu_ready",
                    "hidden_ready", "hidden_turned", "hidden_taken", "down_done", "rows_ready", "rows_stored", "slots_moved"))
            pairs = E // 2
            c0 = moe_at[l]
            quarters = [slice(q * BLK, (q + 1) * BLK) for q in range(4)]
            W = D // 4

            def value(eng, n, low=1):
                return eng.value_load(table[0:1, n], min_val=low, max_val=MAXB)

            def rows_at(g):
                return ybuf[bass.ds(g * BLK, BLK), :].rearrange("r (q n) -> q r n", q=4)

            with nc.Block() as block:
                @block.sync
                def _(sp):
                    with sp.Fori(0, pairs - 1) as i:
                        for e in range(2):
                            end = value(sp, bass.ds(2 * i + e + 1, 1))
                            sp.wait_ge(s_down, end)
                            for j in range(3):
                                load_expert_chunk(sp, l, 2 * i + 2 + e, j, c0 + 3 * e + j)
                    if l < 2:
                        for e in range(2):
                            sp.wait_ge(s_down, value(sp, slice(E - 1 + e, E + e)))
                            for j in range(3):
                                load_chunk(sp, mixer_at[l + 1] + 3 * e + j)

                @block.tensor
                def _(pe):
                    def gather():
                        for j in range(NT):
                            for q, at in enumerate(quarters):
                                ins = pe.matmul(ps[at, 0, 0:W], hit[:, j, :],
                                                x_tok[:, j, :].rearrange("p (h q c) -> p h q c", h=2, q=4)[:, :, q, :],
                                                start=(j == 0), stop=(j == NT - 1))
                        ins.then_inc(s_got, 1)

                    def turn_inputs():
                        for h in range(2):
                            ins = pe.transpose(ps[:, 1, h * P:(h + 1) * P], x_rows[:, h, :], ident)
                        ins.then_inc(s_turned, 1)

                    pe.wait_ge(s_hit, 1)
                    gather()
                    pe.wait_ge(s_rows, 1)
                    turn_inputs()
                    with pe.Fori(0, pairs) as i:
                        for e in range(2):
                            first_chunk = c0 + 3 * e
                            sg, sd = (first_chunk + kinds(first_chunk).index(kind) for kind in (0, 2))
                            w_gu = ring[:, sg % SLOTS * NK * CH:(sg % SLOTS + 2) * NK * CH] \
                                .rearrange("p (w k n) -> p w k n", w=2, k=NK)
                            wd = slot(sd % SLOTS).rearrange("p (k n) -> p k n", k=NT)
                            start, end = value(pe, bass.ds(2 * i + e, 1), 0), value(pe, bass.ds(2 * i + e + 1, 1))
                            with pe.Fori(start, end) as g:
                                for n in range(first_chunk, first_chunk + 3):
                                    pe.wait_ge(arrived[n % SLOTS].sem, i * 16 + 16 * (n // SLOTS + 1))
                                pe.wait_ge(s_xg, g + 1)
                                for k in range(NK):
                                    for q, at in enumerate(quarters):
                                        ins = pe.matmul(ps[at, 2, 0:W], xg[:, k, :], w_gu[:, :, k, q * P:(q + 1) * P],
                                                        start=(k == 0), stop=(k == NK - 1))
                                ins.then_inc(s_gu, 1)
                                pe.wait_ge(s_hit, g + 2)
                                gather()
                                pe.wait_ge(s_h, g + 1)
                                pe.transpose(ps[:, 3, 0:P], hidden, ident).then_inc(s_hturned, 1)
                                pe.wait_ge(s_rows, g + 2)
                                turn_inputs()
                                pe.wait_ge(s_hT, g + 1)
                                pe.wait_ge(s_y, g + 1)
                                for f in range(NT):
                                    for q, at in enumerate(quarters):
                                        ins = pe.matmul(ps[at, 4, 0:W], hT[:, f * BLK:(f + 1) * BLK], wd[:, f, q * W:(q + 1) * W],
                                                        start=(f == 0), stop=(f == NT - 1))
                                ins.then_inc(s_down, 1)

                @block.scalar
                def _(act):
                    def take_rows():
                        act.activation(x_rows, ps[:, 0, 0:W].rearrange("p (h c) -> p h c", h=2), ACT.Copy).then_inc(s_rows, 1)

                    act.dma_start(rows_at(0), y_sb).then_inc(s_stored, 16)
                    total = value(act, slice(E + 1, E + 2))
                    act.wait_ge(s_got, 1)
                    take_rows()
                    with act.Fori(0, total) as g:
                        act.wait_ge(s_gu, g + 1)
                        act.activation(silu_g, ps[:, 2, 0:P], ACT.Silu).then_inc(s_silu, 1)
                        act.wait_ge(s_got, g + 2)
                        take_rows()
                        act.wait_ge(s_y, g + 2)
                        act.dma_start(rows_at(g), y_sb).then_inc(s_stored, 16)
                    act.wait_ge(s_stored, total * 16 + 16)
                    act.activation(mean_var[:, 4:5], eps_ln, ACT.Copy)

                @block.vector
                def _(dve):
                    def select(g):
                        dve.tensor_tensor(hit1, mid(iota_f, NT), bc(slots_now[:, 0, :], BLK), ALU.is_equal)
                        dve.tensor_tensor(hit2, mid(iota_f, NT), bc(slots_now[:, 1, :], BLK), ALU.is_equal).then_inc(s_slots, 1)
                        dve.wait_ge(s_slots, g * 2 + 1)
                        dve.tensor_tensor(hit, hit1, hit2, ALU.add).then_inc(s_hit, 1)
                        dve.tensor_scalar(slots_now, slots_now, float(BLK), None, ALU.subtract).then_inc(s_slots, 1)
                        dve.wait_ge(s_slots, g * 2 + 2)

                    def take_inputs():
                        dve.tensor_copy(xg.rearrange("p k s -> p (k s)"), ps[:, 1, 0:W]).then_inc(s_xg, 1)

                    total = value(dve, slice(E + 1, E + 2))
                    dve.memset(mean_var[:, 5:6], 0.0).then_inc(s_y, 1)
                    select(0)
                    dve.wait_ge(s_turned, 1)
                    take_inputs()
                    with dve.Fori(0, total) as g:
                        dve.wait_ge(s_got, g + 1)
                        select(g + 1)
                        dve.wait_ge(s_silu, g + 1)
                        dve.tensor_tensor(hidden, silu_g, ps[:, 2, P:2 * P], ALU.mult).then_inc(s_h, 1)
                        dve.wait_ge(s_hturned, g + 1)
                        dve.tensor_copy(hT, ps[:, 3, 0:P]).then_inc(s_hT, 1)
                        dve.wait_ge(s_turned, g + 2)
                        take_inputs()
                        dve.wait_ge(s_down, g + 1)
                        dve.wait_ge(s_stored, g * 16 + 16)
                        dve.tensor_copy(y_sb, ps[:, 4, 0:W]).then_inc(s_y, 1)

            r0, s0, q0, l1 = loaded.take(16 * 8), stat.take(NT), sq.take(NT), loaded.take(32)
            with nc.Block() as block:
                @block.gpsimd
                def _(pool):
                    for j in range(NT):
                        for n, y in enumerate((y1, y2)):
                            pool.indirect_dma_start(out=y[:, j, :], out_offset=None, in_=ybuf,
                                                    in_offset=bass.IndirectOffsetOnAxis(ap=slots_i[:, n, j:j + 1], axis=0))\
                                .then_inc(loaded.sem, 16)
                    load_norm_rows(pool, g_src, b_src)

                @block.scalar
                def _(act):
                    deviations(act, s0)

                @block.vector
                def _(dve):
                    link = Chain(dve, dve_chain)
                    dve.wait_ge(loaded.sem, l1 + 32)
                    for j in range(NT):
                        xj = x_tok[:, j, :]
                        link(dve.tensor_scalar(xj, xj, alpha, None, ALU.mult))
                        link(dve.scalar_tensor_tensor(xj, y1[:, j, :], w1[:, j:j + 1], xj, ALU.mult, ALU.add))
                        link(dve.scalar_tensor_tensor(xj, y2[:, j, :], w2[:, j:j + 1], xj, ALU.mult, ALU.add))
                        normalise(dve, link, j, q0)
            if not last:
                transpose_stage(lambda j, k: x_tok[:, j, k * P:(k + 1) * P], xT)

        q2 = view(arena, 0, DA_HEADS, T)
        k2 = view(arena, NK * T, DA_HEADS, T)
        v2 = view(arena, 2 * NK * T, NT, D)
        o2 = view(arena, 3 * NK * T, NT, D)
        lam = cols[:, 8:9]
        lam_rows = rows[:, 0:256].rearrange("p (n d) -> p n d", n=4)
        subln = rows[:, 256:256 + P]

        def qkv_stage():
            first = mixer_at[1]
            m0, e0, l0 = mm.take(24), ev.take(24), loaded.take(32)
            for c in range(6):
                used[first + c] = (mm.sem, m0 + 4 * (c + 1))
            prods = view(rows, 512, 2, HD)
            sums = cols[:, 16:18]
            x0, a0 = dve_a.take(1), act_a.take(1)
            with nc.Block() as block:
                @block.sync
                def _(sp):
                    stream_mixer(sp, first + SLOTS, first + 12)

                @block.gpsimd
                def _(pool):
                    pool.dma_start(lam_rows, a["attn_lambda_2"][0].partition_broadcast(P)).then_inc(loaded.sem, 16)
                    pool.dma_start(subln, a["attn_subln_g_2"][0].partition_broadcast(P)).then_inc(loaded.sem, 16)

                @block.tensor
                def _(pe):
                    for n in range(24):
                        c, j = n // 4, n % 4
                        if n >= 8:
                            pe.wait_ge(ev.sem, e0 + n - 7)
                        if j == 0:
                            wait_chunk(pe, first + c)
                        w = slot((first + c) % SLOTS).rearrange("p (k n) -> p k n", k=NK)
                        for k in range(NK):
                            wj, xj = w[:, k, :], xT[:, k, :]
                            if c < 4:
                                wj = w[:, k, j * P:(j + 1) * P]
                            else:
                                xj = xT[:, k, j * P:(j + 1) * P]
                            lhs, rhs = (wj, xj) if c < 4 else (xj, wj)
                            ins = pe.matmul(ps[:, n % 8, :], lhs, rhs, start=(k == 0), stop=(k == NK - 1))
                        ins.then_inc(mm.sem, 1)

                @block.scalar
                def _(act):
                    act.wait_ge(dve_a.sem, x0 + 1)
                    act.activation(sums, sums, ACT.Exp).then_inc(act_a.sem, 1)
                    for n in range(24):
                        c, j = n // 4, n % 4
                        act.wait_ge(mm.sem, m0 + n + 1)
                        dst = (q2, k2)[c // 2][:, 4 * (c % 2) + j, :] if c < 4 else v2[:, j, (c - 4) * CH:(c - 3) * CH]
                        act.activation(dst, ps[:, n % 8, :], ACT.Copy).then_inc(ev.sem, 1)

                @block.vector
                def _(dve):
                    link = Chain(dve, dve_chain)
                    dve.wait_ge(loaded.sem, l0 + 32)
                    link(dve.tensor_tensor(prods, lam_rows[:, 0:4:2, :], lam_rows[:, 1:4:2, :], ALU.mult))
                    dve.tensor_reduce(sums, prods, AX, ALU.add).then_inc(dve_a.sem, 1)
                    dve.wait_ge(act_a.sem, a0 + 1)
                    link(dve.tensor_tensor(lam, sums[:, 0:1], sums[:, 1:2], ALU.subtract))
                    dve.tensor_scalar(lam, lam, LAMBDA_INIT, None, ALU.add)

        def subln_stage():
            squares = view(xt_mem, 0, NT, D)
            ms = cols[:, 16:48]
            x0, a0 = dve_a.take(1), act_a.take(1)
            heads = "p j (h d) -> p (j h) d"
            with nc.Block() as block:
                @block.scalar
                def _(act):
                    act.wait_ge(dve_a.sem, x0 + 1)
                    act.activation(ms, ms, ACT.Sqrt).then_inc(act_a.sem, 1)

                @block.vector
                def _(dve):
                    link = Chain(dve, dve_chain)
                    o = o2.rearrange(heads, h=DA_HEADS)
                    link(dve.tensor_tensor(squares, o2, o2, ALU.mult))
                    link(dve.tensor_reduce(ms, squares.rearrange(heads, h=DA_HEADS), AX, ALU.add))
                    dve.tensor_scalar(ms, ms, 1.0 / P, RMS_EPS, ALU.mult, ALU.add).then_inc(dve_a.sem, 1)
                    link(dve.tensor_scalar(subln, subln, 1.0 - LAMBDA_INIT, None, ALU.mult))
                    dve.wait_ge(act_a.sem, a0 + 1)
                    link(dve.reciprocal(ms, ms))
                    link(dve.tensor_tensor(o, o, ms.unsqueeze(2).to_broadcast([P, 32, P]), ALU.mult))
                    dve.tensor_tensor(o, o, subln.unsqueeze(1).to_broadcast([P, 32, P]), ALU.mult)

        rT = view(arena, 0, NK, T)
        k3 = view(arena, NK * T, NK, T)
        v3 = view(arena, 2 * NK * T, NT, D)
        w2a2 = rows[:, 0:D]
        h_wa = rows[:, D:D + T]
        h_g = rows[:, D + T:D + 2 * T]
        h_g2 = small[0:GATE_LORA - P, 40:40 + T]
        N_PAR = 5
        K_K, K_A, R_K, W0, A0 = range(N_PAR)
        par = view(small, 552, N_PAR, NK)
        same_head = small[:, 592:720]

        def rkv_stage():
            first = mixer_at[2]
            mixes = {"w": 3, "a": 4, "g": 5, "r": 0, "k": 1, "v": 2}
            xx = view(arena, 3 * NK * T, NK, T)
            buf = {"w": view(arena, 2 * NK * T, NK, T), "a": k3}
            buf.update(g=buf["w"], r=buf["a"], k=buf["w"], v=xx)
            w1 = view(arena, 0, NK, DECAY_LORA)
            a1 = view(arena, 512, NK, AAA_LORA)
            g1 = view(arena, 1024, NK, GATE_LORA)
            mu = view(arena, 4 * NK * T, 6, NK)
            jobs = ["w", "a", "g", "g2"] + [(n, c, j) for n in "rkv" for c in range(2) for j in range(4)]
            m0, e0, l0 = mm.take(28), ev.take(28), loaded.take(16 * 16)
            x0, c0 = dve_a.take(6), consts.take(1)
            for c in range(6):
                used[first + c] = (mm.sem, m0 + 4 + 4 * (c + 1))
            with nc.Block() as block:
                @block.sync
                def _(sp):
                    stream_mixer(sp, first + SLOTS, first + 11)

                @block.gpsimd
                def _(pool):
                    def load(dst, src):
                        pool.dma_start(dst, src).then_inc(loaded.sem, 16)

                    with nc.allow_non_contiguous_dma("parameter columns"):
                        for n in range(6):
                            load(mu[:, n, :], a["rw_mu_2"][0][n].rearrange("(k p) -> p k", p=P))
                        load(w1, a["rw_w1_2"][0].rearrange("(k p) n -> p k n", p=P))
                        load(a1, a["rw_a1_2"][0].rearrange("(k p) n -> p k n", p=P))
                        load(g1, a["rw_g1_2"][0].rearrange("(k p) n -> p k n", p=P))
                        load(w2a2[0:64, :], a["rw_w2_2"][0])
                        load(w2a2[64:128, :], a["rw_a2_2"][0])
                        for n, src in ((K_K, "rw_k_k_2"), (K_A, "rw_k_a_2"), (W0, "rw_w0_2"), (A0, "rw_a0_2")):
                            load(par[:, n, :], a[src][0].rearrange("(k p) -> p k", p=P))
                        load(par[:, R_K, :], a["rw_r_k_2"][0].rearrange("h n -> (h n)").rearrange("(k p) -> p k", p=P))
                    link = Chain(pool, pool_chain)
                    link(pool.memset(same_head, 0.0))
                    pool.memset(same_head[0:HD, 0:HD], 1.0)
                    pool.memset(same_head[HD:P, HD:P], 1.0).then_inc(consts.sem, 1)

                @block.vector
                def _(dve):
                    link = Chain(dve, dve_chain)
                    dve.tensor_tensor(xx[:, :, 1:T], xT[:, :, 0:T - 1], xT[:, :, 1:T], ALU.subtract)
                    link(dve.tensor_scalar(xx[:, :, 0:1], xT[:, :, 0:1], -1.0, None, ALU.mult))
                    dve.wait_ge(loaded.sem, l0 + 16 * 16)
                    for n, name in enumerate(mixes):
                        if name in "grk":
                            dve.wait_ge(mm.sem, m0 + {"g": 1, "r": 2, "k": 4}[name])
                        for k in range(NK):
                            ins = dve.scalar_tensor_tensor(buf[name][:, k, :], xx[:, k, :], mu[:, mixes[name], k:k + 1],
                                                           xT[:, k, :], ALU.mult, ALU.add)
                        ins.then_inc(dve_a.sem, 1)

                @block.tensor
                def _(pe):
                    pe.wait_ge(loaded.sem, l0 + 16 * 16)
                    order = list(mixes)
                    for n, job in enumerate(jobs):
                        if n >= 8:
                            pe.wait_ge(ev.sem, e0 + n - 7)
                        bank = ps[:, n % 8, :]
                        name = job[0]
                        pe.wait_ge(dve_a.sem, x0 + order.index(name) + 1)
                        xm = buf[name]
                        if n < 4:
                            w, o = ((w1, bank[0:64, :]), (a1, bank[64:128, :]),
                                    (g1[:, :, 0:P], bank), (g1[:, :, P:GATE_LORA], bank[0:GATE_LORA - P, :]))[n]
                            for k in range(NK):
                                ins = pe.matmul(o, w[:, k, :], xm[:, k, :], start=(k == 0), stop=(k == NK - 1))
                        else:
                            _, c, j = job
                            ch = first + 2 * "rkv".index(name) + c
                            if j == 0:
                                wait_chunk(pe, ch)
                            w = slot(ch % SLOTS).rearrange("p (k n) -> p k n", k=NK)
                            for k in range(NK):
                                if name == "v":
                                    ins = pe.matmul(bank, xm[:, k, j * P:(j + 1) * P], w[:, k, :],
                                                    start=(k == 0), stop=(k == NK - 1))
                                else:
                                    ins = pe.matmul(bank, w[:, k, j * P:(j + 1) * P], xm[:, k, :],
                                                    start=(k == 0), stop=(k == NK - 1))
                        ins.then_inc(mm.sem, 1)

                @block.scalar
                def _(act):
                    for n, job in enumerate(jobs):
                        act.wait_ge(mm.sem, m0 + n + 1)
                        bank = ps[:, n % 8, :]
                        if n < 4:
                            dst, src, f = ((h_wa[0:64, :], bank[0:64, :], ACT.Tanh), (h_wa[64:128, :], bank[64:128, :], ACT.Copy),
                                           (h_g, bank, ACT.Sigmoid), (h_g2, bank[0:GATE_LORA - P, :], ACT.Sigmoid))[n]
                        else:
                            name, c, j = job
                            src, f = bank, ACT.Copy
                            dst = v3[:, j, c * CH:(c + 1) * CH] if name == "v" else (rT if name == "r" else k3)[:, 4 * c + j, :]
                        act.activation(dst, src, f).then_inc(ev.sem, 1)

        def wkv_stage():
            s = [view(arena, 3 * NK * T + n * T, T) for n in range(8)] + [view(xt_mem, n * T, T) for n in range(8)]
            keep, logd, cum, decay, inv, before_d, lr, kk = s[0:8]
            tile4 = "p (j t) -> p j t"
            AR = view(xt_mem, 0, NT, 2, P)
            A_T, R_T = AR[:, :, 0, :], AR[:, :, 1, :]
            B_T, K_T = s[10], s[11]
            A_tok, B_tok, K_tok, V = (s[n].rearrange("p (j c) -> p j c", j=NT) for n in (12, 13, 14, 15))
            XX = view(arena, 3 * NK * T + T, 8, 2 * P)
            S = s[5].rearrange("p (c i) -> p c i", c=NC_R)
            TT = view(arena, 3 * NK * T + 6 * T, 8, P)
            Z = view(arena, 3 * NK * T + T, 8, P)
            QC = view(xt_mem, 2 * T, 8, P)
            LKV = view(arena, 3 * NK * T + 4 * T, 8, HD)
            Y0 = view(arena, 3 * NK * T + T, NT, 2, HD)
            MT = view(arena, 3 * NK * T + 6 * T, NC_R, P)
            low_st_d = mask_sq
            NN = view(arena, 3 * NK * T + 3 * T, NC_R, HD)
            AKM = slot((mixer_at[2] + 11) % SLOTS).rearrange("p (u c) -> p u c", u=8)
            w2a2_now = AKM[:, 0, 0:P]
            masks = cst[:, 6 * P:8 * P]
            pcol = cols[:, 16:16 + N_PAR]
            p_end = cols[:, 24:24 + NC_R]
            units = [(e, j) for e in range(2) for j in range(NT)]
            ROUNDS = RB.bit_length() - 2
            assert RC == 2 * RB
            names = ("lora2", "lora", "par", "sig", "sq", "shift", "ssq", "exp", "ops", "turned", "tok", "val", "low", "lowm",
                     "lkv", "lkvc", "q", "c", "qc", "z", "zc", "q2", "q2c", "mt0", "r2", "r2c", "y0", "y0c", "mn", "mnc", "yy", "yc")
            E = {n: signal(f"wkv_{n}").sem for n in names}
            p_akm, d_akm, p_sq, a_sq, p_tt, d_tt = (signal(f"wkv_{n}").sem for n in (
                "products", "masked", "squared", "squares_taken", "t_products", "t_added"))
            p_s, d_s = signal("wkv_state_product").sem, signal("wkv_state").sem
            chain_v, d_low = signal("wkv_dve_chain").sem, signal("wkv_low_masked").sem

            class LoopChain:

                def __init__(self, eng, sem, turn, n):
                    self.eng, self.sem, self.turn, self.n, self.at = eng, sem, turn, n, 0

                def __call__(self, ins):
                    self.at += 1
                    ins.then_inc(self.sem, 1)
                    self.eng.wait_ge(self.sem, self.turn * self.n + self.at)

                def end(self):
                    assert self.at == self.n, self.at

            def rows_of(e):
                return slice(e * HD, (e + 1) * HD)

            with nc.Block() as block:
                @block.gpsimd
                def _(pool):
                    link = Chain(pool, pool_chain)
                    link(pool.memset(keep, 1.0))
                    link(pool.memset(keep.rearrange("p (c t) -> p c t", c=NC_R)[:, :, 0:1], 0.0))
                    link(pool.tensor_copy(low_st_d, low_st))
                    for r in range(P // RB - 1):
                        link(pool.memset(low_st_d[r * RB:(r + 1) * RB, (r + 1) * RB:P], 0.0))
                    pool.tensor_copy(cols[:, 32:33], one_col).then_inc(consts.sem, 1)
                    with pool.Fori(0, NK) as i:
                        pool.wait_ge(E["yc"], i + 1)
                        pool.tensor_copy(w2a2_now, w2a2[:, bass.ds(i * P, P)]).then_inc(E["lora2"], 1)
                        pool.tensor_copy(V, v3[:, :, bass.ds(i * P, P)]).then_inc(E["val"], 1)
                        pool.wait_ge(E["q2"], i + 1)
                        for e in range(2):
                            off = slice((1 - e) * HD, (2 - e) * HD)
                            zero = low_st[rows_of(e), off].unsqueeze(1).to_broadcast([HD, NC_R, HD])
                            ins = pool.tensor_tensor(MT[rows_of(e), :, off], zero, zero, ALU.add)
                        ins.then_inc(E["mt0"], 1)

                @block.tensor
                def _(pe):
                    with pe.Fori(0, NK) as i:
                        pe.wait_ge(E["yc"], i + 1)
                        pe.wait_ge(E["lora2"], i + 1)
                        for e in range(2):
                            ins = pe.matmul(ps[:, e, :], w2a2_now[rows_of(e), :], h_wa[rows_of(e), :],
                                            start=True, stop=True)
                        ins.then_inc(E["lora"], 1)
                        pe.wait_ge(E["sq"], i + 1)
                        pe.matmul(ps[:, 2, :], same_head, kk, start=True, stop=True).then_inc(E["ssq"], 1)
                        pe.wait_ge(E["ops"], i + 1)
                        for n, src in enumerate((A_T, B_T.rearrange(tile4, j=NT), K_T.rearrange(tile4, j=NT))):
                            for j in range(NT):
                                pe.transpose(ps[:, 3 + n, j * P:(j + 1) * P], src[:, j, :], ident)
                        for j in range(NT):
                            ins = pe.matmul(ps[:, 6, 2 * j:2 * j + 2], decay[:, j * P:(j + 1) * P], same_head[:, 0:P:HD],
                                            start=True, stop=True)
                        ins.then_inc(E["turned"], 1)
                        for u, (e, j) in enumerate(units):
                            ins = pe.matmul(ps[:, e, j * P:(j + 1) * P], A_T[rows_of(e), j, :],
                                            B_T[rows_of(e), j * P:(j + 1) * P], start=True, stop=True)
                        ins.then_inc(E["low"], 1)
                        for u, (e, j) in enumerate(units):
                            bank = (u + 2) % 8
                            if u == 1:
                                pe.wait_ge(E["tok"], i + 1)
                            if u == 6:
                                pe.wait_ge(E["lowm"], i + 1)
                            for n, src in enumerate((B_T, K_T)):
                                ins = pe.matmul(ps[:, bank, 2 * n * P:2 * (n + 1) * P], src[rows_of(e), j * P:(j + 1) * P],
                                                AR[rows_of(e), j, :, :], start=True, stop=True)
                            ins.then_inc(p_akm, 1)
                        for r in range(ROUNDS):
                            for u in range(8):
                                if r == 0:
                                    pe.wait_ge(d_akm, i * 8 + min(u + 7, 8))
                                else:
                                    pe.wait_ge(a_sq, i * 8 * ROUNDS + 8 * (r - 1) + u + 1)
                                    pe.wait_ge(d_tt, i * 8 * ROUNDS + 8 * (r - 1) + u + 1)
                                x, xt = XX[:, u, 0:P], XX[:, u, P:2 * P]
                                pe.matmul(ps[:, u, 0:P], xt, x, start=True, stop=True)
                                pe.matmul(ps[:, u, P:2 * P], x, xt, start=True, stop=True).then_inc(p_sq, 1)
                            for u in range(8):
                                pe.wait_ge(a_sq, i * 8 * ROUNDS + 8 * r + u + 1)
                                pe.matmul(ps[:, u, 2 * P:3 * P], XX[:, u, 0:P], TT[:, u, :], start=True, stop=True)\
                                  .then_inc(p_tt, 1)
                        pe.wait_ge(d_tt, (i + 1) * (8 * ROUNDS))
                        pe.wait_ge(E["val"], i + 1)
                        for u, (e, j) in enumerate(units):
                            ins = pe.matmul(ps[:, 0, u * HD:(u + 1) * HD], AKM[:, u, 2 * P:3 * P], V[:, j, rows_of(e)],
                                            start=True, stop=True)
                        ins.then_inc(E["lkv"], 1)
                        for u, (e, j) in enumerate(units):
                            ins = pe.matmul(ps[:, 1 + u // 4, (u % 4) * P:(u % 4) * P + HD], TT[:, u, :], A_tok[:, j, rows_of(e)],
                                            start=True, stop=True)
                        pe.wait_ge(E["lkvc"], i + 1)
                        for u, (e, j) in enumerate(units):
                            ins = pe.matmul(ps[:, 1 + u // 4, (u % 4) * P + HD:(u % 4 + 1) * P], TT[:, u, :], LKV[:, u, :],
                                            start=True, stop=True)
                        ins.then_inc(E["q"], 1)
                        pe.wait_ge(E["qc"], i + 1)
                        for u in range(8):
                            ins = pe.matmul(ps[:, 5 + u // 4, (u % 4) * P:(u % 4 + 1) * P], AKM[:, u, 0:P], QC[:, u, :],
                                            start=True, stop=True)
                        ins.then_inc(E["z"], 1)
                        pe.wait_ge(E["zc"], i + 1)
                        for u in range(8):
                            ins = pe.matmul(ps[:, 1 + u // 4, (u % 4) * P:(u % 4 + 1) * P], TT[:, u, :], Z[:, u, :],
                                            start=True, stop=True)
                        ins.then_inc(E["q2"], 1)
                        pe.wait_ge(E["q2c"], i + 1)
                        for u, (e, j) in enumerate(units):
                            ins = pe.matmul(ps[rows_of(e), 3, j * P:(j + 1) * P], QC[:, u, 0:HD], AKM[:, u, P:2 * P],
                                            start=True, stop=True)
                        ins.then_inc(E["r2"], 1)
                        for half in range(2):
                            hs = rows_of(half)
                            for u, (e, j) in enumerate(units):
                                at = slice(j * HD, (j + 1) * HD)
                                m, n = ps[rows_of(e), 5 + half, at], ps[rows_of(e), 7 * (1 - half), at]
                                pe.matmul(m, ident[hs, hs], ident[hs, hs], start=True, stop=False)
                                pe.matmul(m, QC[hs, u, 0:HD], B_tok[hs, j, rows_of(e)], start=False, stop=True)
                                pe.matmul(n, B_tok[hs, j, rows_of(e)], QC[hs, u, HD:P], start=True, stop=False)
                                ins = pe.matmul(n, K_tok[hs, j, rows_of(e)], V[hs, j, rows_of(e)], start=False, stop=True)
                        ins.then_inc(E["mn"], 1)
                        for u, (e, j) in enumerate(units):
                            o = ps[:, 4, (2 * j + e) * HD:(2 * j + e + 1) * HD]
                            pe.matmul(o, AKM[:, u, P:2 * P], QC[:, u, HD:P], start=True, stop=False)
                            ins = pe.matmul(o, AKM[:, u, 3 * P:4 * P], V[:, j, rows_of(e)], start=False, stop=True)
                        ins.then_inc(E["y0"], 1)
                        pe.wait_ge(E["mnc"], i + 1)
                        for c in range(1, NC_R):
                            if c >= 2:
                                pe.wait_ge(d_s, i * (NC_R - 1) + c - 1)
                            pe.matmul(ps[:, 1, c * HD:(c + 1) * HD], MT[:, c - 1, :], S[:, c - 1, :],
                                      start=True, stop=True).then_inc(p_s, 1)
                        pe.wait_ge(E["r2c"], i + 1)
                        pe.wait_ge(E["y0c"], i + 1)
                        pe.wait_ge(d_s, (i + 1) * (NC_R - 1))
                        for e, j in units:
                            ins = pe.matmul(ps[:, 3 + e, j * P:(j + 1) * P], R_T[rows_of(e), j, :],
                                            S[rows_of(e), 2 * j:2 * j + 2, :], start=True, stop=True)
                        ins.then_inc(E["yy"], 1)

                @block.scalar
                def _(act):
                    with act.Fori(0, NK) as i:
                        act.wait_ge(E["lora"], i + 1)
                        act.wait_ge(E["par"], i + 1)
                        act.activation(logd, ps[:, 0, :], ACT.Sigmoid, bias=pcol[:, W0:W0 + 1])
                        act.activation(lr, ps[:, 1, :], ACT.Sigmoid, bias=pcol[:, A0:A0 + 1]).then_inc(E["sig"], 1)
                        act.wait_ge(E["shift"], i + 1)
                        act.activation(decay, cum, ACT.Exp)
                        act.activation(inv, cum, ACT.Exp, scale=-1.0)
                        act.activation(before_d, before_d, ACT.Exp)
                        act.wait_ge(E["ssq"], i + 1)
                        act.activation(B_T, ps[:, 2, :], ACT.Sqrt).then_inc(E["exp"], 1)
                        act.wait_ge(E["turned"], i + 1)
                        for n, dst in enumerate((A_tok, B_tok, K_tok)):
                            act.activation(dst, ps[:, 3 + n, :].rearrange(tile4, j=NT), ACT.Copy)
                        act.activation(k3[:, bass.ds(i, 1), 0:2 * NT], ps[:, 6, 0:2 * NT].unsqueeze(1), ACT.Copy).then_inc(E["tok"], 1)
                        for r in range(ROUNDS):
                            for u in range(8):
                                act.wait_ge(p_sq, i * 8 * ROUNDS + 8 * r + u + 1)
                                act.activation(XX[:, u, :], ps[:, u, 0:2 * P], ACT.Copy).then_inc(a_sq, 1)
                        act.wait_ge(E["lkv"], i + 1)
                        act.activation(LKV, ps[:, 0, :].rearrange("p (u c) -> p u c", u=8), ACT.Copy).then_inc(E["lkvc"], 1)
                        act.wait_ge(E["q"], i + 1)
                        act.activation(QC, ps[:, 1:3, :].rearrange("p b (u c) -> p (b u) c", u=4), ACT.Copy).then_inc(E["qc"], 1)
                        act.wait_ge(E["z"], i + 1)
                        act.activation(Z, ps[:, 5:7, :].rearrange("p b (u c) -> p (b u) c", u=4), ACT.Copy).then_inc(E["zc"], 1)
                        act.wait_ge(E["y0"], i + 1)
                        act.activation(Y0, ps[:, 4, :].rearrange("p (j e c) -> p j e c", j=NT, e=2), ACT.Copy).then_inc(E["y0c"], 1)

                @block.vector
                def _(dve):
                    c0 = consts.total + 1
                    dve.memset(mean_var[:, 5:6], 0.0).then_inc(E["yc"], 1)
                    with dve.Fori(0, NK) as i:
                        link = LoopChain(dve, chain_v, i, 13)
                        r_now, k_now = rT[:, bass.ds(i, 1), :].rearrange("p o t -> p (o t)"), k3[:, bass.ds(i, 1), :].rearrange("p o t -> p (o t)")
                        dve.tensor_copy(pcol, par[:, :, bass.ds(i, 1)].rearrange("p n o -> p (n o)")).then_inc(E["par"], 1)
                        dve.wait_ge(E["par"], i + 1)
                        link(dve.tensor_scalar(B_T, k_now, pcol[:, K_K:K_K + 1], None, ALU.mult))
                        dve.tensor_tensor(kk, B_T, B_T, ALU.mult).then_inc(E["sq"], 1)
                        dve.wait_ge(E["sig"], i + 1)
                        dve.wait_ge(consts.sem, c0)
                        link(dve.tensor_scalar(logd, logd, -float(np.exp(-0.5)), None, ALU.mult))
                        link(dve.tensor_tensor_scan(cum, keep, logd, 0.0, ALU.mult, ALU.add))
                        dve.tensor_tensor(before_d, cum, logd, ALU.subtract).then_inc(E["shift"], 1)
                        link(dve.tensor_scalar(K_T, lr, 1.0, pcol[:, K_A:K_A + 1], ALU.subtract, ALU.mult))
                        link(dve.scalar_tensor_tensor(K_T, K_T, 1.0, k_now, ALU.add, ALU.mult))
                        dve.wait_ge(E["exp"], i + 1)
                        link(dve.tensor_scalar(B_T, B_T, 1e-12, None, ALU.max))
                        link(dve.reciprocal(B_T, B_T))
                        link(dve.tensor_scalar(kk, k_now, pcol[:, K_K:K_K + 1], None, ALU.mult))
                        link(dve.tensor_tensor(kk, kk, B_T, ALU.mult))
                        dve.scalar_tensor_tensor(A_T, kk.rearrange(tile4, j=NT), -1.0, before_d.rearrange(tile4, j=NT), ALU.mult, ALU.mult)
                        link(dve.tensor_tensor(B_T, kk, lr, ALU.mult))
                        dve.tensor_tensor(B_T, B_T, inv, ALU.mult)
                        dve.tensor_tensor(R_T, r_now.rearrange(tile4, j=NT), decay.rearrange(tile4, j=NT), ALU.mult)
                        link(dve.tensor_copy(p_end, decay[:, RC - 1::RC]))
                        link(dve.scalar_tensor_tensor(decay, r_now, pcol[:, R_K:R_K + 1], K_T, ALU.mult, ALU.mult))
                        dve.tensor_tensor(K_T, K_T, inv, ALU.mult).then_inc(E["ops"], 1)
                        dve.wait_ge(E["low"], i + 1)
                        dve.wait_ge(E["turned"], i + 1)
                        dve.tensor_tensor(XX[:, :, 0:P], ps[:, 0:2, :].rearrange("p b (u c) -> p (b u) c", u=4),
                                          low_ts.unsqueeze(1).to_broadcast([P, 8, P]), ALU.mult).then_inc(E["lowm"], 1)
                        for u in range(8):
                            dve.wait_ge(p_akm, i * 8 + u + 1)
                            bank = ps[:, (u + 2) % 8, :]
                            dve.tensor_tensor(XX[:, u, P:2 * P], bank[:, 0:P], low_st_d, ALU.mult)
                            dve.tensor_tensor(AKM[:, u, :].rearrange("p (a c) -> p a c", a=2),
                                              bank.rearrange("p (a c) -> p a c", a=2),
                                              masks.unsqueeze(1).to_broadcast([P, 2, 2 * P]), ALU.mult).then_inc(d_low, 1)
                            dve.wait_ge(d_low, i * 8 + u + 1)
                            dve.tensor_tensor(AKM[:, u, 0:P], AKM[:, u, 0:P], XX[:, u, P:2 * P], ALU.subtract)
                            dve.tensor_tensor(TT[:, u, :], XX[:, u, P:2 * P], ident, ALU.add).then_inc(d_akm, 1)
                        for r in range(ROUNDS):
                            for u in range(8):
                                dve.wait_ge(p_tt, i * 8 * ROUNDS + 8 * r + u + 1)
                                dve.tensor_tensor(TT[:, u, :], TT[:, u, :], ps[:, u, 2 * P:3 * P], ALU.add).then_inc(d_tt, 1)
                        dve.wait_ge(E["q2"], i + 1)
                        dve.tensor_tensor(QC, QC, ps[:, 1:3, :].rearrange("p b (u c) -> p (b u) c", u=4), ALU.add).then_inc(E["q2c"], 1)
                        dve.wait_ge(E["r2"], i + 1)
                        dve.tensor_tensor(R_T, R_T, ps[:, 3, :].rearrange(tile4, j=NT), ALU.add).then_inc(E["r2c"], 1)
                        dve.wait_ge(E["mn"], i + 1)
                        pe2 = p_end.rearrange("p (j h) -> p j h", h=2)
                        dve.wait_ge(E["mt0"], i + 1)
                        mt, nn = (m.rearrange("p (j h) i -> p j h i", h=2) for m in (MT, NN))
                        for half in range(2):
                            for e in range(2):
                                dve.tensor_copy(mt[rows_of(e), :, half, e * HD:(e + 1) * HD],
                                                ps[rows_of(e), 5 + half, 0:NT * HD].rearrange("p (j i) -> p j i", j=NT))
                            ins = dve.tensor_tensor(nn[:, :, half, :], ps[:, 7 * (1 - half), 0:NT * HD].rearrange("p (j i) -> p j i", j=NT),
                                                    pe2[:, :, half].unsqueeze(2).to_broadcast([P, NT, HD]), ALU.mult)
                        link(ins)
                        dve.memset(S[:, 0, :], 0.0).then_inc(E["mnc"], 1)
                        for c in range(1, NC_R):
                            dve.wait_ge(p_s, i * (NC_R - 1) + c)
                            dve.scalar_tensor_tensor(S[:, c, :], ps[:, 1, c * HD:(c + 1) * HD], p_end[:, c - 1:c],
                                                     NN[:, c - 1, :], ALU.mult, ALU.add).then_inc(d_s, 1)
                        dve.wait_ge(E["yy"], i + 1)
                        for e in range(2):
                            for h in range(2):
                                ins = dve.tensor_tensor(r_now[rows_of(h), :].rearrange("p (j e v) -> p j e v", j=NT, e=2)[:, :, e, :],
                                                        ps[rows_of(h), 3 + e, :].rearrange("p (j v) -> p j v", j=NT)[:, :, rows_of(h)],
                                                        Y0[rows_of(h), :, e, :], ALU.add)
                        ins.then_inc(E["yc"], 1)
                        link.end()
            consts.take(1)

        def wkv_out_stage():
            y = arena[:, 0:NK * T].rearrange("p (n v) -> p n v", v=HD)
            by_tile = "p (c j v) -> p c j v"
            yc = arena[:, 0:NK * T].rearrange(by_tile, c=NK, j=NT)
            tmp = arena[:, NK * T:2 * NK * T].rearrange("p (n v) -> p n v", v=HD)
            tmp_c = arena[:, NK * T:2 * NK * T].rearrange(by_tile, c=NK, j=NT)
            g2a, g2b, ln_g, ln_b = (view(arena, 3 * NK * T + n * D, D) for n in range(4))
            bonus_all = view(rows, 128, NK, NT, 2)
            mean, var = view(rows, 0, 64), view(rows, 64, 64)
            l0, x0, a0, m0 = loaded.take(64), dve_a.take(1), act_a.take(1), mm.take(2 * NT)

            def by_channel(row):
                return row.rearrange("p (c v) -> p c v", c=NK).unsqueeze(2).to_broadcast([P, NK, NT, P])

            with nc.Block() as block:
                @block.sync
                def _(sp):
                    stream_mixer(sp, mixer_at[2] + 11, mixer_at[2] + 12)

                @block.gpsimd
                def _(pool):
                    for dst, src in ((g2a, a["rw_g2_2"][0][0:P]), (g2b[0:GATE_LORA - P, :], a["rw_g2_2"][0][P:GATE_LORA]),
                                     (ln_g, a["rw_lnx_g_2"][0].partition_broadcast(P)),
                                     (ln_b, a["rw_lnx_b_2"][0].partition_broadcast(P))):
                        pool.dma_start(dst, src).then_inc(loaded.sem, 16)

                @block.tensor
                def _(pe):
                    pe.wait_ge(loaded.sem, l0 + 64)
                    for n in range(2 * NT):
                        j, c = n // 2, n % 2
                        pe.matmul(ps[:, n, :], h_g[:, j * P:(j + 1) * P], g2a[:, c * CH:(c + 1) * CH], start=True, stop=False)
                        pe.matmul(ps[:, n, :], h_g2[:, j * P:(j + 1) * P], g2b[0:GATE_LORA - P, c * CH:(c + 1) * CH],
                                  start=False, stop=True).then_inc(mm.sem, 1)

                @block.scalar
                def _(act):
                    act.wait_ge(dve_a.sem, x0 + 1)
                    act.activation(var, var, ACT.Sqrt, bias=eps_gn).then_inc(act_a.sem, 1)

                @block.vector
                def _(dve):
                    link = Chain(dve, dve_chain)
                    wide = [P, 64, HD]
                    link(dve.tensor_copy(bonus_all.rearrange("p c j e -> p c (j e)"), k3[:, :, 0:2 * NT]))
                    link(dve.tensor_reduce(mean, y, AX, ALU.add))
                    link(dve.tensor_scalar(mean, mean, 1.0 / HD, None, ALU.mult))
                    link(dve.tensor_tensor(y, y, mean.unsqueeze(2).to_broadcast(wide), ALU.subtract))
                    link(dve.tensor_tensor(tmp, y, y, ALU.mult))
                    link(dve.tensor_reduce(var, tmp, AX, ALU.add))
                    dve.tensor_scalar(var, var, 1.0 / HD, None, ALU.mult).then_inc(dve_a.sem, 1)
                    for c in range(NK):
                        ins = dve.tensor_tensor(tmp_c[:, c, :, :].rearrange("p j (e v) -> p j e v", e=2),
                                                v3[:, :, c * P:(c + 1) * P].rearrange("p j (e v) -> p j e v", e=2),
                                                bonus_all[:, c, :, :].unsqueeze(3).to_broadcast([P, NT, 2, HD]), ALU.mult)
                    link(ins)
                    dve.wait_ge(act_a.sem, a0 + 1)
                    link(dve.reciprocal(var, var))
                    link(dve.tensor_tensor(y, y, var.unsqueeze(2).to_broadcast(wide), ALU.mult))
                    dve.wait_ge(loaded.sem, l0 + 64)
                    link(dve.tensor_tensor(yc, yc, by_channel(ln_g), ALU.mult))
                    link(dve.tensor_tensor(yc, yc, by_channel(ln_b), ALU.add))
                    link(dve.tensor_tensor(y, y, tmp, ALU.add))
                    for n in range(2 * NT):
                        j, c = n // 2, n % 2
                        dve.wait_ge(mm.sem, m0 + n + 1)
                        dve.tensor_tensor(yc[:, 4 * c:4 * c + 4, j, :], yc[:, 4 * c:4 * c + 4, j, :],
                                          ps[:, n, :].rearrange("p (c v) -> p c v", c=4), ALU.mult)

        def store_stage():
            o0 = stored.take(16)
            with nc.Block() as block:
                @block.sync
                def _(sp):
                    sp.dma_start(out[0].rearrange("(j p) d -> p j d", p=P), x_tok).then_inc(stored.sem, 16)
                    sp.wait_ge(stored.sem, o0 + 16)

        def program():
            start_stage()
            in_proj_stage()
            decay_stage()
            ssd_stage()
            attention_stage(1, lambda h, c: qT[HD * (h % 2):HD * (h % 2 + 1), h // 2, :],
                            lambda h, c: kT[HD * (h % 2):HD * (h % 2 + 1), h // 2, :], v_tok, HD,
                            lambda h, j: merged_a[:, j, h * HD:(h + 1) * HD], forget=True)
            mT = view(arena, 0, NK, T)
            transpose_stage(lambda j, k: (merged_s if k < 4 else merged_a)[:, j, (k % 4) * P:(k % 4 + 1) * P], mT)
            project_out_stage(0, ALPHA_1, mT, a["ln1_g"][0], a["ln1_b"][0])
            if stop == "h1":
                return
            moe_stage(0, ALPHA_1, a["ln2_g"][0], a["ln2_b"][0], False)
            if stop == "x1":
                return
            qkv_stage()
            attention_stage(2, lambda h, c: q2[HD * c:HD * (c + 1), h, :], lambda h, c: k2[HD * c:HD * (c + 1), h, :],
                            v2, 2 * HD, lambda h, j: o2[:, j, h * P:(h + 1) * P], lam=lam)
            subln_stage()
            transpose_stage(lambda j, k: o2[:, j, k * P:(k + 1) * P], mT)
            project_out_stage(1, ALPHA_2, mT, a["ln1_g_2"][0], a["ln1_b_2"][0])
            if stop == "h2":
                return
            moe_stage(1, ALPHA_2, a["ln2_g_2"][0], a["ln2_b_2"][0], False)
            if stop == "x2":
                return
            rkv_stage()
            wkv_stage()
            wkv_out_stage()
            mT3 = view(arena, NK * T, NK, T)
            y3 = rT.rearrange("p c (j v) -> p c j v", j=NT)
            transpose_stage(lambda j, k: y3[:, k, j, :], mT3)
            project_out_stage(2, ALPHA_2, mT3, a["ln1_g_2"][1], a["ln1_b_2"][1])
            if stop == "h3":
                return
            moe_stage(2, ALPHA_2, a["ln2_g_2"][1], a["ln2_b_2"][1], True)

        program()
        store_stage()


_INS = ["x", "w_in", "b_in", "conv_w", "conv_b", "a_log", "d_skip", "ssd_norm_g", "w_out", "ln1_g", "ln1_b",
        "router_group_w", "router_group_b", "router_expert_w", "router_expert_b", "w_gate", "w_up", "w_down",
        "ln2_g", "ln2_b", "ln1_g_2", "ln1_b_2", "ln2_g_2", "ln2_b_2", "attn_w_qkv_2", "attn_w_o_2", "attn_lambda_2",
        "attn_subln_g_2", "rw_mu_2", "rw_w_rkv_2", "rw_w_o_2", "rw_w0_2", "rw_w1_2", "rw_w2_2", "rw_a0_2", "rw_a1_2",
        "rw_a2_2", "rw_g1_2", "rw_g2_2", "rw_k_k_2", "rw_k_a_2", "rw_r_k_2", "rw_lnx_g_2", "rw_lnx_b_2",
        "rw_v0_2", "rw_v1_2", "rw_v2_2",
        "moe_rg_w_2", "moe_rg_b_2", "moe_re_w_2", "moe_re_b_2", "moe_w_gu_2", "moe_w_down_2"]
_OUT_SHAPE = (1, T, D)
_STOP = None


def kernel(**inputs):
    import concourse.bacc as bacc
    from concourse.bass_utils import run_bass_kernel_spmd

    nc = bacc.Bacc("TRN2", target_bir_lowering=False, num_devices=1)
    arrays, aps = {}, {}
    for name in _INS:
        arr = np.ascontiguousarray(inputs[name])
        if not arr.size:
            continue
        arrays[f"in_{name}"] = arr
        aps[name] = nc.dram_tensor(f"in_{name}", arr.shape, mybir.dt.from_np(arr.dtype), kind="ExternalInput").ap()
    out = nc.dram_tensor("out", _OUT_SHAPE, F32, kind="ExternalOutput").ap()
    build(nc, aps, out, _STOP)
    r = run_bass_kernel_spmd(nc, [arrays], core_ids=[0])
    return r.results[0]["out"]
```

```python
from contextlib import ExitStack

import numpy as np

import concourse.bass as bass
from concourse import mybir

F32 = mybir.dt.float32
I32 = mybir.dt.int32
U32 = mybir.dt.uint32
ALU = mybir.AluOpType
ACT = mybir.ActivationFunctionType
AX = mybir.AxisListType.X

P = 128
T = 512
D = 1024
NT = T // P
NK = D // P
CH = 512
SLOTS = 6
LN_EPS = 1e-5
RMS_EPS = 1e-5
NEG = -1e30
BLK = 32

HEADS = 8
HD = 64
STATE = 128
GROUPS = 2
CONV_W = 4
O_Z, O_XS, O_BC, O_DT, O_Q, O_K, O_V, O_F = 0, 512, 1024, 1536, 1544, 2056, 2568, 3080
F_ROW = 32
ALPHA_1 = 2.0 ** 0.25
ALPHA_2 = 4.0 ** 0.25
SCALE = HD ** -0.5
LAMBDA_INIT = 0.8 - 0.6
DA_HEADS = 8

RC = 64
NC_R = T // RC
RB = 32
DECAY_LORA, AAA_LORA, GATE_LORA = 64, 64, 160
GN_EPS = 64e-5


class Signal:

    def __init__(self, sem):
        self.sem = sem
        self.total = 0

    def take(self, n):
        base = self.total
        self.total += n
        return base


class Chain:

    def __init__(self, eng, steps):
        self.eng, self.steps = eng, steps

    def __call__(self, ins):
        self.steps.total += 1
        ins.then_inc(self.steps.sem, 1)
        self.eng.wait_ge(self.steps.sem, self.steps.total)


def build(nc, a, out, stop=None):
    ctx = ExitStack()
    with ctx:
        def sb(name, cols, dt=F32):
            return ctx.enter_context(nc.sbuf_tensor(name, [P, cols], dt))

        def signal(name):
            return Signal(ctx.enter_context(nc.semaphore(name)))

        ring = sb("ring", SLOTS * NK * CH)
        x_tok = sb("x_tok", NT * D)[:, :].rearrange("p (j d) -> p j d", j=NT)
        xt_mem = sb("xt_mem", NK * T)
        xT = xt_mem[:, :].rearrange("p (k t) -> p k t", k=NK)
        arena = sb("arena", 16448)
        rows = sb("rows", 2 * D)
        cst = sb("cst", 8 * P + BLK + 64)
        small = sb("small", 760)
        ps = ctx.enter_context(nc.psum_tensor("ps", [P, 8, 512], F32))
        ybuf = nc.dram_tensor("ybuf", [(2 * T // BLK + 32) * BLK, D], F32).ap()

        def const(n, w=P):
            return cst[:, n * P:n * P + w]

        ident, mask_qk, mask_sq, before, ones, low_ts, low_st, upto_st = (const(n) for n in range(8))
        iota_f = cst[:, 8 * P:8 * P + BLK]
        cols = cst[:, 8 * P + BLK:8 * P + BLK + 64]
        eps_ln = cols[:, 0:1]
        one_col = cols[:, 1:2]
        eps_gn = cols[:, 2:3]

        def view(mem, at, *shape):
            n = int(np.prod(shape))
            v = mem[:, at:at + n]
            if len(shape) == 2:
                return v.rearrange("p (a b) -> p a b", a=shape[0])
            if len(shape) == 3:
                return v.rearrange("p (a b c) -> p a b c", a=shape[0], b=shape[1])
            return v

        def slot(n):
            return ring[:, n * NK * CH:(n + 1) * NK * CH]

        arrived = [signal(f"chunk_arrived{n}") for n in range(SLOTS)]
        arrived_x = [signal(f"third_expert_{kind}_arrived") for kind in ("gate", "up", "down")]
        loaded = signal("params_loaded")
        x_loaded = signal("x_loaded")
        zeroed = signal("ybuf_zeroed")
        consts = signal("consts_ready")
        mm = signal("matmuls_done")
        tr = signal("transposes_done")
        ev = signal("act_evacuated")
        dv = signal("dve_evacuated")
        dve_chain = signal("dve_chain")
        act_chain = signal("act_chain")
        pool_chain = signal("pool_chain")
        ln_done = signal("ln_done")
        stat = signal("variance_ready")
        sq = signal("deviation_ready")
        stored = signal("output_stored")
        pe_a = signal("pe_a_done")
        pe_b = signal("pe_b_done")
        pe_c = signal("pe_c_done")
        act_a = signal("act_a_done")
        act_b = signal("act_b_done")
        dve_a = signal("dve_a_done")
        dve_b = signal("dve_b_done")
        dve_c = signal("dve_c_done")

        def cols_of(w, c0):
            return w.rearrange("(k p) n -> p k n", p=P)[:, :, c0:c0 + CH]

        def layer_chunks(ws):
            return [cols_of(w, c) for w, cs in ws for c in cs]

        w_in, w_out = a["w_in"][0], a["w_out"][0]
        w_qkv, w_o2 = a["attn_w_qkv_2"][0], a["attn_w_o_2"][0]
        rkv, w_o3 = a["rw_w_rkv_2"][0], a["rw_w_o_2"][0]
        stream = []
        mixer_at, moe_at = [], []
        n_experts = [16, 32, 32]
        for n, ws in enumerate((
                [(w_in, (O_Z, O_XS, O_BC, O_Q, O_K, O_V)), (w_out, (0, CH))],
                [(w_qkv, range(0, 3 * D, CH)), (w_o2, (0, CH))],
                [(rkv[0], (0, CH)), (rkv[1], (0, CH)), (rkv[2], (0, CH)), (w_o3, (0, CH))])):
            mixer_at.append(len(stream))
            stream += layer_chunks(ws)
            moe_at.append(len(stream))
            stream += [None] * (3 * (n_experts[n] - n_experts[n] // 3))

        def chunk_dst(src, n):
            return slot(n % SLOTS).rearrange("p (k n) -> p k n", k=src.shape[1])

        def load_chunk(eng, n):
            eng.dma_start(chunk_dst(stream[n], n), stream[n]).then_inc(arrived[n % SLOTS].sem, 16)

        def wait_chunk(eng, n):
            eng.wait_ge(arrived[n % SLOTS].sem, 16 * (n // SLOTS + 1))

        gu = a["moe_w_gu_2"]
        gate_src = [a["w_gate"][0], gu[0][:, :, 0:CH], gu[1][:, :, 0:CH]]
        up_src = [a["w_up"][0], gu[0][:, :, CH:D], gu[1][:, :, CH:D]]
        down_src = [a["w_down"][0], a["moe_w_down_2"][0], a["moe_w_down_2"][1]]

        def kinds(n):
            return (0, 1, 2) if n % SLOTS != SLOTS - 1 else (2, 0, 1)

        def expert_src(l, e, kind):
            return (gate_src, up_src, down_src)[kind][l][bass.ds(e, 1), :, :].rearrange("e (k p) n -> p (e k) n", p=P)

        def load_expert_chunk(eng, l, e, j, n):
            src = expert_src(l, e, kinds(n - j)[j])
            eng.dma_start(chunk_dst(src, n), src).then_inc(arrived[n % SLOTS].sem, 16)

        used = {}

        def stream_mixer(sp, first, last):
            for n in range(first, last):
                if n - SLOTS in used:
                    sp.wait_ge(*used[n - SLOTS])
                if stream[n] is not None:
                    load_chunk(sp, n)
                else:
                    l = max(i for i in range(3) if moe_at[i] <= n)
                    load_expert_chunk(sp, l, (n - moe_at[l]) // 3, (n - moe_at[l]) % 3, n)

        def transpose_stage(src, dst):
            t0 = tr.take(NK)
            with nc.Block() as block:
                @block.tensor
                def _(pe):
                    for k in range(NK):
                        for j in range(NT):
                            ins = pe.transpose(ps[:, k, j * P:(j + 1) * P], src(j, k), ident)
                        ins.then_inc(tr.sem, 1)

                @block.scalar
                def _(act):
                    for k in range(0, NK, 2):
                        act.wait_ge(tr.sem, t0 + k + 1)
                        act.activation(dst[:, k, :], ps[:, k, :], ACT.Copy)

                @block.vector
                def _(dve):
                    for k in range(1, NK, 2):
                        dve.wait_ge(tr.sem, t0 + k + 1)
                        dve.tensor_copy(dst[:, k, :], ps[:, k, :])

        mean_var = view(small, 0, 32)
        g_row, b_row = view(rows, 0, D), view(rows, D, D)

        def normalise(dve, link, j, sq_at):
            xj = x_tok[:, j, :]
            st = mean_var[:, 16:28]
            for c in range(2):
                ins = dve.bn_stats(st[:, 6 * c:6 * c + 6], xj[:, c * CH:(c + 1) * CH])
            link(ins)
            dve.bn_aggr(mean_var[:, 0:2], st).then_inc(stat.sem, 1)
            dve.wait_ge(sq.sem, sq_at + j + 1)
            link(dve.reciprocal(mean_var[:, 3:4], mean_var[:, 2:3]))
            link(dve.tensor_scalar(xj, xj, mean_var[:, 0:1], mean_var[:, 3:4], ALU.subtract, ALU.mult))
            link(dve.tensor_tensor(xj, xj, g_row, ALU.mult))
            link(dve.tensor_tensor(xj, xj, b_row, ALU.add))

        def deviations(act, stat_at):
            for j in range(NT):
                act.wait_ge(stat.sem, stat_at + j + 1)
                act.activation(mean_var[:, 2:3], mean_var[:, 1:2], ACT.Sqrt, bias=eps_ln).then_inc(sq.sem, 1)

        def load_norm_rows(pool, g_src, b_src):
            pool.dma_start(g_row, g_src.partition_broadcast(P)).then_inc(loaded.sem, 16)
            pool.dma_start(b_row, b_src.partition_broadcast(P)).then_inc(loaded.sem, 16)

        def project_out_stage(l, alpha, mT, g_src, b_src):
            first = moe_at[l] - 2
            m0, s0, q0, l0 = mm.take(2 * NT), stat.take(NT), sq.take(NT), loaded.take(32)
            for c in range(2):
                used[first + c] = (mm.sem, m0 + 2 * NT - 1 + c)
            with nc.Block() as block:
                @block.sync
                def _(sp):
                    stream_mixer(sp, first + SLOTS, first + SLOTS + 2)

                @block.gpsimd
                def _(pool):
                    load_norm_rows(pool, g_src, b_src)

                @block.tensor
                def _(pe):
                    for j in range(NT):
                        for c in range(2):
                            if j == 0:
                                wait_chunk(pe, first + c)
                            w = slot((first + c) % SLOTS).rearrange("p (k n) -> p k n", k=NK)
                            for k in range(NK):
                                ins = pe.matmul(ps[:, 2 * j + c, :], mT[:, k, j * P:(j + 1) * P], w[:, k, :],
                                                start=(k == 0), stop=(k == NK - 1))
                            ins.then_inc(mm.sem, 1)

                @block.scalar
                def _(act):
                    deviations(act, s0)

                @block.vector
                def _(dve):
                    link = Chain(dve, dve_chain)
                    for j in range(NT):
                        for c in range(2):
                            dve.wait_ge(mm.sem, m0 + 2 * j + c + 1)
                            xc = x_tok[:, j, c * CH:(c + 1) * CH]
                            ins = dve.scalar_tensor_tensor(xc, xc, alpha, ps[:, 2 * j + c, :],
                                                           ALU.mult, ALU.add)
                        link(ins)
                        if j == 0:
                            dve.wait_ge(loaded.sem, l0 + 32)
                        normalise(dve, link, j, q0)
            transpose_stage(lambda j, k: x_tok[:, j, k * P:(k + 1) * P], xT)

        zeros = view(arena, 14368, D)

        def start_stage():
            l0, z0 = x_loaded.take(16), consts.take(1)
            zeroed.take(16)
            with nc.Block() as block:
                @block.sync
                def _(sp):
                    sp.dma_start(x_tok, a["x"][0].rearrange("(j p) d -> p j d", p=P)).then_inc(x_loaded.sem, 16)
                    stream_mixer(sp, 0, SLOTS)
                    sp.wait_ge(x_loaded.sem, l0 + 16)

                @block.scalar
                def _(act):
                    act.wait_ge(consts.sem, z0 + 1)
                    act.dma_start(ybuf.rearrange("(r p) d -> p r d", p=P),
                                  zeros.unsqueeze(1).to_broadcast([P, ybuf.shape[0] // P, D])).then_inc(zeroed.sem, 16)

                @block.gpsimd
                def _(pool):
                    link = Chain(pool, pool_chain)
                    pool.memset(zeros, 0.0).then_inc(consts.sem, 1)

                    def select(m, fill, op, base, step, mult):
                        link(pool.affine_select(out=m, in_=m, pattern=[[step, P]], compare_op=op, fill=fill,
                                                base=base, channel_multiplier=mult))

                    for m, v in ((ident, 0.0), (mask_qk, 0.0), (mask_sq, 0.0), (before, 1.0), (ones, 1.0),
                                 (low_ts, 1.0), (low_st, 1.0), (upto_st, 1.0)):
                        pool.memset(m, v)
                    pool.memset(eps_ln, LN_EPS)
                    pool.memset(one_col, 1.0)
                    pool.memset(eps_gn, GN_EPS)
                    link(pool.iota(iota_f, pattern=[[1, BLK]], base=0, channel_multiplier=0,
                                   allow_small_or_imprecise_dtypes=True))
                    select(ident, 1.0, ALU.not_equal, 0, -1, 1)
                    select(mask_qk, NEG, ALU.is_ge, 0, -1, 1)
                    select(mask_sq, NEG, ALU.is_ge, 0, 1, -1)
                    select(before, 0.0, ALU.is_gt, 0, 1, -1)
                    select(low_ts, 0.0, ALU.is_gt, 0, -1, 1)
                    select(low_st, 0.0, ALU.is_gt, 0, 1, -1)
                    select(upto_st, 0.0, ALU.is_ge, 0, 1, -1)
                    for m in (low_st, upto_st):
                        link(pool.memset(m[0:RC, RC:P], 0.0))
                    for r in range(1, P // RB):
                        link(pool.memset(low_ts[r * RB:(r + 1) * RB, 0:r * RB], 0.0))
            transpose_stage(lambda j, k: x_tok[:, j, k * P:(k + 1) * P], xT)

        xbc = view(arena, 0, 8, 516)
        xbc_a = view(arena, 4128, 8, T)
        z_s = view(arena, 8224, NT, T)
        v_tok = view(arena, 10272, NT, T)
        qT = view(arena, 12320, 4, T)
        kT = view(arena, 14368, 4, T)
        gate_u = rows[0:64, 1024:1536]
        gate_c = rows[0:64, 1536:2048]

        def in_proj_stage():
            wsmall = view(arena, 4128, NK, 64)
            brow = rows[0:1, 0:2 * T]
            bcol = view(small, 32, 16)
            convw = view(small, 48, 8, CONV_W)
            convb = view(small, 80, 8)
            sign, bgate = small[0:64, 88:89], small[0:64, 89:90]
            b_in = a["b_in"][0]
            l0, c0, m0, e0, z0 = loaded.take(16 * 13), consts.take(1), mm.take(25), ev.take(25), dve_a.take(32)
            first = mixer_at[0]
            for c in range(6):
                used[first + c] = (mm.sem, m0 + 1 + 4 * (c + 1))
            with nc.Block() as block:
                @block.sync
                def _(sp):
                    stream_mixer(sp, first + SLOTS, first + 12)

                @block.gpsimd
                def _(pool):
                    link = Chain(pool, pool_chain)
                    pool.memset(wsmall, 0.0)
                    pool.memset(sign, -1.0)
                    pool.memset(bgate, 0.0)
                    link(pool.memset(xbc[:, :, 0:CONV_W - 1], 0.0))
                    link(pool.memset(sign[0:32, :], 1.0))

                    def load(dst, src):
                        pool.dma_start(dst, src).then_inc(loaded.sem, 16)

                    wk = w_in.rearrange("(k p) n -> p k n", p=P)
                    with nc.allow_non_contiguous_dma("bias columns"):
                        load(wsmall[:, :, 0:HEADS], wk[:, :, O_DT:O_DT + HEADS])
                        load(wsmall[:, :, F_ROW:F_ROW + HEADS], wk[:, :, O_F:O_F + HEADS])
                        load(bgate[0:HEADS, :], b_in[O_DT:O_DT + HEADS].unsqueeze(1))
                        load(bgate[F_ROW:F_ROW + HEADS, :], b_in[O_F:O_F + HEADS].unsqueeze(1))
                        load(brow[:, 0:T], b_in[O_Z:O_Z + T].unsqueeze(0))
                        load(brow[:, T:2 * T], b_in[O_V:O_V + T].unsqueeze(0))
                        load(bcol[:, 0:8], b_in[O_XS:O_XS + 8 * P].rearrange("(c p) -> p c", p=P))
                        load(bcol[:, 8:16], b_in[O_Q:O_Q + 8 * P].rearrange("(c p) -> p c", p=P))
                        for k in range(CONV_W):
                            load(convw[:, :, k], a["conv_w"][0][k].rearrange("(c p) -> p c", p=P))
                        load(convb, a["conv_b"][0].rearrange("(c p) -> p c", p=P))
                    pool.wait_ge(loaded.sem, l0 + 16 * 13)
                    pool.tensor_tensor(bgate, bgate, sign, ALU.mult).then_inc(consts.sem, 1)

                def is_tok(c):
                    return c in (0, 5)

                @block.tensor
                def _(pe):
                    pe.wait_ge(loaded.sem, l0 + 16 * 13)
                    for n in range(25):
                        if n >= 8:
                            pe.wait_ge(ev.sem, e0 + n - 7)
                        bank = ps[:, n % 8, :]
                        if n == 0:
                            for k in range(NK):
                                ins = pe.matmul(bank[0:64, :], wsmall[:, k, :], xT[:, k, :],
                                                start=(k == 0), stop=(k == NK - 1))
                            ins.then_inc(mm.sem, 1)
                            continue
                        c, j = (n - 1) // 4, (n - 1) % 4
                        if j == 0:
                            wait_chunk(pe, first + c)
                        w = slot((first + c) % SLOTS).rearrange("p (k n) -> p k n", k=NK)
                        if is_tok(c):
                            pe.matmul(bank, ones[0:1, :], brow[:, (c // 5) * T:(c // 5 + 1) * T], start=True, stop=False)
                        for k in range(NK):
                            if is_tok(c):
                                ins = pe.matmul(bank, xT[:, k, j * P:(j + 1) * P], w[:, k, :],
                                                start=False, stop=(k == NK - 1))
                            else:
                                ins = pe.matmul(bank, w[:, k, j * P:(j + 1) * P], xT[:, k, :],
                                                start=(k == 0), stop=(k == NK - 1))
                        ins.then_inc(mm.sem, 1)

                @block.scalar
                def _(act):
                    act.wait_ge(consts.sem, c0 + 1)
                    for n in range(25):
                        act.wait_ge(mm.sem, m0 + n + 1)
                        bank = ps[:, n % 8, :]
                        c, j = (n - 1) // 4, (n - 1) % 4
                        if (c, j) == (4, 0):
                            act.wait_ge(zeroed.sem, 16)
                        if n == 0:
                            ins = act.activation(gate_u, bank[0:64, :], ACT.Identity, bias=bgate, scale=sign)
                        elif c == 0:
                            ins = act.activation(z_s[:, j, :], bank, ACT.Silu)
                        elif c == 5:
                            ins = act.activation(v_tok[:, j, :], bank, ACT.Copy)
                        else:
                            dst = (xbc[:, j, 3:515], xbc[:, 4 + j, 3:515], qT[:, j, :], kT[:, j, :])[c - 1]
                            ins = act.activation(dst, bank, ACT.Identity, bias=bcol[:, 4 * (c - 1) + j:4 * (c - 1) + j + 1])
                        ins.then_inc(ev.sem, 1)
                    for c in range(8):
                        act.wait_ge(dve_a.sem, z0 + 25 + c)
                        act.activation(xbc_a[:, c, :], xbc_a[:, c, :], ACT.Silu)

                @block.vector
                def _(dve):
                    dve.wait_ge(consts.sem, c0 + 1)
                    dve.wait_ge(mm.sem, m0 + 1)
                    for k in range(CONV_W):
                        tap = CONV_W - 1 - k
                        for c in range(8):
                            if k == 0:
                                dve.wait_ge(ev.sem, e0 + 5 + c + 1)
                            else:
                                dve.wait_ge(dve_a.sem, z0 + 8 * (k - 1) + c + 1)
                            shifted = xbc[:, c, tap:tap + T]
                            if k == 0:
                                ins = dve.tensor_scalar(xbc_a[:, c, :], shifted, convw[:, c, tap:tap + 1],
                                                        convb[:, c:c + 1], ALU.mult, ALU.add)
                            else:
                                ins = dve.scalar_tensor_tensor(xbc_a[:, c, :], shifted, convw[:, c, tap:tap + 1],
                                                               xbc_a[:, c, :], ALU.mult, ALU.add)
                            ins.then_inc(dve_a.sem, 1)

        xs_tok = view(arena, 0, NT, T)
        xdt = view(arena, 2048, NT, T)
        merged_s = view(arena, 4128, NT, T)
        merged_a = view(arena, 4128 + 2048, NT, T)
        CB_AT = (0, 512, 896, 1152)
        TRI = 1280
        cb = view(xt_mem, 0, GROUPS, TRI)
        sel = view(rows, 0, HEADS, P)
        gate_c_tok = view(small, 96, NT, 64)
        gate_u_tok = view(small, 96 + 256, NT, 64)
        dskip = view(small, 620, HEADS)
        coef = small[0:64, 628:629]
        neg_c = view(small, 630, NT, HEADS)
        sumsq = view(small, 664, 32)

        def decay_stage():
            tmp = xt_mem[0:64, 3072:3584]
            l0, a0, d0 = loaded.take(32), act_a.take(6), dve_a.take(1)
            t0, b0, e0 = tr.take(5), pe_a.take(8), dve_b.take(8)
            with nc.Block() as block:
                @block.gpsimd
                def _(pool):
                    with nc.allow_non_contiguous_dma("one value per partition"):
                        pool.dma_start(coef[0:HEADS, :], a["a_log"][0].unsqueeze(1)).then_inc(loaded.sem, 16)
                    pool.dma_start(dskip, a["d_skip"][0].partition_broadcast(P)).then_inc(loaded.sem, 16)
                    pool.wait_ge(loaded.sem, l0 + 32)

                @block.scalar
                def _(act):
                    link = Chain(act, act_chain)
                    act.wait_ge(loaded.sem, l0 + 32)
                    act.activation(coef[0:HEADS, :], coef[0:HEADS, :], ACT.Exp).then_inc(act_a.sem, 1)
                    link(act.activation(tmp, gate_u, ACT.Abs))
                    link(act.activation(tmp, tmp, ACT.Exp, scale=-1.0))
                    act.activation(tmp, tmp, ACT.Ln, bias=one_col[0:64, :]).then_inc(act_a.sem, 1)
                    for j in range(NT):
                        act.wait_ge(tr.sem, t0 + j + 1)
                        act.activation(xs_tok[:, j, :], ps[:, j, :], ACT.Copy).then_inc(act_a.sem, 1)

                @block.vector
                def _(dve):
                    link = Chain(dve, dve_chain)
                    dve.wait_ge(act_a.sem, a0 + 2)
                    link(dve.tensor_scalar(gate_u, gate_u, 0.0, None, ALU.max))
                    link(dve.tensor_tensor(gate_u, gate_u, tmp, ALU.add))
                    dve.tensor_scalar(tmp[32:64, :], gate_u[32:64, :], -1.0, None, ALU.mult)
                    link(dve.tensor_scalar(tmp[0:32, :], gate_u[0:32, :], -1.0, None, ALU.mult))
                    link(dve.tensor_scalar(tmp[0:HEADS, :], tmp[0:HEADS, :], coef[0:HEADS, :], None, ALU.mult))
                    dve.tensor_tensor_scan(gate_c, ones[0:64, 0:1].to_broadcast([64, T]), tmp, 0.0,
                                           ALU.mult, ALU.add).then_inc(dve_a.sem, 1)
                    link(dve.tensor_copy(sel[0:64, :, :],
                                         ident[0:64, 0:HEADS].unsqueeze(2).to_broadcast([64, HEADS, P])))
                    dve.tensor_scalar(sel[32:64, :, :],
                                      ident[32:64, F_ROW:F_ROW + HEADS].unsqueeze(2).to_broadcast([32, HEADS, P]),
                                      -1.0 / SCALE, None, ALU.mult)
                    dve.wait_ge(tr.sem, t0 + 5)
                    dve.tensor_copy(gate_c_tok, ps[:, 4, 0:256].rearrange("p (j r) -> p j r", j=NT))
                    link(dve.tensor_copy(gate_u_tok, ps[:, 4, 256:512].rearrange("p (j r) -> p j r", j=NT)))
                    dve.tensor_scalar(neg_c, gate_c_tok[:, :, 0:HEADS], -1.0, None, ALU.mult)
                    for j in range(NT):
                        dve.wait_ge(act_a.sem, a0 + 3 + j)
                        dve.tensor_tensor(xdt[:, j, :].rearrange("p (h d) -> p h d", h=HEADS),
                                          xs_tok[:, j, :].rearrange("p (h d) -> p h d", h=HEADS),
                                          gate_u_tok[:, j, 0:HEADS].unsqueeze(2).to_broadcast([P, HEADS, HD]),
                                          ALU.mult)
                    for n in range(8):
                        g, i = n // 4, n % 4
                        dve.wait_ge(pe_a.sem, b0 + n + 1)
                        dve.tensor_copy(cb[:, g, CB_AT[i]:CB_AT[i] + T - i * P], ps[:, 5 + n % 3, 0:T - i * P])\
                           .then_inc(dve_b.sem, 1)

                @block.tensor
                def _(pe):
                    for j in range(NT):
                        for c in range(4):
                            ins = pe.transpose(ps[:, j, c * P:(c + 1) * P], xbc_a[:, c, j * P:(j + 1) * P], ident)
                        ins.then_inc(tr.sem, 1)
                    pe.wait_ge(dve_a.sem, d0 + 1)
                    for j in range(NT):
                        pe.transpose(ps[:, 4, j * 64:(j + 1) * 64], gate_c[:, j * P:(j + 1) * P], ident[0:64, 0:64])
                        ins = pe.transpose(ps[:, 4, 256 + j * 64:256 + (j + 1) * 64], gate_u[:, j * P:(j + 1) * P],
                                           ident[0:64, 0:64])
                    ins.then_inc(tr.sem, 1)
                    for n in range(8):
                        g, i = n // 4, n % 4
                        if n >= 3:
                            pe.wait_ge(dve_b.sem, e0 + n - 2)
                        pe.matmul(ps[:, 5 + n % 3, 0:T - i * P], xbc_a[:, 4 + g, i * P:(i + 1) * P],
                                  xbc_a[:, 6 + g, i * P:T], start=True, stop=True).then_inc(pe_a.sem, 1)

        def ssd_stage():
            eb = [view(xt_mem, 2 * TRI, TRI), view(arena, 4128 + 2048, TRI)]
            gnorm = rows[:, 2 * T:3 * T]
            l0 = loaded.take(16)
            m0, e0, g0 = pe_a.take(4 * HEADS), act_a.take(4 * HEADS + 2), dve_a.take(4 * HEADS)
            y0, d0 = pe_b.take(HEADS), dve_b.take(HEADS)
            k0 = dve_c.take(2)
            with nc.Block() as block:
                @block.gpsimd
                def _(pool):
                    pool.dma_start(gnorm, a["ssd_norm_g"][0].partition_broadcast(P)).then_inc(loaded.sem, 16)

                @block.tensor
                def _(pe):
                    def decays(h):
                        for i in range(NT):
                            n = 4 * h + i
                            if h >= 1:
                                pe.wait_ge(act_a.sem, e0 + n - 3)
                            w = T - i * P
                            d, row = sel[0:HEADS, h, :], gate_c[0:HEADS, :]
                            pe.matmul(ps[:, i, 0:P], ident, mask_sq, start=True, stop=False)
                            ins = pe.matmul(ps[:, i, 0:P], d, row[:, i * P:(i + 1) * P], start=False, stop=True)
                            if w > P:
                                ins = pe.matmul(ps[:, i, P:w], d, row[:, (i + 1) * P:T], start=True, stop=True)
                            ins.then_inc(pe_a.sem, 1)

                    decays(0)
                    for h in range(HEADS):
                        if h + 1 < HEADS:
                            decays(h + 1)
                        pe.wait_ge(dve_a.sem, g0 + 4 * h + 4)
                        if h >= 2:
                            pe.wait_ge(dve_b.sem, d0 + h - 1)
                        for j in range(NT):
                            for i in range(j + 1):
                                at = CB_AT[i] + (j - i) * P
                                ins = pe.matmul(ps[:, 4 + h % 2, j * HD:(j + 1) * HD], eb[h % 2][:, at:at + P],
                                                xdt[:, i, h * HD:(h + 1) * HD], start=(i == 0), stop=(i == j))
                        ins.then_inc(pe_b.sem, 1)

                @block.scalar
                def _(act):
                    for h in range(HEADS):
                        if h >= 2:
                            act.wait_ge(pe_b.sem, y0 + h - 1)
                        for i in range(NT):
                            w = T - i * P
                            act.wait_ge(pe_a.sem, m0 + 4 * h + i + 1)
                            act.activation(eb[h % 2][:, CB_AT[i]:CB_AT[i] + w], ps[:, i, 0:w], ACT.Exp,
                                           bias=neg_c[:, i, h:h + 1]).then_inc(act_a.sem, 1)
                    act.wait_ge(dve_c.sem, k0 + 1)
                    for j in range(NT):
                        for g in range(GROUPS):
                            ins = act.activation(xdt[:, j, g * 256:(g + 1) * 256], merged_s[:, j, g * 256:(g + 1) * 256],
                                                 ACT.Square, accum_out=sumsq[:, 2 * j + g:2 * j + g + 1])
                    ins.then_inc(act_a.sem, 1)
                    act.wait_ge(dve_c.sem, k0 + 2)
                    act.activation(sumsq[:, 16:24], sumsq[:, 8:16], ACT.Sqrt).then_inc(act_a.sem, 1)

                @block.vector
                def _(dve):
                    link = Chain(dve, dve_chain)

                    def take_y(h):
                        dve.wait_ge(pe_b.sem, y0 + h + 1)
                        dve.scalar_tensor_tensor(merged_s[:, :, h * HD:(h + 1) * HD], xs_tok[:, :, h * HD:(h + 1) * HD],
                                                 dskip[:, h:h + 1],
                                                 ps[:, 4 + h % 2, 0:4 * HD].rearrange("p (j d) -> p j d", j=NT),
                                                 ALU.mult, ALU.add).then_inc(dve_b.sem, 1)

                    for h in range(HEADS):
                        g = h // (HEADS // GROUPS)
                        for i in range(NT):
                            dve.wait_ge(act_a.sem, e0 + 4 * h + i + 1)
                            e = eb[h % 2][:, CB_AT[i]:CB_AT[i] + T - i * P]
                            dve.tensor_tensor(e, e, cb[:, g, CB_AT[i]:CB_AT[i] + T - i * P], ALU.mult)\
                               .then_inc(dve_a.sem, 1)
                        if h >= 1:
                            take_y(h - 1)
                    take_y(HEADS - 1)
                    dve.wait_ge(dve_b.sem, d0 + HEADS)
                    for j in range(NT):
                        ins = dve.tensor_tensor(merged_s[:, j, :], merged_s[:, j, :], z_s[:, j, :], ALU.mult)
                    ins.then_inc(dve_c.sem, 1)
                    dve.wait_ge(act_a.sem, e0 + 4 * HEADS + 1)
                    dve.tensor_scalar(sumsq[:, 8:16], sumsq[:, 0:8], 1.0 / 256, RMS_EPS, ALU.mult, ALU.add)\
                       .then_inc(dve_c.sem, 1)
                    dve.wait_ge(act_a.sem, e0 + 4 * HEADS + 2)
                    link(dve.reciprocal(sumsq[:, 24:32], sumsq[:, 16:24]))
                    dve.wait_ge(loaded.sem, l0 + 16)
                    for j in range(NT):
                        for g in range(GROUPS):
                            y = merged_s[:, j, g * 256:(g + 1) * 256]
                            dve.scalar_tensor_tensor(y, y, sumsq[:, 24 + 2 * j + g:25 + 2 * j + g],
                                                     gnorm[:, g * 256:(g + 1) * 256], ALU.mult, ALU.mult)

        def attention_stage(n_comp, q, k, v, dv_head, put, lam=None, forget=False):
            jobs = HEADS * NT
            prob = [[view(xt_mem, (2 * b + c) * T, T) for c in range(2)] for b in range(2)]
            turned = [view(xt_mem, (4 + b) * T, T) for b in range(2)]
            st = view(small, 696, 2, 8)
            m0, x0, e0, n0 = pe_a.take(jobs * n_comp), dve_a.take(jobs * n_comp), act_a.take(jobs * n_comp), dve_b.take(jobs)
            t0, c0, o0, d0 = tr.take(jobs), act_b.take(jobs), pe_b.take(jobs), dve_c.take(jobs)

            def width(n):
                return (n % NT + 1) * P

            def score(n, c):
                return ps[:, n_comp * (n % 2) + c, 0:width(n)]

            with nc.Block() as block:
                @block.tensor
                def _(pe):
                    def scores(n):
                        h, j = n // NT, n % NT
                        for c in range(n_comp):
                            if n >= 2:
                                pe.wait_ge(act_a.sem, e0 + n_comp * (n - 2) + c + 1)
                            qj = q(h, c)[:, j * P:(j + 1) * P]
                            for lo, hi in ((j * P, (j + 1) * P), (0, j * P))[0:1 + (j > 0)]:
                                part = score(n, c)[:, lo:hi]
                                if lo == j * P:
                                    pe.matmul(part, ident, mask_qk, start=True, stop=False)
                                if forget:
                                    pe.matmul(part, sel[F_ROW:F_ROW + HEADS, h, :], gate_c[F_ROW:F_ROW + HEADS, lo:hi],
                                              start=(lo != j * P), stop=False)
                                ins = pe.matmul(part, qj, k(h, c)[:, lo:hi], start=(lo != j * P and not forget), stop=True)
                            ins.then_inc(pe_a.sem, 1)

                    def turn(n):
                        pe.wait_ge(dve_b.sem, n0 + n + 1)
                        if n >= 2:
                            pe.wait_ge(act_b.sem, c0 + n - 1)
                        for i in range(n % NT + 1):
                            ins = pe.transpose(ps[:, 4 + n % 2, i * P:(i + 1) * P],
                                               prob[n % 2][0][:, i * P:(i + 1) * P], ident)
                        ins.then_inc(tr.sem, 1)

                    def product(n):
                        h = n // NT
                        pe.wait_ge(act_b.sem, c0 + n + 1)
                        if n >= 2:
                            pe.wait_ge(dve_c.sem, d0 + n - 1)
                        for i in range(n % NT + 1):
                            ins = pe.matmul(ps[:, 6 + n % 2, 0:dv_head], turned[n % 2][:, i * P:(i + 1) * P],
                                            v[:, i, h * dv_head:(h + 1) * dv_head],
                                            start=(i == 0), stop=(i == n % NT))
                        ins.then_inc(pe_b.sem, 1)

                    for s in range(jobs + 3):
                        if s < jobs:
                            scores(s)
                        if 0 <= s - 2 < jobs:
                            turn(s - 2)
                        if 0 <= s - 3 < jobs:
                            product(s - 3)

                @block.scalar
                def _(act):
                    for s in range(jobs + 2):
                        if s < jobs:
                            for c in range(n_comp):
                                act.wait_ge(dve_a.sem, x0 + n_comp * s + c + 1)
                                if s >= 2:
                                    act.wait_ge(tr.sem, t0 + s - 1)
                                act.activation(prob[s % 2][c][:, 0:width(s)], score(s, c), ACT.Exp,
                                               bias=st[:, s % 2, 2 + c:3 + c], scale=SCALE,
                                               accum_out=st[:, s % 2, 4 + c:5 + c]).then_inc(act_a.sem, 1)
                        n = s - 2
                        if 0 <= n:
                            act.wait_ge(tr.sem, t0 + n + 1)
                            if n >= 2:
                                act.wait_ge(pe_b.sem, o0 + n - 1)
                            act.activation(turned[n % 2][:, 0:width(n)], ps[:, 4 + n % 2, 0:width(n)], ACT.Copy)\
                               .then_inc(act_b.sem, 1)

                @block.vector
                def _(dve):
                    link = Chain(dve, dve_chain)

                    def maxima(n):
                        for c in range(n_comp):
                            dve.wait_ge(pe_a.sem, m0 + n_comp * n + c + 1)
                            link(dve.tensor_reduce(st[:, n % 2, c:c + 1], score(n, c), AX, ALU.max))
                            dve.tensor_scalar(st[:, n % 2, 2 + c:3 + c], st[:, n % 2, c:c + 1], -SCALE, None, ALU.mult)\
                               .then_inc(dve_a.sem, 1)

                    def divide(n):
                        p, r = prob[n % 2], st[:, n % 2, 6:8]
                        dve.wait_ge(act_a.sem, e0 + n_comp * (n + 1))
                        link(dve.reciprocal(r[:, 0:n_comp], st[:, n % 2, 4:4 + n_comp]))
                        p0 = p[0][:, 0:width(n)]
                        if n_comp == 1:
                            dve.tensor_scalar(p0, p0, r[:, 0:1], None, ALU.mult).then_inc(dve_b.sem, 1)
                        else:
                            p1 = p[1][:, 0:width(n)]
                            link(dve.tensor_scalar(p1, p1, r[:, 1:2], lam, ALU.mult, ALU.mult))
                            dve.scalar_tensor_tensor(p0, p0, r[:, 0:1], p1, ALU.mult, ALU.subtract).then_inc(dve_b.sem, 1)

                    for s in range(jobs + 4):
                        if s < jobs:
                            maxima(s)
                        if 0 <= s - 1 < jobs:
                            divide(s - 1)
                        n = s - 4
                        if 0 <= n:
                            dve.wait_ge(pe_b.sem, o0 + n + 1)
                            dve.tensor_copy(put(n // NT, n % NT), ps[:, 6 + n % 2, 0:dv_head]).then_inc(dve_c.sem, 1)

        def moe_stage(l, alpha, g_src, b_src, last):
            E, EPG = n_experts[l], n_experts[l] // 4
            G = 4
            NR = G + E
            MAXB = 2 * T // BLK + E
            wr = view(arena, 0, NK, NR)
            brow = arena[0:1, 300:300 + NR]
            at = [400]

            def take(*shape, dt=F32):
                v = view(arena, at[0], *shape)
                at[0] += int(np.prod(shape))
                return v.bitcast(dt) if dt != F32 else v

            logits, expo, pen = take(NT, NR), take(NT, G), take(NT, G)
            gmax, gsum, m1, m2 = take(NT), take(NT), take(NT), take(NT)
            iota_g, iota_e = take(G), take(E)
            first, pick_g = take(NT), take(NT, G)
            es, es2 = take(NT, E), take(NT, E)
            pick1, pick2, pick = take(NT, E), take(NT, E), take(NT, E)
            w1, w2, ratio = take(NT), take(NT), take(NT)
            count_i, count_s = take(E, dt=I32), take(E, dt=I32)
            nblk, ends, starts = take(E), take(E), take(E)
            table = take(E + 3, dt=I32)
            pos = take(NT, E)
            slots = take(2, NT)
            slots_i = take(2, NT, dt=U32)
            slots_now = take(2, NT)
            hit1, hit2, hit = take(NT, BLK), take(NT, BLK), take(NT, BLK)
            x_rows, xg = take(2, P), take(NK, BLK)
            silu_g, hidden, hT = take(P), take(P), take(P)
            y_sb = take(2, D // 4)
            total_i = take(2, dt=I32)
            third = at[0]
            y1, y2 = take(NT, D), take(NT, D)
            assert at[0] <= 16448

            def bc(v, n):
                return v.unsqueeze(2).to_broadcast([P, v.shape[1], n])

            def mid(v, n):
                return v.unsqueeze(1).to_broadcast([P, n, v.shape[1]])

            l0, m0, d0, a0 = loaded.total, mm.take(2), dve_a.take(3), act_a.take(2)
            p0 = pool_chain.take(0)
            router = ((a["router_group_w"][0], a["router_group_b"][0], None, a["router_expert_b"][0]),
                      (a["moe_rg_w_2"][0], a["moe_rg_b_2"][0], a["moe_re_w_2"][0], a["moe_re_b_2"][0]),
                      (a["moe_rg_w_2"][1], a["moe_rg_b_2"][1], a["moe_re_w_2"][1], a["moe_re_b_2"][1]))[l]
            n_w = 5 if l == 0 else 2
            loaded.total = l0 + 16 * (n_w + 2)
            ready = consts.take(1)
            with nc.Block() as block:
                @block.gpsimd
                def _(pool):
                    def load(dst, src):
                        pool.dma_start(dst, src).then_inc(loaded.sem, 16)

                    with nc.allow_non_contiguous_dma("router columns"):
                        load(wr[:, :, 0:G], router[0].rearrange("(k p) g -> p k g", p=P))
                        if l == 0:
                            for g in range(G):
                                load(wr[:, :, G + g * EPG:G + (g + 1) * EPG],
                                     a["router_expert_w"][0][g].rearrange("(k p) e -> p k e", p=P))
                        else:
                            load(wr[:, :, G:NR], router[2].rearrange("(k p) e -> p k e", p=P))
                        load(brow[:, 0:G], router[1].unsqueeze(0))
                        load(brow[:, G:NR], (router[3].rearrange("g e -> (g e)") if l == 0 else router[3]).unsqueeze(0))
                    pool.iota(iota_g, pattern=[[1, G]], base=0, channel_multiplier=0, allow_small_or_imprecise_dtypes=True)
                    pool.iota(iota_e, pattern=[[1, E]], base=0, channel_multiplier=0, allow_small_or_imprecise_dtypes=True)
                    pool.memset(table, 0).then_inc(consts.sem, 1)

                @block.tensor
                def _(pe):
                    pe.wait_ge(loaded.sem, l0 + 16 * (n_w + 2))
                    for j in range(NT):
                        pe.matmul(ps[:, j, 0:NR], ones[0:1, :], brow, start=True, stop=False)
                        for k in range(NK):
                            ins = pe.matmul(ps[:, j, 0:NR], xT[:, k, j * P:(j + 1) * P], wr[:, k, :],
                                            start=False, stop=(k == NK - 1))
                    ins.then_inc(mm.sem, 1)
                    pe.wait_ge(dve_a.sem, d0 + 3)
                    for j in range(NT):
                        for i in range(j + 1):
                            pe.matmul(ps[:, 4, j * E:(j + 1) * E], before if i == j else ones, pick[:, i, :],
                                      start=(i == 0), stop=(i == j))
                    for i in range(NT):
                        ins = pe.matmul(ps[:, 5, 0:E], ones, pick[:, i, :], start=(i == 0), stop=(i == NT - 1))
                    ins.then_inc(mm.sem, 1)

                @block.scalar
                def _(act):
                    act.wait_ge(dve_a.sem, d0 + 1)
                    act.activation(expo, expo, ACT.Exp).then_inc(act_a.sem, 1)
                    act.wait_ge(dve_a.sem, d0 + 2)
                    act.activation(ratio, ratio, ACT.Exp).then_inc(act_a.sem, 1)

                @block.vector
                def _(dve):
                    link = Chain(dve, dve_chain)

                    def pick_max(dst, tmp, x, m, iota, n):
                        link(dve.tensor_reduce(m, x, AX, ALU.max))
                        link(dve.tensor_tensor(tmp, x, bc(m, n), ALU.is_equal))
                        link(dve.scalar_tensor_tensor(tmp, tmp, -1000.0, mid(iota, NT), ALU.mult, ALU.add))
                        link(dve.tensor_reduce(first, tmp, AX, ALU.min))
                        link(dve.tensor_tensor(dst, tmp, bc(first, n), ALU.is_equal))

                    dve.wait_ge(consts.sem, ready + 1)
                    dve.wait_ge(mm.sem, m0 + 1)
                    link(dve.tensor_copy(logits, ps[:, 0:NT, 0:NR]))
                    gl, el = logits[:, :, 0:G], logits[:, :, G:NR]
                    pick_max(pick_g, pen, gl, gmax, iota_g, G)
                    dve.tensor_tensor(expo, gl, bc(gmax, G), ALU.subtract).then_inc(dve_a.sem, 1)
                    link(dve.tensor_scalar(pen, pick_g, -NEG, NEG, ALU.mult, ALU.add))
                    link(dve.tensor_tensor(es.rearrange("p j (g e) -> p j g e", g=G),
                                           el.rearrange("p j (g e) -> p j g e", g=G),
                                           pen.unsqueeze(3).to_broadcast([P, NT, G, EPG]), ALU.add))
                    pick_max(pick1, es2, es, m1, iota_e, E)
                    link(dve.scalar_tensor_tensor(es, pick1, 2 * NEG, es, ALU.mult, ALU.add))
                    pick_max(pick2, es2, es, m2, iota_e, E)
                    dve.tensor_tensor(ratio, m2, m1, ALU.subtract).then_inc(dve_a.sem, 1)
                    dve.tensor_tensor(pick, pick1, pick2, ALU.add).then_inc(dve_a.sem, 1)
                    dve.wait_ge(act_a.sem, a0 + 2)
                    link(dve.tensor_reduce(gsum, expo, AX, ALU.add))
                    link(dve.tensor_scalar(w2, ratio, 1.0, None, ALU.add))
                    link(dve.tensor_tensor(w1, gsum, w2, ALU.mult))
                    link(dve.reciprocal(w1, w1))
                    dve.tensor_tensor(w2, w1, ratio, ALU.mult)
                    dve.wait_ge(mm.sem, m0 + 2)
                    link(dve.tensor_scalar(count_i, ps[:, 5, 0:E], float(BLK - 1), None, ALU.add))
                    link(dve.tensor_scalar(count_s, count_i, BLK.bit_length() - 1, None, ALU.arith_shift_right))
                    link(dve.tensor_scalar(nblk, count_s, 1.0, None, ALU.max))
                    link(dve.tensor_tensor_scan(ends, ones[:, 0:E], nblk, 0.0, ALU.mult, ALU.add))
                    link(dve.tensor_tensor(starts, ends, nblk, ALU.subtract))
                    link(dve.tensor_scalar(total_i[:, 0:1], ends[:, E - 1:E], 1.0, None, ALU.add))
                    link(dve.tensor_scalar(total_i[:, 1:2], total_i[:, 0:1], 1, None, ALU.arith_shift_right))
                    link(dve.tensor_copy(table[:, 1:E], ends[:, 0:E - 1]))
                    for n in (E, E + 1):
                        dve.tensor_scalar(table[:, n:n + 1], total_i[:, 1:2], 2.0, None, ALU.mult)
                    dve.tensor_copy(table[:, E + 2:E + 3], total_i[:, 1:2])
                    link(dve.scalar_tensor_tensor(pos, mid(starts, NT), float(BLK),
                                                  ps[:, 4, 0:NT * E].rearrange("p (j e) -> p j e", j=NT),
                                                  ALU.mult, ALU.add))
                    for n, pk in enumerate((pick1, pick2)):
                        link(dve.tensor_tensor(es, pos, pk, ALU.mult))
                        link(dve.tensor_reduce(slots[:, n, :], es, AX, ALU.add))
                    dve.tensor_copy(slots_i, slots)
                    dve.tensor_copy(slots_now, slots)
                    dve.memset(y_sb, 0.0)

            s_hit, s_got, s_rows, s_turned, s_xg, s_gu, s_silu, s_h, s_hturned, s_hT, s_down, s_y, s_even, s_odd, s_slots = (
                signal(f"{n}{l}").sem for n in (
                    "selection_ready", "gathered", "rows_taken", "inputs_turned", "inputs_ready", "gate_up_done", "silu_ready",
                    "hidden_ready", "hidden_turned", "hidden_taken", "down_done", "rows_ready", "even_rows_stored", "odd_rows_stored", "slots_moved"))
            s_stored = (s_even, s_odd)
            c0 = moe_at[l]
            quarters = [slice(q * BLK, (q + 1) * BLK) for q in range(4)]
            W = D // 4
            third_at = [arena[:, third:third + NK * CH], arena[:, third + NK * CH:third + 2 * NK * CH], xt_mem[:, :]]

            def value(eng, n, low=1, high=MAXB):
                return eng.value_load(table[0:1, n], min_val=low, max_val=high)

            def rows_at(g):
                return ybuf[bass.ds(g * BLK, BLK), :].rearrange("r (q n) -> q r n", q=4)

            with nc.Block() as block:
                @block.sync
                def _(sp):
                    def load_third(e):
                        for kind in range(3):
                            src = expert_src(l, e, kind)
                            sp.dma_start(third_at[kind].rearrange("p (k n) -> p k n", k=src.shape[1]), src)\
                              .then_inc(arrived_x[kind].sem, 16)

                    def follow(i, q):
                        sp.wait_ge(s_down, value(sp, bass.ds(3 * i + q + 1, 1)))
                        if q == 2:
                            load_third(3 * i + q + 3)
                        else:
                            for j in range(3):
                                load_expert_chunk(sp, l, 3 * i + q + 3, j, c0 + 3 * q + j)

                    load_third(2)
                    with sp.Fori(0, (E - 3) // 3) as i:
                        for q in range(3):
                            follow(i, q)
                    for q in range((E - 3) % 3):
                        follow((E - 3) // 3, q)
                    if l < 2:
                        for n in range(mixer_at[l + 1], mixer_at[l + 1] + SLOTS):
                            k = (n - SLOTS - c0) // 3
                            e = 3 * (k // 2) + k % 2
                            sp.wait_ge(s_down, value(sp, slice(e + 1, e + 2)))
                            load_chunk(sp, n)

                @block.tensor
                def _(pe):
                    def gather():
                        for j in range(NT):
                            for q, at in enumerate(quarters):
                                ins = pe.matmul(ps[at, 0, 0:W], hit[:, j, :],
                                                x_tok[:, j, :].rearrange("p (h q c) -> p h q c", h=2, q=4)[:, :, q, :],
                                                start=(j == 0), stop=(j == NT - 1))
                        ins.then_inc(s_got, 1)

                    def turn_inputs():
                        for h in range(2):
                            ins = pe.transpose(ps[:, 1, h * P:(h + 1) * P], x_rows[:, h, :], ident)
                        ins.then_inc(s_turned, 1)

                    pe.wait_ge(s_hit, 1)
                    gather()
                    pe.wait_ge(s_rows, 1)
                    turn_inputs()
                    def expert(i, q):
                        if q < 2:
                            first_chunk = c0 + 3 * q
                            sg, sd = (first_chunk + kinds(first_chunk).index(kind) for kind in (0, 2))
                            gu_mem = ring[:, sg % SLOTS * NK * CH:(sg % SLOTS + 2) * NK * CH]
                            d_mem = slot(sd % SLOTS)
                            there = [(arrived[n % SLOTS].sem, i * 16 + 16 * (n // SLOTS + 1))
                                     for n in range(first_chunk, first_chunk + 3)]
                        else:
                            gu_mem, d_mem = arena[:, third:third + 2 * NK * CH], third_at[2]
                            there = [(x.sem, i * 16 + 16 * (x.total // 16 + 1)) for x in arrived_x]
                        w_gu = gu_mem.rearrange("p (w k n) -> p w k n", w=2, k=NK)
                        wd = d_mem.rearrange("p (k n) -> p k n", k=NT)
                        start, end = value(pe, bass.ds(3 * i + q, 1), 0), value(pe, bass.ds(3 * i + q + 1, 1))
                        with pe.Fori(start, end) as g:
                            for chunk in there:
                                pe.wait_ge(*chunk)
                            pe.wait_ge(s_xg, g + 1)
                            for k in range(NK):
                                for q, at in enumerate(quarters):
                                    ins = pe.matmul(ps[at, 2, 0:W], xg[:, k, :], w_gu[:, :, k, q * P:(q + 1) * P],
                                                    start=(k == 0), stop=(k == NK - 1))
                            ins.then_inc(s_gu, 1)
                            pe.wait_ge(s_hit, g + 2)
                            gather()
                            pe.wait_ge(s_h, g + 1)
                            pe.transpose(ps[:, 3, 0:P], hidden, ident).then_inc(s_hturned, 1)
                            pe.wait_ge(s_rows, g + 2)
                            turn_inputs()
                            pe.wait_ge(s_hT, g + 1)
                            pe.wait_ge(s_y, g + 1)
                            for f in range(NT):
                                for q, at in enumerate(quarters):
                                    ins = pe.matmul(ps[at, 4, 0:W], hT[:, f * BLK:(f + 1) * BLK], wd[:, f, q * W:(q + 1) * W],
                                                    start=(f == 0), stop=(f == NT - 1))
                            ins.then_inc(s_down, 1)

                    with pe.Fori(0, E // 3) as i:
                        for q in range(3):
                            expert(i, q)
                    for q in range(E % 3):
                        expert(E // 3, q)

                @block.scalar
                def _(act):
                    def take_rows():
                        act.activation(x_rows, ps[:, 0, 0:W].rearrange("p (h c) -> p h c", h=2), ACT.Copy).then_inc(s_rows, 1)

                    for b in range(2):
                        act.dma_start(rows_at(b), y_sb[:, b, :]).then_inc(s_stored[b], 16)
                    pairs = value(act, slice(E + 2, E + 3), high=MAXB // 2)
                    act.wait_ge(s_got, 1)
                    take_rows()
                    with act.Fori(0, pairs) as p:
                        for b in range(2):
                            g = 2 * p + b
                            act.wait_ge(s_gu, g + 1)
                            act.activation(silu_g, ps[:, 2, 0:P], ACT.Silu).then_inc(s_silu, 1)
                            act.wait_ge(s_got, g + 2)
                            take_rows()
                            act.wait_ge(s_y, g + 2)
                            act.dma_start(rows_at(g), y_sb[:, b, :]).then_inc(s_stored[b], 16)
                    for b in range(2):
                        act.wait_ge(s_stored[b], pairs * 16 + 16)
                    act.activation(mean_var[:, 4:5], eps_ln, ACT.Copy)

                @block.vector
                def _(dve):
                    def select(g):
                        dve.tensor_tensor(hit1, mid(iota_f, NT), bc(slots_now[:, 0, :], BLK), ALU.is_equal)
                        dve.tensor_tensor(hit2, mid(iota_f, NT), bc(slots_now[:, 1, :], BLK), ALU.is_equal).then_inc(s_slots, 1)
                        dve.wait_ge(s_slots, g * 2 + 1)
                        dve.tensor_tensor(hit, hit1, hit2, ALU.add).then_inc(s_hit, 1)
                        dve.tensor_scalar(slots_now, slots_now, float(BLK), None, ALU.subtract).then_inc(s_slots, 1)
                        dve.wait_ge(s_slots, g * 2 + 2)

                    def take_inputs():
                        dve.tensor_copy(xg.rearrange("p k s -> p (k s)"), ps[:, 1, 0:W]).then_inc(s_xg, 1)

                    pairs = value(dve, slice(E + 2, E + 3), high=MAXB // 2)
                    dve.memset(mean_var[:, 5:6], 0.0).then_inc(s_y, 1)
                    select(0)
                    dve.wait_ge(s_turned, 1)
                    take_inputs()
                    with dve.Fori(0, pairs) as p:
                        for b in range(2):
                            g = 2 * p + b
                            dve.wait_ge(s_got, g + 1)
                            select(g + 1)
                            dve.wait_ge(s_silu, g + 1)
                            dve.tensor_tensor(hidden, silu_g, ps[:, 2, P:2 * P], ALU.mult).then_inc(s_h, 1)
                            dve.wait_ge(s_hturned, g + 1)
                            dve.tensor_copy(hT, ps[:, 3, 0:P]).then_inc(s_hT, 1)
                            dve.wait_ge(s_turned, g + 2)
                            take_inputs()
                            dve.wait_ge(s_down, g + 1)
                            dve.wait_ge(s_stored[b], p * 16 + 16)
                            dve.tensor_copy(y_sb[:, b, :], ps[:, 4, 0:W]).then_inc(s_y, 1)
            for x in arrived_x:
                x.take(16 * (E // 3))

            r0, s0, q0, l1 = loaded.take(16 * 8), stat.take(NT), sq.take(NT), loaded.take(32)
            with nc.Block() as block:
                @block.gpsimd
                def _(pool):
                    for j in range(NT):
                        for n, y in enumerate((y1, y2)):
                            pool.indirect_dma_start(out=y[:, j, :], out_offset=None, in_=ybuf,
                                                    in_offset=bass.IndirectOffsetOnAxis(ap=slots_i[:, n, j:j + 1], axis=0))\
                                .then_inc(loaded.sem, 16)
                    load_norm_rows(pool, g_src, b_src)

                @block.scalar
                def _(act):
                    deviations(act, s0)

                @block.vector
                def _(dve):
                    link = Chain(dve, dve_chain)
                    dve.wait_ge(loaded.sem, l1 + 32)
                    for j in range(NT):
                        xj = x_tok[:, j, :]
                        link(dve.tensor_scalar(xj, xj, alpha, None, ALU.mult))
                        link(dve.scalar_tensor_tensor(xj, y1[:, j, :], w1[:, j:j + 1], xj, ALU.mult, ALU.add))
                        link(dve.scalar_tensor_tensor(xj, y2[:, j, :], w2[:, j:j + 1], xj, ALU.mult, ALU.add))
                        normalise(dve, link, j, q0)
            if not last:
                transpose_stage(lambda j, k: x_tok[:, j, k * P:(k + 1) * P], xT)

        q2 = view(arena, 0, DA_HEADS, T)
        k2 = view(arena, NK * T, DA_HEADS, T)
        v2 = view(arena, 2 * NK * T, NT, D)
        o2 = view(arena, 3 * NK * T, NT, D)
        lam = cols[:, 8:9]
        lam_rows = rows[:, 0:256].rearrange("p (n d) -> p n d", n=4)
        subln = rows[:, 256:256 + P]

        def qkv_stage():
            first = mixer_at[1]
            m0, e0, l0 = mm.take(24), ev.take(24), loaded.take(32)
            for c in range(6):
                used[first + c] = (mm.sem, m0 + 4 * (c + 1))
            prods = view(rows, 512, 2, HD)
            sums = cols[:, 16:18]
            x0, a0 = dve_a.take(1), act_a.take(1)
            with nc.Block() as block:
                @block.sync
                def _(sp):
                    stream_mixer(sp, first + SLOTS, first + 12)

                @block.gpsimd
                def _(pool):
                    pool.dma_start(lam_rows, a["attn_lambda_2"][0].partition_broadcast(P)).then_inc(loaded.sem, 16)
                    pool.dma_start(subln, a["attn_subln_g_2"][0].partition_broadcast(P)).then_inc(loaded.sem, 16)

                @block.tensor
                def _(pe):
                    for n in range(24):
                        c, j = n // 4, n % 4
                        if n >= 8:
                            pe.wait_ge(ev.sem, e0 + n - 7)
                        if j == 0:
                            wait_chunk(pe, first + c)
                        w = slot((first + c) % SLOTS).rearrange("p (k n) -> p k n", k=NK)
                        for k in range(NK):
                            wj, xj = w[:, k, :], xT[:, k, :]
                            if c < 4:
                                wj = w[:, k, j * P:(j + 1) * P]
                            else:
                                xj = xT[:, k, j * P:(j + 1) * P]
                            lhs, rhs = (wj, xj) if c < 4 else (xj, wj)
                            ins = pe.matmul(ps[:, n % 8, :], lhs, rhs, start=(k == 0), stop=(k == NK - 1))
                        ins.then_inc(mm.sem, 1)

                @block.scalar
                def _(act):
                    act.wait_ge(dve_a.sem, x0 + 1)
                    act.activation(sums, sums, ACT.Exp).then_inc(act_a.sem, 1)
                    for n in range(24):
                        c, j = n // 4, n % 4
                        act.wait_ge(mm.sem, m0 + n + 1)
                        dst = (q2, k2)[c // 2][:, 4 * (c % 2) + j, :] if c < 4 else v2[:, j, (c - 4) * CH:(c - 3) * CH]
                        act.activation(dst, ps[:, n % 8, :], ACT.Copy).then_inc(ev.sem, 1)

                @block.vector
                def _(dve):
                    link = Chain(dve, dve_chain)
                    dve.wait_ge(loaded.sem, l0 + 32)
                    link(dve.tensor_tensor(prods, lam_rows[:, 0:4:2, :], lam_rows[:, 1:4:2, :], ALU.mult))
                    dve.tensor_reduce(sums, prods, AX, ALU.add).then_inc(dve_a.sem, 1)
                    dve.wait_ge(act_a.sem, a0 + 1)
                    link(dve.tensor_tensor(lam, sums[:, 0:1], sums[:, 1:2], ALU.subtract))
                    dve.tensor_scalar(lam, lam, LAMBDA_INIT, None, ALU.add)

        def subln_stage():
            squares = view(xt_mem, 0, NT, D)
            ms = cols[:, 16:48]
            x0, a0 = dve_a.take(1), act_a.take(1)
            heads = "p j (h d) -> p (j h) d"
            with nc.Block() as block:
                @block.scalar
                def _(act):
                    act.wait_ge(dve_a.sem, x0 + 1)
                    act.activation(ms, ms, ACT.Sqrt).then_inc(act_a.sem, 1)

                @block.vector
                def _(dve):
                    link = Chain(dve, dve_chain)
                    o = o2.rearrange(heads, h=DA_HEADS)
                    link(dve.tensor_tensor(squares, o2, o2, ALU.mult))
                    link(dve.tensor_reduce(ms, squares.rearrange(heads, h=DA_HEADS), AX, ALU.add))
                    dve.tensor_scalar(ms, ms, 1.0 / P, RMS_EPS, ALU.mult, ALU.add).then_inc(dve_a.sem, 1)
                    link(dve.tensor_scalar(subln, subln, 1.0 - LAMBDA_INIT, None, ALU.mult))
                    dve.wait_ge(act_a.sem, a0 + 1)
                    link(dve.reciprocal(ms, ms))
                    link(dve.tensor_tensor(o, o, ms.unsqueeze(2).to_broadcast([P, 32, P]), ALU.mult))
                    dve.tensor_tensor(o, o, subln.unsqueeze(1).to_broadcast([P, 32, P]), ALU.mult)

        rT = view(arena, 0, NK, T)
        k3 = view(arena, NK * T, NK, T)
        v3 = view(arena, 2 * NK * T, NT, D)
        w2a2 = rows[:, 0:D]
        h_wa = rows[:, D:D + T]
        h_g = rows[:, D + T:D + 2 * T]
        h_g2 = small[0:GATE_LORA - P, 40:40 + T]
        N_PAR = 5
        K_K, K_A, R_K, W0, A0 = range(N_PAR)
        par = view(small, 552, N_PAR, NK)
        same_head = small[:, 592:720]

        def rkv_stage():
            first = mixer_at[2]
            mixes = {"w": 3, "a": 4, "g": 5, "r": 0, "k": 1, "v": 2}
            xx = view(arena, 3 * NK * T, NK, T)
            buf = {"w": view(arena, 2 * NK * T, NK, T), "a": k3}
            buf.update(g=buf["w"], r=buf["a"], k=buf["w"], v=xx)
            w1 = view(arena, 0, NK, DECAY_LORA)
            a1 = view(arena, 512, NK, AAA_LORA)
            g1 = view(arena, 1024, NK, GATE_LORA)
            mu = view(arena, 4 * NK * T, 6, NK)
            jobs = ["w", "a", "g", "g2"] + [(n, c, j) for n in "rkv" for c in range(2) for j in range(4)]
            m0, e0, l0 = mm.take(28), ev.take(28), loaded.take(16 * 16)
            x0, c0 = dve_a.take(6), consts.take(1)
            for c in range(6):
                used[first + c] = (mm.sem, m0 + 4 + 4 * (c + 1))
            with nc.Block() as block:
                @block.sync
                def _(sp):
                    stream_mixer(sp, first + SLOTS, first + 8)

                @block.gpsimd
                def _(pool):
                    def load(dst, src):
                        pool.dma_start(dst, src).then_inc(loaded.sem, 16)

                    with nc.allow_non_contiguous_dma("parameter columns"):
                        for n in range(6):
                            load(mu[:, n, :], a["rw_mu_2"][0][n].rearrange("(k p) -> p k", p=P))
                        load(w1, a["rw_w1_2"][0].rearrange("(k p) n -> p k n", p=P))
                        load(a1, a["rw_a1_2"][0].rearrange("(k p) n -> p k n", p=P))
                        load(g1, a["rw_g1_2"][0].rearrange("(k p) n -> p k n", p=P))
                        load(w2a2[0:64, :], a["rw_w2_2"][0])
                        load(w2a2[64:128, :], a["rw_a2_2"][0])
                        for n, src in ((K_K, "rw_k_k_2"), (K_A, "rw_k_a_2"), (W0, "rw_w0_2"), (A0, "rw_a0_2")):
                            load(par[:, n, :], a[src][0].rearrange("(k p) -> p k", p=P))
                        load(par[:, R_K, :], a["rw_r_k_2"][0].rearrange("h n -> (h n)").rearrange("(k p) -> p k", p=P))
                    link = Chain(pool, pool_chain)
                    link(pool.memset(same_head, 0.0))
                    pool.memset(same_head[0:HD, 0:HD], 1.0)
                    pool.memset(same_head[HD:P, HD:P], 1.0).then_inc(consts.sem, 1)

                @block.vector
                def _(dve):
                    link = Chain(dve, dve_chain)
                    dve.tensor_tensor(xx[:, :, 1:T], xT[:, :, 0:T - 1], xT[:, :, 1:T], ALU.subtract)
                    link(dve.tensor_scalar(xx[:, :, 0:1], xT[:, :, 0:1], -1.0, None, ALU.mult))
                    dve.wait_ge(loaded.sem, l0 + 16 * 16)
                    for n, name in enumerate(mixes):
                        if name in "grk":
                            dve.wait_ge(mm.sem, m0 + {"g": 1, "r": 2, "k": 4}[name])
                        for k in range(NK):
                            ins = dve.scalar_tensor_tensor(buf[name][:, k, :], xx[:, k, :], mu[:, mixes[name], k:k + 1],
                                                           xT[:, k, :], ALU.mult, ALU.add)
                        ins.then_inc(dve_a.sem, 1)

                @block.tensor
                def _(pe):
                    pe.wait_ge(loaded.sem, l0 + 16 * 16)
                    order = list(mixes)
                    for n, job in enumerate(jobs):
                        if n >= 8:
                            pe.wait_ge(ev.sem, e0 + n - 7)
                        bank = ps[:, n % 8, :]
                        name = job[0]
                        pe.wait_ge(dve_a.sem, x0 + order.index(name) + 1)
                        xm = buf[name]
                        if n < 4:
                            w, o = ((w1, bank[0:64, :]), (a1, bank[64:128, :]),
                                    (g1[:, :, 0:P], bank), (g1[:, :, P:GATE_LORA], bank[0:GATE_LORA - P, :]))[n]
                            for k in range(NK):
                                ins = pe.matmul(o, w[:, k, :], xm[:, k, :], start=(k == 0), stop=(k == NK - 1))
                        else:
                            _, c, j = job
                            ch = first + 2 * "rkv".index(name) + c
                            if j == 0:
                                wait_chunk(pe, ch)
                            w = slot(ch % SLOTS).rearrange("p (k n) -> p k n", k=NK)
                            for k in range(NK):
                                if name == "v":
                                    ins = pe.matmul(bank, xm[:, k, j * P:(j + 1) * P], w[:, k, :],
                                                    start=(k == 0), stop=(k == NK - 1))
                                else:
                                    ins = pe.matmul(bank, w[:, k, j * P:(j + 1) * P], xm[:, k, :],
                                                    start=(k == 0), stop=(k == NK - 1))
                        ins.then_inc(mm.sem, 1)

                @block.scalar
                def _(act):
                    for n, job in enumerate(jobs):
                        act.wait_ge(mm.sem, m0 + n + 1)
                        bank = ps[:, n % 8, :]
                        if n < 4:
                            dst, src, f = ((h_wa[0:64, :], bank[0:64, :], ACT.Tanh), (h_wa[64:128, :], bank[64:128, :], ACT.Copy),
                                           (h_g, bank, ACT.Sigmoid), (h_g2, bank[0:GATE_LORA - P, :], ACT.Sigmoid))[n]
                        else:
                            name, c, j = job
                            src, f = bank, ACT.Copy
                            dst = v3[:, j, c * CH:(c + 1) * CH] if name == "v" else (rT if name == "r" else k3)[:, 4 * c + j, :]
                        act.activation(dst, src, f).then_inc(ev.sem, 1)

        def wkv_stage():
            first = mixer_at[2]
            mem = [slot((first + 2 + n) % SLOTS) for n in range(4)]
            logd, lr, cum, before_d, inv, decay, kk, norm = (view(mem[0], n * T, T) for n in range(8))
            XX = view(mem[1], 0, 8, 2 * P)
            TT = view(mem[1], 16 * P, 8, P)
            QC = view(mem[1], 24 * P, 8, P)
            Z = view(mem[2], 0, 8, P)
            MT = view(mem[2], 8 * P, NC_R, P)
            NN = view(mem[2], 16 * P, NC_R, HD)
            S = view(mem[2], 20 * P, NC_R, HD)
            Y0 = view(mem[2], 24 * P, NT, 2, HD)
            AKM = view(mem[3], 0, 8, 4 * P)
            spare = 3 * NK * T
            keep, rkr, RQ = (view(arena, spare + n * T, T) for n in range(3))
            RH = view(arena, spare + 3 * T, 8, P)
            lora2 = view(arena, spare + 5 * T, 2, P)
            tile4 = "p (j t) -> p j t"
            AR = view(xt_mem, 0, NT, 2, P)
            A_T, R_T = AR[:, :, 0, :], AR[:, :, 1, :]
            B_T, K_T = view(xt_mem, 2 * T, T), view(xt_mem, 3 * T, T)
            B_tok, K_tok, V = (view(xt_mem, n * T, NT, P) for n in (4, 5, 6))
            low_st_d = mask_sq
            masks = cst[:, 6 * P:8 * P]
            pcol = cols[:, 16:16 + N_PAR]
            p_end = cols[:, 24:24 + NC_R]
            heads = view(cols, 33, NT, 2)
            strip = slice(3 * P, 4 * P)
            units = [(e, j) for e in range(2) for j in range(NT)]
            ROUNDS = RB.bit_length() - 2
            assert RC == 2 * RB
            names = ("lora2", "first_lora", "lora", "par", "sig", "sq", "shift", "first_sums", "ssq", "exp", "inverse", "first_wide", "ops", "turned", "tok", "val", "low", "lowm",
                     "q", "qc", "qc2", "z", "zc", "zc2", "q2", "q2c", "r2", "r2c", "y0", "y0c", "mn", "mnc", "yy", "yc")
            E = {n: signal(f"wkv_{n}").sem for n in names}
            p_akm, d_low, d_akm, p_sq, a_sq, p_tt, d_tt = (signal(f"wkv_{n}").sem for n in (
                "products", "low_masked", "masked", "squared", "squares_taken", "t_products", "t_added"))
            p_s, d_s = signal("wkv_state_product").sem, signal("wkv_state").sem
            chain_v = signal("wkv_dve_chain").sem
            PREPARE_LINKS, TURN_LINKS = 11, 13

            class LoopChain:

                def __init__(self, eng, sem, base, turn, n):
                    self.eng, self.sem, self.base, self.turn, self.n, self.at = eng, sem, base, turn, n, 0

                def __call__(self, ins):
                    self.at += 1
                    ins.then_inc(self.sem, 1)
                    self.eng.wait_ge(self.sem, self.turn * self.n + self.base + self.at)

            def rows_of(e):
                return slice(e * HD, (e + 1) * HD)

            def tile_of(mem3, n):
                return mem3[:, bass.ds(n, 1), :].rearrange("p o t -> p (o t)")

            def turns(eng, turn):
                with eng.Fori(0, NK - 1) as i:
                    turn(i, True)
                turn(NK - 1, False)

            with nc.Block() as block:
                @block.gpsimd
                def _(pool):
                    def take_lora2(n):
                        for e in range(2):
                            ins = pool.tensor_tensor(lora2[:, e, :], w2a2[:, bass.ds(n * P, P)],
                                                     same_head[:, e * HD:e * HD + 1].to_broadcast([P, P]), ALU.mult)
                        ins.then_inc(E["lora2"], 1)

                    def turn(i, more):
                        if more:
                            pool.wait_ge(E["lora"], i + 1)
                            take_lora2(i + 1)
                        for u in range(8):
                            pool.wait_ge(d_low, i * 8 + u + 1)
                            pool.tensor_tensor(AKM[:, u, 0:P], AKM[:, u, 0:P], XX[:, u, P:2 * P], ALU.subtract)
                            pool.tensor_tensor(TT[:, u, :], XX[:, u, P:2 * P], ident, ALU.add).then_inc(d_akm, 1)
                        pool.wait_ge(E["yc"], i + 1)
                        pool.tensor_copy(V, v3[:, :, bass.ds(i * P, P)]).then_inc(E["val"], 1)

                    link = Chain(pool, pool_chain)
                    link(pool.memset(keep, 1.0))
                    link(pool.memset(keep.rearrange("p (c t) -> p c t", c=NC_R)[:, :, 0:1], 0.0))
                    link(pool.memset(MT, 0.0))
                    link(pool.tensor_copy(low_st_d, low_st))
                    for r in range(P // RB - 1):
                        link(pool.memset(low_st_d[r * RB:(r + 1) * RB, (r + 1) * RB:P], 0.0))
                    pool.tensor_copy(cols[:, 32:33], one_col).then_inc(consts.sem, 1)
                    take_lora2(0)
                    turns(pool, turn)

                @block.tensor
                def _(pe):
                    def lora(u):
                        return pe.matmul(ps[:, u, strip], lora2[:, u // NT, :], h_wa[:, u % NT * P:(u % NT + 1) * P],
                                         start=True, stop=True)

                    def head_sums():
                        for j in range(NT):
                            ins = pe.matmul(ps[:, 0, 3 * P + 2 * j:3 * P + 2 * j + 2], norm[:, j * P:(j + 1) * P],
                                            same_head[:, 0:P:HD], start=True, stop=True)
                        return ins

                    def wide(j):
                        return pe.transpose(ps[:, j, strip], norm[:, j * P:(j + 1) * P], ident)

                    def turn(i, more):
                        pe.wait_ge(E["ops"], i + 1)
                        for n, src in enumerate((A_T, B_T.rearrange(tile4, j=NT), K_T.rearrange(tile4, j=NT))):
                            for j in range(NT):
                                pe.transpose(ps[:, n, j * P:(j + 1) * P], src[:, j, :], ident)
                        for j in range(NT):
                            ins = pe.matmul(ps[:, 3, 2 * j:2 * j + 2], rkr[:, j * P:(j + 1) * P], same_head[:, 0:P:HD],
                                            start=True, stop=True)
                        ins.then_inc(E["turned"], 1)
                        for u, (e, j) in enumerate(units):
                            ins = pe.matmul(ps[:, 4 + e, j * P:(j + 1) * P], A_T[rows_of(e), j, :],
                                            B_T[rows_of(e), j * P:(j + 1) * P], start=True, stop=True)
                        ins.then_inc(E["low"], 1)
                        for u, (e, j) in enumerate(units):
                            if u == 0:
                                pe.wait_ge(E["tok"], i + 1)
                            if u == 4:
                                pe.wait_ge(E["lowm"], i + 1)
                            if u == 6:
                                pe.wait_ge(E["yc"], i + 1)
                            for n, src in enumerate((B_T, K_T)):
                                ins = pe.matmul(ps[:, u, 2 * n * P:2 * (n + 1) * P], src[rows_of(e), j * P:(j + 1) * P],
                                                AR[rows_of(e), j, :, :], start=True, stop=True)
                            ins.then_inc(p_akm, 1)
                        for r in range(ROUNDS):
                            for u in range(8):
                                if r == 0:
                                    pe.wait_ge(d_akm, i * 8 + u + 1)
                                else:
                                    pe.wait_ge(a_sq, i * 8 * ROUNDS + 8 * (r - 1) + u + 1)
                                    pe.wait_ge(d_tt, i * 8 * ROUNDS + 8 * (r - 1) + u + 1)
                                x, xt = XX[:, u, 0:P], XX[:, u, P:2 * P]
                                pe.matmul(ps[:, u, 0:P], xt, x, start=True, stop=True)
                                pe.matmul(ps[:, u, P:2 * P], x, xt, start=True, stop=True).then_inc(p_sq, 1)
                            if more and r == 0:
                                pe.wait_ge(E["lora2"], i + 2)
                            if more and r == 1:
                                pe.wait_ge(E["sq"], i + 2)
                            if more and r == 2:
                                pe.wait_ge(E["inverse"], i + 2)
                            if r == 3:
                                pe.wait_ge(E["val"], i + 1)
                            for u in range(8):
                                pe.wait_ge(a_sq, i * 8 * ROUNDS + 8 * r + u + 1)
                                ins = pe.matmul(ps[:, u, 2 * P:3 * P], XX[:, u, 0:P], TT[:, u, :], start=True, stop=True)
                                if more and r == 0:
                                    ins = lora(u)
                                if more and r == 1 and u == 0:
                                    ins = head_sums()
                                if more and r == 2 and u < NT:
                                    ins = wide(u)
                                if r == 3:
                                    e, j = units[u]
                                    ins = pe.matmul(ps[:, u, 3 * P:3 * P + HD], AKM[:, u, 2 * P:3 * P], V[:, j, rows_of(e)],
                                                    start=True, stop=True)
                                ins.then_inc(p_tt, 1)
                        def four(half, bank, lhs, rhs, done):
                            for u in range(4 * half, 4 * half + 4):
                                ins = pe.matmul(ps[:, bank + half, u % 4 * P:(u % 4 + 1) * P], lhs(u), rhs[:, u, :],
                                                start=True, stop=True)
                            ins.then_inc(done, 1)

                        def r2(u):
                            e, j = units[u]
                            return pe.matmul(ps[rows_of(e), 3, j * P:(j + 1) * P], QC[:, u, 0:HD], AKM[:, u, P:2 * P],
                                             start=True, stop=True)

                        pe.wait_ge(d_tt, (i + 1) * (8 * ROUNDS))
                        for half in range(2):
                            four(half, 1, lambda u: TT[:, u, :], RH, E["q"])
                        for half in range(2):
                            pe.wait_ge(E[("qc", "qc2")[half]], i + 1)
                            four(half, 5, lambda u: AKM[:, u, 0:P], QC, E["z"])
                        for half in range(2):
                            pe.wait_ge(E[("zc", "zc2")[half]], i + 1)
                            four(half, 1, lambda u: TT[:, u, :], Z, E["q2"])
                        pe.wait_ge(E["q2c"], 2 * i + 1)
                        for u in range(4):
                            r2(u)
                        pe.wait_ge(E["q2c"], 2 * i + 2)
                        r2(4)
                        for half in range(2):
                            hs = rows_of(half)
                            m = [ps[rows_of(e), 5 + half, j * HD:(j + 1) * HD] for e, j in units]
                            n = [ps[rows_of(e), 7 * (1 - half), j * HD:(j + 1) * HD] for e, j in units]
                            in_turn = [(u, *units[u]) for j in range(NT) for u in (j, NT + j)]
                            for u, e, j in in_turn:
                                pe.matmul(m[u], QC[hs, u, 0:HD], B_tok[hs, j, rows_of(e)], start=True, stop=True)
                            for u, e, j in in_turn:
                                pe.matmul(n[u], B_tok[hs, j, rows_of(e)], QC[hs, u, HD:P], start=True, stop=False)
                                ins = pe.matmul(n[u], K_tok[hs, j, rows_of(e)], V[hs, j, rows_of(e)], start=False, stop=True)
                            ins.then_inc(E["mn"], 1)
                        pe.wait_ge(E["mnc"], i + 1)
                        for c in range(1, NC_R + 1):
                            if 2 <= c < NC_R:
                                pe.wait_ge(d_s, i * (NC_R - 1) + c - 1)
                            if c < NC_R:
                                pe.matmul(ps[:, 1, c * HD:(c + 1) * HD], MT[:, c - 1, :], S[:, c - 1, :],
                                          start=True, stop=True).then_inc(p_s, 1)
                            if c <= 3:
                                ins = r2(c + 4)
                            if c == 3:
                                ins.then_inc(E["r2"], 1)
                            e, j = units[c - 1]
                            o = ps[:, 4, (2 * j + e) * HD:(2 * j + e + 1) * HD]
                            pe.matmul(o, AKM[:, c - 1, P:2 * P], QC[:, c - 1, HD:P], start=True, stop=False)
                            ins = pe.matmul(o, AKM[:, c - 1, 3 * P:4 * P], V[:, j, rows_of(e)], start=False, stop=True)
                        ins.then_inc(E["y0"], 1)
                        pe.wait_ge(E["r2c"], i + 1)
                        pe.wait_ge(E["y0c"], i + 1)
                        pe.wait_ge(d_s, (i + 1) * (NC_R - 1))
                        for e, j in units:
                            ins = pe.matmul(ps[:, 6 + e, j * P:(j + 1) * P], RQ[rows_of(e), j * P:(j + 1) * P],
                                            S[rows_of(e), 2 * j:2 * j + 2, :], start=True, stop=True)
                        ins.then_inc(E["yy"], 1)

                    pe.wait_ge(E["lora2"], 1)
                    for u in range(8):
                        ins = lora(u)
                    ins.then_inc(E["first_lora"], 1)
                    pe.wait_ge(E["sq"], 1)
                    pe.wait_ge(E["lora"], 1)
                    head_sums().then_inc(E["first_sums"], 1)
                    pe.wait_ge(E["inverse"], 1)
                    for j in range(NT):
                        ins = wide(j)
                    ins.then_inc(E["first_wide"], 1)
                    turns(pe, turn)

                @block.scalar
                def _(act):
                    def sigmoids(n):
                        act.wait_ge(E["lora"], n + 1)
                        act.wait_ge(E["par"], n + 1)
                        act.activation(logd, logd, ACT.Sigmoid, bias=pcol[:, W0:W0 + 1])
                        act.activation(lr, lr, ACT.Sigmoid, bias=pcol[:, A0:A0 + 1]).then_inc(E["sig"], 1)

                    def exponentials(n):
                        act.wait_ge(E["shift"], n + 1)
                        act.activation(decay, cum, ACT.Exp)
                        act.activation(inv, cum, ACT.Exp, scale=-1.0)
                        act.activation(before_d, before_d, ACT.Exp)
                        act.wait_ge(E["ssq"], n + 1)
                        act.activation(heads, heads, ACT.Sqrt).then_inc(E["exp"], 1)

                    def turn(i, more):
                        act.wait_ge(E["turned"], i + 1)
                        act.activation(RH.rearrange("p (e j) c -> p j e c", e=2)[:, :, :, 0:HD],
                                       ps[:, 0, :].rearrange("p (j e c) -> p j e c", j=NT, e=2), ACT.Copy)
                        for n, dst in enumerate((B_tok, K_tok)):
                            act.activation(dst, ps[:, 1 + n, :].rearrange(tile4, j=NT), ACT.Copy)
                        act.activation(k3[:, bass.ds(i, 1), 0:2 * NT], ps[:, 3, 0:2 * NT].unsqueeze(1), ACT.Copy).then_inc(E["tok"], 1)
                        act.wait_ge(E["yc"], i + 1)
                        act.activation(RQ.rearrange(tile4, j=NT), R_T, ACT.Copy)
                        for r in range(ROUNDS):
                            for u in range(8):
                                act.wait_ge(p_sq, i * 8 * ROUNDS + 8 * r + u + 1)
                                act.activation(XX[:, u, :], ps[:, u, 0:2 * P], ACT.Copy).then_inc(a_sq, 1)
                            if more and r == 0:
                                sigmoids(i + 1)
                            if more and r == 1:
                                exponentials(i + 1)
                        for bank, dst, done, taken in ((1, QC, "q", "qc"), (5, Z, "z", "zc")):
                            act.wait_ge(E[done], 2 * i + 1)
                            act.activation(dst[:, 0:4, :], ps[:, bank, :].rearrange("p (u c) -> p u c", u=4), ACT.Copy)\
                               .then_inc(E[taken], 1)
                        act.wait_ge(E["y0"], i + 1)
                        act.activation(Y0, ps[:, 4, :].rearrange("p (j e c) -> p j e c", j=NT, e=2), ACT.Copy).then_inc(E["y0c"], 1)

                    sigmoids(0)
                    exponentials(0)
                    turns(act, turn)

                @block.vector
                def _(dve):
                    c0 = consts.total + 1

                    def take_lora(u):
                        return dve.tensor_copy((logd, lr)[u // NT][:, u % NT * P:(u % NT + 1) * P], ps[:, u, strip])

                    def take_sums():
                        return dve.tensor_copy(heads, ps[:, 0, 3 * P:3 * P + 2 * NT].rearrange("p (j e) -> p j e", j=NT))

                    def unit_kk(j):
                        kj = kk[:, j * P:(j + 1) * P]
                        return dve.tensor_tensor(kj, kj, ps[:, j, strip], ALU.mult)

                    def squares(n, link):
                        dve.tensor_copy(pcol, par[:, :, bass.ds(n, 1)].rearrange("p n o -> p (n o)")).then_inc(E["par"], 1)
                        dve.wait_ge(E["par"], n + 1)
                        link(dve.tensor_scalar(kk, tile_of(k3, n), pcol[:, K_K:K_K + 1], None, ALU.mult))
                        dve.tensor_tensor(norm, kk, kk, ALU.mult).then_inc(E["sq"], 1)

                    def log_decays(n, link):
                        dve.wait_ge(E["sig"], n + 1)
                        link(dve.tensor_scalar(logd, logd, -float(np.exp(-0.5)), None, ALU.mult))
                        link(dve.tensor_tensor_scan(cum, keep, logd, 0.0, ALU.mult, ALU.add))
                        dve.tensor_tensor(before_d, cum, logd, ALU.subtract).then_inc(E["shift"], 1)
                        link(dve.tensor_scalar(K_T, lr, 1.0, pcol[:, K_A:K_A + 1], ALU.subtract, ALU.mult))
                        link(dve.scalar_tensor_tensor(K_T, K_T, 1.0, tile_of(k3, n), ALU.add, ALU.mult))

                    def inverse_norms(n, link):
                        dve.wait_ge(E["exp"], n + 1)
                        link(dve.tensor_scalar(heads, heads, 1e-12, None, ALU.max))
                        link(dve.reciprocal(heads, heads))
                        dve.tensor_copy(norm.rearrange("p (j e c) -> p j e c", j=NT, e=2),
                                        heads.unsqueeze(3).to_broadcast([P, NT, 2, HD])).then_inc(E["inverse"], 1)

                    def operands(n, link):
                        dve.scalar_tensor_tensor(A_T, kk.rearrange(tile4, j=NT), -1.0, before_d.rearrange(tile4, j=NT), ALU.mult, ALU.mult)
                        link(dve.tensor_tensor(B_T, kk, lr, ALU.mult))
                        dve.tensor_tensor(B_T, B_T, inv, ALU.mult)
                        dve.tensor_tensor(R_T, tile_of(rT, n).rearrange(tile4, j=NT), decay.rearrange(tile4, j=NT), ALU.mult)
                        link(dve.scalar_tensor_tensor(rkr, tile_of(rT, n), pcol[:, R_K:R_K + 1], K_T, ALU.mult, ALU.mult))
                        link(dve.tensor_tensor(K_T, K_T, inv, ALU.mult))
                        dve.memset(mean_var[:, 5:6], 0.0).then_inc(E["ops"], 1)

                    def turn(i, more):
                        link = LoopChain(dve, chain_v, PREPARE_LINKS, i, TURN_LINKS)
                        link(dve.tensor_copy(p_end, decay[:, RC - 1::RC]))
                        dve.wait_ge(E["low"], i + 1)
                        dve.tensor_tensor(XX[:, :, 0:P], ps[:, 4:6, :].rearrange("p b (u c) -> p (b u) c", u=4),
                                          low_ts.unsqueeze(1).to_broadcast([P, 8, P]), ALU.mult).then_inc(E["lowm"], 1)
                        for u in range(8):
                            dve.wait_ge(p_akm, i * 8 + u + 1)
                            dve.tensor_tensor(XX[:, u, P:2 * P], ps[:, u, 0:P], low_st_d, ALU.mult)
                            dve.tensor_tensor(AKM[:, u, :].rearrange("p (a c) -> p a c", a=2),
                                              ps[:, u, :].rearrange("p (a c) -> p a c", a=2),
                                              masks.unsqueeze(1).to_broadcast([P, 2, 2 * P]), ALU.mult).then_inc(d_low, 1)
                        if more:
                            squares(i + 1, link)
                        for r in range(ROUNDS):
                            for u in range(8):
                                dve.wait_ge(p_tt, i * 8 * ROUNDS + 8 * r + u + 1)
                                ins = dve.tensor_tensor(TT[:, u, :], TT[:, u, :], ps[:, u, 2 * P:3 * P], ALU.add)
                                if more and r == 0:
                                    ins = take_lora(u)
                                if more and r == 1 and u == 0:
                                    ins = take_sums()
                                if more and r == 2 and u < NT:
                                    ins = unit_kk(u)
                                if r == 3:
                                    ins = dve.tensor_copy(RH[:, u, HD:P], ps[:, u, 3 * P:3 * P + HD])
                                ins.then_inc(d_tt, 1)
                            if more and r == 0:
                                dve.memset(mean_var[:, 5:6], 0.0).then_inc(E["lora"], 1)
                            if more and r == 1:
                                dve.memset(mean_var[:, 5:6], 0.0).then_inc(E["ssq"], 1)
                            if more and r == 0:
                                log_decays(i + 1, link)
                            if more and r == 1:
                                inverse_norms(i + 1, link)
                            if more and r == 2:
                                link(dve.memset(mean_var[:, 5:6], 0.0))
                                dve.wait_ge(E["tok"], i + 1)
                                operands(i + 1, link)
                        for bank, dst, done, taken in ((2, QC, "q", "qc2"), (6, Z, "z", "zc2")):
                            dve.wait_ge(E[done], 2 * i + 2)
                            dve.tensor_copy(dst[:, 4:8, :], ps[:, bank, :].rearrange("p (u c) -> p u c", u=4)).then_inc(E[taken], 1)
                        for half in range(2):
                            dve.wait_ge(E["q2"], 2 * i + 1 + half)
                            dve.wait_ge(E[("qc", "qc2")[half]], i + 1)
                            qc = QC[:, 4 * half:4 * half + 4, :]
                            dve.tensor_tensor(qc, qc, ps[:, 1 + half, :].rearrange("p (u c) -> p u c", u=4), ALU.add)\
                               .then_inc(E["q2c"], 1)
                        pe2 = p_end.rearrange("p (j h) -> p j h", h=2)
                        mt, nn = (m.rearrange("p (j h) i -> p j h i", h=2) for m in (MT, NN))
                        for half in range(2):
                            dve.wait_ge(E["mn"], 2 * i + 1 + half)
                            for e in range(2):
                                dve.tensor_tensor(mt[rows_of(e), :, half, e * HD:(e + 1) * HD],
                                                  ps[rows_of(e), 5 + half, 0:NT * HD].rearrange("p (j i) -> p j i", j=NT),
                                                  ident[rows_of(e), rows_of(e)].unsqueeze(1).to_broadcast([HD, NT, HD]), ALU.add)
                            ins = dve.tensor_tensor(nn[:, :, half, :], ps[:, 7 * (1 - half), 0:NT * HD].rearrange("p (j i) -> p j i", j=NT),
                                                    pe2[:, :, half].unsqueeze(2).to_broadcast([P, NT, HD]), ALU.mult)
                        link(ins)
                        dve.memset(S[:, 0, :], 0.0).then_inc(E["mnc"], 1)
                        for c in range(1, NC_R):
                            dve.wait_ge(p_s, i * (NC_R - 1) + c)
                            dve.scalar_tensor_tensor(S[:, c, :], ps[:, 1, c * HD:(c + 1) * HD], p_end[:, c - 1:c],
                                                     NN[:, c - 1, :], ALU.mult, ALU.add).then_inc(d_s, 1)
                            if c == 4:
                                dve.wait_ge(E["r2"], i + 1)
                                dve.tensor_tensor(RQ, RQ, ps[:, 3, :], ALU.add).then_inc(E["r2c"], 1)
                        dve.wait_ge(E["y0c"], i + 1)
                        dve.wait_ge(E["yy"], i + 1)
                        for e in range(2):
                            for h in range(2):
                                ins = dve.tensor_tensor(tile_of(rT, i)[rows_of(h), :].rearrange("p (j e v) -> p j e v", j=NT, e=2)[:, :, e, :],
                                                        ps[rows_of(h), 6 + e, :].rearrange("p (j v) -> p j v", j=NT)[:, :, rows_of(h)],
                                                        Y0[rows_of(h), :, e, :], ALU.add)
                        ins.then_inc(E["yc"], 1)

                    dve.memset(mean_var[:, 5:6], 0.0).then_inc(E["yc"], 1)
                    dve.wait_ge(consts.sem, c0)
                    link = LoopChain(dve, chain_v, 0, 0, 0)
                    squares(0, link)
                    dve.wait_ge(E["first_lora"], 1)
                    for u in range(8):
                        ins = take_lora(u)
                    ins.then_inc(E["lora"], 1)
                    log_decays(0, link)
                    dve.wait_ge(E["first_sums"], 1)
                    take_sums().then_inc(E["ssq"], 1)
                    inverse_norms(0, link)
                    dve.wait_ge(E["first_wide"], 1)
                    for j in range(NT):
                        ins = unit_kk(j)
                    link(ins)
                    operands(0, link)
                    assert link.at == PREPARE_LINKS, link.at
                    turns(dve, turn)
            consts.take(1)

        def wkv_out_stage():
            y = arena[:, 0:NK * T].rearrange("p (n v) -> p n v", v=HD)
            by_tile = "p (c j v) -> p c j v"
            yc = arena[:, 0:NK * T].rearrange(by_tile, c=NK, j=NT)
            tmp = arena[:, NK * T:2 * NK * T].rearrange("p (n v) -> p n v", v=HD)
            tmp_c = arena[:, NK * T:2 * NK * T].rearrange(by_tile, c=NK, j=NT)
            g2a, g2b, ln_g, ln_b = (view(arena, 3 * NK * T + n * D, D) for n in range(4))
            bonus_all = view(rows, 128, NK, NT, 2)
            mean, var = view(rows, 0, 64), view(rows, 64, 64)
            l0, x0, a0, m0 = loaded.take(64), dve_a.take(1), act_a.take(1), mm.take(2 * NT)

            def by_channel(row):
                return row.rearrange("p (c v) -> p c v", c=NK).unsqueeze(2).to_broadcast([P, NK, NT, P])

            with nc.Block() as block:
                @block.sync
                def _(sp):
                    stream_mixer(sp, mixer_at[2] + 8, mixer_at[2] + 12)

                @block.gpsimd
                def _(pool):
                    for dst, src in ((g2a, a["rw_g2_2"][0][0:P]), (g2b[0:GATE_LORA - P, :], a["rw_g2_2"][0][P:GATE_LORA]),
                                     (ln_g, a["rw_lnx_g_2"][0].partition_broadcast(P)),
                                     (ln_b, a["rw_lnx_b_2"][0].partition_broadcast(P))):
                        pool.dma_start(dst, src).then_inc(loaded.sem, 16)

                @block.tensor
                def _(pe):
                    pe.wait_ge(loaded.sem, l0 + 64)
                    for n in range(2 * NT):
                        j, c = n // 2, n % 2
                        pe.matmul(ps[:, n, :], h_g[:, j * P:(j + 1) * P], g2a[:, c * CH:(c + 1) * CH], start=True, stop=False)
                        pe.matmul(ps[:, n, :], h_g2[:, j * P:(j + 1) * P], g2b[0:GATE_LORA - P, c * CH:(c + 1) * CH],
                                  start=False, stop=True).then_inc(mm.sem, 1)

                @block.scalar
                def _(act):
                    act.wait_ge(dve_a.sem, x0 + 1)
                    act.activation(var, var, ACT.Sqrt, bias=eps_gn).then_inc(act_a.sem, 1)

                @block.vector
                def _(dve):
                    link = Chain(dve, dve_chain)
                    wide = [P, 64, HD]
                    link(dve.tensor_copy(bonus_all.rearrange("p c j e -> p c (j e)"), k3[:, :, 0:2 * NT]))
                    link(dve.tensor_reduce(mean, y, AX, ALU.add))
                    link(dve.tensor_scalar(mean, mean, 1.0 / HD, None, ALU.mult))
                    link(dve.tensor_tensor(y, y, mean.unsqueeze(2).to_broadcast(wide), ALU.subtract))
                    link(dve.tensor_tensor(tmp, y, y, ALU.mult))
                    link(dve.tensor_reduce(var, tmp, AX, ALU.add))
                    dve.tensor_scalar(var, var, 1.0 / HD, None, ALU.mult).then_inc(dve_a.sem, 1)
                    for c in range(NK):
                        ins = dve.tensor_tensor(tmp_c[:, c, :, :].rearrange("p j (e v) -> p j e v", e=2),
                                                v3[:, :, c * P:(c + 1) * P].rearrange("p j (e v) -> p j e v", e=2),
                                                bonus_all[:, c, :, :].unsqueeze(3).to_broadcast([P, NT, 2, HD]), ALU.mult)
                    link(ins)
                    dve.wait_ge(act_a.sem, a0 + 1)
                    link(dve.reciprocal(var, var))
                    link(dve.tensor_tensor(y, y, var.unsqueeze(2).to_broadcast(wide), ALU.mult))
                    dve.wait_ge(loaded.sem, l0 + 64)
                    link(dve.tensor_tensor(yc, yc, by_channel(ln_g), ALU.mult))
                    link(dve.tensor_tensor(yc, yc, by_channel(ln_b), ALU.add))
                    link(dve.tensor_tensor(y, y, tmp, ALU.add))
                    for n in range(2 * NT):
                        j, c = n // 2, n % 2
                        dve.wait_ge(mm.sem, m0 + n + 1)
                        dve.tensor_tensor(yc[:, 4 * c:4 * c + 4, j, :], yc[:, 4 * c:4 * c + 4, j, :],
                                          ps[:, n, :].rearrange("p (c v) -> p c v", c=4), ALU.mult)

        def store_stage():
            o0 = stored.take(16)
            with nc.Block() as block:
                @block.sync
                def _(sp):
                    sp.dma_start(out[0].rearrange("(j p) d -> p j d", p=P), x_tok).then_inc(stored.sem, 16)
                    sp.wait_ge(stored.sem, o0 + 16)

        def program():
            start_stage()
            in_proj_stage()
            decay_stage()
            ssd_stage()
            attention_stage(1, lambda h, c: qT[HD * (h % 2):HD * (h % 2 + 1), h // 2, :],
                            lambda h, c: kT[HD * (h % 2):HD * (h % 2 + 1), h // 2, :], v_tok, HD,
                            lambda h, j: merged_a[:, j, h * HD:(h + 1) * HD], forget=True)
            mT = view(arena, 0, NK, T)
            transpose_stage(lambda j, k: (merged_s if k < 4 else merged_a)[:, j, (k % 4) * P:(k % 4 + 1) * P], mT)
            project_out_stage(0, ALPHA_1, mT, a["ln1_g"][0], a["ln1_b"][0])
            if stop == "h1":
                return
            moe_stage(0, ALPHA_1, a["ln2_g"][0], a["ln2_b"][0], False)
            if stop == "x1":
                return
            qkv_stage()
            attention_stage(2, lambda h, c: q2[HD * c:HD * (c + 1), h, :], lambda h, c: k2[HD * c:HD * (c + 1), h, :],
                            v2, 2 * HD, lambda h, j: o2[:, j, h * P:(h + 1) * P], lam=lam)
            subln_stage()
            transpose_stage(lambda j, k: o2[:, j, k * P:(k + 1) * P], mT)
            project_out_stage(1, ALPHA_2, mT, a["ln1_g_2"][0], a["ln1_b_2"][0])
            if stop == "h2":
                return
            moe_stage(1, ALPHA_2, a["ln2_g_2"][0], a["ln2_b_2"][0], False)
            if stop == "x2":
                return
            rkv_stage()
            wkv_stage()
            wkv_out_stage()
            mT3 = view(arena, NK * T, NK, T)
            y3 = rT.rearrange("p c (j v) -> p c j v", j=NT)
            transpose_stage(lambda j, k: y3[:, k, j, :], mT3)
            project_out_stage(2, ALPHA_2, mT3, a["ln1_g_2"][1], a["ln1_b_2"][1])
            if stop == "h3":
                return
            moe_stage(2, ALPHA_2, a["ln2_g_2"][1], a["ln2_b_2"][1], True)

        program()
        store_stage()


_INS = ["x", "w_in", "b_in", "conv_w", "conv_b", "a_log", "d_skip", "ssd_norm_g", "w_out", "ln1_g", "ln1_b",
        "router_group_w", "router_group_b", "router_expert_w", "router_expert_b", "w_gate", "w_up", "w_down",
        "ln2_g", "ln2_b", "ln1_g_2", "ln1_b_2", "ln2_g_2", "ln2_b_2", "attn_w_qkv_2", "attn_w_o_2", "attn_lambda_2",
        "attn_subln_g_2", "rw_mu_2", "rw_w_rkv_2", "rw_w_o_2", "rw_w0_2", "rw_w1_2", "rw_w2_2", "rw_a0_2", "rw_a1_2",
        "rw_a2_2", "rw_g1_2", "rw_g2_2", "rw_k_k_2", "rw_k_a_2", "rw_r_k_2", "rw_lnx_g_2", "rw_lnx_b_2",
        "rw_v0_2", "rw_v1_2", "rw_v2_2",
        "moe_rg_w_2", "moe_rg_b_2", "moe_re_w_2", "moe_re_b_2", "moe_w_gu_2", "moe_w_down_2"]
_OUT_SHAPE = (1, T, D)
_STOP = None


def kernel(**inputs):
    import concourse.bacc as bacc
    from concourse.bass_utils import run_bass_kernel_spmd

    nc = bacc.Bacc("TRN2", target_bir_lowering=False, num_devices=1)
    arrays, aps = {}, {}
    for name in _INS:
        arr = np.ascontiguousarray(inputs[name])
        if not arr.size:
            continue
        arrays[f"in_{name}"] = arr
        aps[name] = nc.dram_tensor(f"in_{name}", arr.shape, mybir.dt.from_np(arr.dtype), kind="ExternalInput").ap()
    out = nc.dram_tensor("out", _OUT_SHAPE, F32, kind="ExternalOutput").ap()
    build(nc, aps, out, _STOP)
    r = run_bass_kernel_spmd(nc, [arrays], core_ids=[0])
    return r.results[0]["out"]
```

```python
from contextlib import ExitStack

import numpy as np

import concourse.bass as bass
from concourse import mybir

F32 = mybir.dt.float32
I32 = mybir.dt.int32
U32 = mybir.dt.uint32
ALU = mybir.AluOpType
ACT = mybir.ActivationFunctionType
AX = mybir.AxisListType.X

P = 128
T = 512
D = 1024
NT = T // P
NK = D // P
CH = 512
SLOTS = 6
LN_EPS = 1e-5
RMS_EPS = 1e-5
NEG = -1e30
BLK = 32

HEADS = 8
HD = 64
STATE = 128
GROUPS = 2
CONV_W = 4
O_Z, O_XS, O_BC, O_DT, O_Q, O_K, O_V, O_F = 0, 512, 1024, 1536, 1544, 2056, 2568, 3080
F_ROW = 32
ALPHA_1 = 2.0 ** 0.25
ALPHA_2 = 4.0 ** 0.25
SCALE = HD ** -0.5
LAMBDA_INIT = 0.8 - 0.6
DA_HEADS = 8

RC = 64
NC_R = T // RC
RB = 32
DECAY_LORA, AAA_LORA, GATE_LORA = 64, 64, 160
GN_EPS = 64e-5


class Signal:

    def __init__(self, sem):
        self.sem = sem
        self.total = 0

    def take(self, n):
        base = self.total
        self.total += n
        return base


class Chain:

    def __init__(self, eng, steps):
        self.eng, self.steps = eng, steps

    def __call__(self, ins):
        self.steps.total += 1
        ins.then_inc(self.steps.sem, 1)
        self.eng.wait_ge(self.steps.sem, self.steps.total)


def build(nc, a, out, stop=None):
    ctx = ExitStack()
    with ctx:
        def sb(name, cols, dt=F32):
            return ctx.enter_context(nc.sbuf_tensor(name, [P, cols], dt))

        def signal(name):
            return Signal(ctx.enter_context(nc.semaphore(name)))

        ring = sb("ring", SLOTS * NK * CH)
        x_tok = sb("x_tok", NT * D)[:, :].rearrange("p (j d) -> p j d", j=NT)
        xt_mem = sb("xt_mem", NK * T)
        xT = xt_mem[:, :].rearrange("p (k t) -> p k t", k=NK)
        arena = sb("arena", 16448)
        rows = sb("rows", 2 * D)
        cst = sb("cst", 8 * P + BLK + 64)
        small = sb("small", 760)
        ps = ctx.enter_context(nc.psum_tensor("ps", [P, 8, 512], F32))
        ybuf = nc.dram_tensor("ybuf", [(2 * T // BLK + 32) * BLK, D], F32).ap()

        def const(n, w=P):
            return cst[:, n * P:n * P + w]

        ident, mask_qk, mask_sq, before, ones, low_ts, low_st, upto_st = (const(n) for n in range(8))
        iota_f = cst[:, 8 * P:8 * P + BLK]
        cols = cst[:, 8 * P + BLK:8 * P + BLK + 64]
        eps_ln = cols[:, 0:1]
        one_col = cols[:, 1:2]
        eps_gn = cols[:, 2:3]

        def view(mem, at, *shape):
            n = int(np.prod(shape))
            v = mem[:, at:at + n]
            if len(shape) == 2:
                return v.rearrange("p (a b) -> p a b", a=shape[0])
            if len(shape) == 3:
                return v.rearrange("p (a b c) -> p a b c", a=shape[0], b=shape[1])
            return v

        def slot(n):
            return ring[:, n * NK * CH:(n + 1) * NK * CH]

        arrived = [signal(f"chunk_arrived{n}") for n in range(SLOTS)]
        arrived_x = [signal(f"third_expert_{kind}_arrived") for kind in ("gate", "up", "down")]
        loaded = signal("params_loaded")
        x_loaded = signal("x_loaded")
        router_in = signal("router_loaded")
        mixer_params = signal("mixer_params_loaded")
        zeroed = signal("ybuf_zeroed")
        consts = signal("consts_ready")
        mm = signal("matmuls_done")
        tr = signal("transposes_done")
        ev = signal("act_evacuated")
        padded = signal("queries_padded")
        dve_chain = signal("dve_chain")
        act_chain = signal("act_chain")
        pool_chain = signal("pool_chain")
        scaled = signal("norm_scaled")
        ln_done = signal("norm_done")
        rows_in = [signal(f"expert_rows_gathered{j}") for j in range(NT)]
        stat = signal("variance_ready")
        sq = signal("deviation_ready")
        stored = signal("output_stored")
        pe_a = signal("pe_a_done")
        pe_b = signal("pe_b_done")
        pe_c = signal("pe_c_done")
        act_a = signal("act_a_done")
        act_b = signal("act_b_done")
        dve_a = signal("dve_a_done")
        dve_b = signal("dve_b_done")
        dve_c = signal("dve_c_done")

        def cols_of(w, c0):
            return w.rearrange("(k p) n -> p k n", p=P)[:, :, c0:c0 + CH]

        def layer_chunks(ws):
            return [cols_of(w, c) for w, cs in ws for c in cs]

        w_in, w_out = a["w_in"][0], a["w_out"][0]
        w_qkv, w_o2 = a["attn_w_qkv_2"][0], a["attn_w_o_2"][0]
        rkv, w_o3 = a["rw_w_rkv_2"][0], a["rw_w_o_2"][0]
        stream = []
        mixer_at, moe_at = [], []
        n_experts = [16, 32, 32]
        for n, ws in enumerate((
                [(w_in, (O_Z, O_XS, O_BC, O_Q, O_K, O_V)), (w_out, (0, CH))],
                [(w_qkv, range(0, 3 * D, CH)), (w_o2, (0, CH))],
                [(rkv[0], (0, CH)), (rkv[1], (0, CH)), (rkv[2], (0, CH)), (w_o3, (0, CH))])):
            mixer_at.append(len(stream))
            stream += layer_chunks(ws)
            moe_at.append(len(stream))
            stream += [None] * (3 * (n_experts[n] - n_experts[n] // 3))

        def chunk_dst(src, n):
            return slot(n % SLOTS).rearrange("p (k n) -> p k n", k=src.shape[1])

        def load_chunk(eng, n):
            eng.dma_start(chunk_dst(stream[n], n), stream[n]).then_inc(arrived[n % SLOTS].sem, 16)

        def wait_chunk(eng, n):
            eng.wait_ge(arrived[n % SLOTS].sem, 16 * (n // SLOTS + 1))

        gu = a["moe_w_gu_2"]
        gate_src = [a["w_gate"][0], gu[0][:, :, 0:CH], gu[1][:, :, 0:CH]]
        up_src = [a["w_up"][0], gu[0][:, :, CH:D], gu[1][:, :, CH:D]]
        down_src = [a["w_down"][0], a["moe_w_down_2"][0], a["moe_w_down_2"][1]]

        def kinds(n):
            return (0, 1, 2) if n % SLOTS != SLOTS - 1 else (2, 0, 1)

        def expert_src(l, e, kind):
            return (gate_src, up_src, down_src)[kind][l][bass.ds(e, 1), :, :].rearrange("e (k p) n -> p (e k) n", p=P)

        def load_expert_chunk(eng, l, e, j, n):
            src = expert_src(l, e, kinds(n - j)[j])
            eng.dma_start(chunk_dst(src, n), src).then_inc(arrived[n % SLOTS].sem, 16)

        used = {}

        def stream_mixer(sp, first, last):
            for n in range(first, last):
                if n - SLOTS in used:
                    sp.wait_ge(*used[n - SLOTS])
                if stream[n] is not None:
                    load_chunk(sp, n)
                else:
                    l = max(i for i in range(3) if moe_at[i] <= n)
                    load_expert_chunk(sp, l, (n - moe_at[l]) // 3, (n - moe_at[l]) % 3, n)

        def transpose_stage(src, dst):
            t0 = tr.take(NK)
            with nc.Block() as block:
                @block.tensor
                def _(pe):
                    for k in range(NK):
                        for j in range(NT):
                            ins = pe.transpose(ps[:, k, j * P:(j + 1) * P], src(j, k), ident)
                        ins.then_inc(tr.sem, 1)

                @block.scalar
                def _(act):
                    for k in range(0, NK, 2):
                        act.wait_ge(tr.sem, t0 + k + 1)
                        act.activation(dst[:, k, :], ps[:, k, :], ACT.Copy)

                @block.vector
                def _(dve):
                    for k in range(1, NK, 2):
                        dve.wait_ge(tr.sem, t0 + k + 1)
                        dve.tensor_copy(dst[:, k, :], ps[:, k, :])

        spot = small[:, 0:1]
        g_row, b_row = view(rows, 0, D), view(rows, D, D)
        lnx = small[:, 720:760]
        mean_var = view(lnx, 0, NT, 4)
        sums = view(lnx, 16, 2, 12)

        def measure(dve, link, j):
            for c in range(2):
                ins = dve.bn_stats(sums[:, j % 2, 6 * c:6 * c + 6], x_tok[:, j, c * CH:(c + 1) * CH])
            link(ins)
            dve.bn_aggr(mean_var[:, j, 0:2], sums[:, j % 2, :]).then_inc(stat.sem, 1)

        def scale(dve, link, j, n0):
            xj, mv = x_tok[:, j, :], mean_var[:, j, :]
            dve.wait_ge(sq.sem, n0["sq"] + j + 1)
            link(dve.reciprocal(mv[:, 3:4], mv[:, 2:3]))
            link(dve.tensor_scalar(xj, xj, mv[:, 0:1], mv[:, 3:4], ALU.subtract, ALU.mult))
            ins = dve.tensor_tensor(xj, xj, g_row, ALU.mult)
            if j == NT - 1:
                link(ins)
                ins = dve.tensor_tensor(xj, xj, b_row, ALU.add)
            ins.then_inc(scaled.sem, 1)

        def norm_tiles(dve, link, update, n0):
            for j in range(NT + 1):
                if j < NT:
                    update(j)
                    measure(dve, link, j)
                if j > 0:
                    scale(dve, link, j - 1, n0)

        def deviation(act, j, n0):
            act.wait_ge(stat.sem, n0["stat"] + j + 1)
            act.activation(mean_var[:, j, 2:3], mean_var[:, j, 1:2], ACT.Sqrt, bias=eps_ln).then_inc(sq.sem, 1)

        def shift_tiles(pool, n0):
            for j in range(NT - 1):
                pool.wait_ge(scaled.sem, n0["scaled"] + j + 1)
                pool.tensor_tensor(x_tok[:, j, :], x_tok[:, j, :], b_row, ALU.add).then_inc(ln_done.sem, 1)

        def wait_tile(eng, j, n0):
            if j < NT - 1:
                eng.wait_ge(ln_done.sem, n0["ln_done"] + j + 1)
            else:
                eng.wait_ge(scaled.sem, n0["scaled"] + NT)

        def turn_tile(pe, j, n0):
            wait_tile(pe, j, n0)
            for c in range(2):
                for k in range(4):
                    at = (4 * c + k) * P
                    ins = pe.transpose(ps[:, 2 * j + c, k * P:(k + 1) * P], x_tok[:, j, at:at + P], ident)
                ins.then_inc(tr.sem, 1)

        def take_tile(act, j, n0):
            for c in range(2):
                act.wait_ge(tr.sem, n0["tr"] + 2 * j + c + 1)
                ins = act.activation(xT[:, 4 * c:4 * c + 4, j * P:(j + 1) * P],
                                     ps[:, 2 * j + c, :].rearrange("p (k t) -> p k t", k=4), ACT.Copy)
            return ins

        def norm_bases(turned):
            return {"stat": stat.take(NT), "sq": sq.take(NT), "scaled": scaled.take(NT), "ln_done": ln_done.take(NT - 1),
                    "tr": tr.take(2 * NT if turned else 0)}

        def load_norm_rows(pool, g_src, b_src):
            pool.dma_start(g_row, g_src.partition_broadcast(P)).then_inc(loaded.sem, 16)
            pool.dma_start(b_row, b_src.partition_broadcast(P)).then_inc(loaded.sem, 16)

        R_PAD = 96
        router_mem = arena[:, 2 * NK * T:2 * NK * T + (NK + 1) * R_PAD]

        def router_at(l):
            wr = view(router_mem, 0, NK + 1, R_PAD)
            return 4 + n_experts[l], wr[:, 0:NK, :], wr[0:1, NK, :]

        def router_loads(l):
            return sum((7, 4, 4)[:l + 1])

        def load_router(pool, l):
            NR, wr, brow = router_at(l)

            def load(dst, src):
                pool.dma_start(dst, src).then_inc(router_in.sem, 16)

            link = Chain(pool, pool_chain)
            link(pool.memset(router_mem, 0.0))
            with nc.allow_non_contiguous_dma("router columns"):
                if l == 0:
                    load(wr[:, :, 0:4], a["router_group_w"][0].rearrange("(k p) g -> p k g", p=P))
                    for g in range(4):
                        load(wr[:, :, 4 + g * 4:8 + g * 4], a["router_expert_w"][0][g].rearrange("(k p) e -> p k e", p=P))
                    load(brow[:, 0:4], a["router_group_b"][0].unsqueeze(0))
                    load(brow[:, 4:NR], a["router_expert_b"][0].rearrange("g e -> (g e)").unsqueeze(0))
                else:
                    load(wr[:, :, 0:4], a["moe_rg_w_2"][l - 1].rearrange("(k p) g -> p k g", p=P))
                    load(wr[:, :, 4:NR], a["moe_re_w_2"][l - 1].rearrange("(k p) e -> p k e", p=P))
                    load(brow[:, 0:4], a["moe_rg_b_2"][l - 1].unsqueeze(0))
                    load(brow[:, 4:NR], a["moe_re_b_2"][l - 1].unsqueeze(0))

        def project_out_stage(l, alpha, mT, g_src, b_src):
            first = moe_at[l] - 2
            m0, l0, v0, n0 = mm.take(2 * NT), loaded.take(32), ev.take(NT), norm_bases(True)
            for c in range(2):
                used[first + c] = (mm.sem, m0 + 2 * NT - 1 + c)
            with nc.Block() as block:
                @block.sync
                def _(sp):
                    stream_mixer(sp, first + SLOTS, first + SLOTS + 2)

                @block.gpsimd
                def _(pool):
                    load_norm_rows(pool, g_src, b_src)
                    load_router(pool, l)
                    shift_tiles(pool, n0)

                @block.tensor
                def _(pe):
                    def logits(j):
                        pe.wait_ge(ev.sem, v0 + j + 1)
                        if j == 0:
                            pe.wait_ge(router_in.sem, 16 * router_loads(l))
                        pe.matmul(ps[:, 2 * j, 0:R_PAD], ones[0:1, :], brow, start=True, stop=False)
                        for k in range(NK):
                            ins = pe.matmul(ps[:, 2 * j, 0:R_PAD], xT[:, k, j * P:(j + 1) * P], wr[:, k, :],
                                            start=False, stop=(k == NK - 1))

                    NR, wr, brow = router_at(l)
                    for j in range(NT):
                        for c in range(2):
                            if j == 0:
                                wait_chunk(pe, first + c)
                            w = slot((first + c) % SLOTS).rearrange("p (k n) -> p k n", k=NK)
                            for k in range(NK):
                                ins = pe.matmul(ps[:, 2 * j + c, :], mT[:, k, j * P:(j + 1) * P], w[:, k, :],
                                                start=(k == 0), stop=(k == NK - 1))
                            ins.then_inc(mm.sem, 1)
                        if j >= 2:
                            turn_tile(pe, j - 2, n0)
                    for j in range(NT - 2, NT):
                        logits(j - 2)
                        turn_tile(pe, j, n0)
                    for j in range(NT - 2, NT):
                        logits(j)

                @block.scalar
                def _(act):
                    for j in range(NT):
                        deviation(act, j, n0)
                        if j >= 2:
                            take_tile(act, j - 2, n0).then_inc(ev.sem, 1)
                    for j in range(NT - 2, NT):
                        take_tile(act, j, n0).then_inc(ev.sem, 1)

                @block.vector
                def _(dve):
                    link = Chain(dve, dve_chain)

                    def update(j):
                        for c in range(2):
                            dve.wait_ge(mm.sem, m0 + 2 * j + c + 1)
                            xc = x_tok[:, j, c * CH:(c + 1) * CH]
                            ins = dve.scalar_tensor_tensor(xc, xc, alpha, ps[:, 2 * j + c, :],
                                                           ALU.mult, ALU.add)
                        link(ins)
                        if j == 0:
                            dve.wait_ge(loaded.sem, l0 + 32)

                    norm_tiles(dve, link, update, n0)

        wsmall = view(arena, 4128, NK, 64)
        brow = rows[0:1, 0:2 * T]
        param_rows = view(arena, 12320, P)
        param_cols = small[:, 32:88]
        sign, bgate = small[0:64, 88:89], small[0:64, 89:90]

        def start_stage():
            l0, z0 = x_loaded.take(16), consts.take(1)
            with nc.Block() as block:
                @block.sync
                def _(sp):
                    sp.dma_start(x_tok, a["x"][0].rearrange("(j p) d -> p j d", p=P)).then_inc(x_loaded.sem, 16)
                    stream_mixer(sp, 0, 1)
                    sp.wait_ge(x_loaded.sem, l0 + 16)

                @block.scalar
                def _(act):
                    def load(dst, src):
                        act.dma_start(dst, src).then_inc(mixer_params.sem, 16)

                    act.wait_ge(consts.sem, z0 + 1)
                    wk, b_in = w_in.rearrange("(k p) n -> p k n", p=P), a["b_in"][0]
                    with nc.allow_non_contiguous_dma("narrow columns"):
                        load(param_rows[0:8, :], b_in[O_XS:O_XS + 8 * P].rearrange("(c p) -> c p", p=P))
                        load(param_rows[8:16, :], b_in[O_Q:O_Q + 8 * P].rearrange("(c p) -> c p", p=P))
                        load(param_rows[16:48, :], a["conv_w"][0].rearrange("k (c p) -> (k c) p", p=P))
                        load(param_rows[48:56, :], a["conv_b"][0].rearrange("(c p) -> c p", p=P))
                        load(brow[:, 0:T], b_in[O_Z:O_Z + T].unsqueeze(0))
                        load(brow[:, T:2 * T], b_in[O_V:O_V + T].unsqueeze(0))
                        load(bgate[0:HEADS, :], b_in[O_DT:O_DT + HEADS].unsqueeze(1))
                        load(bgate[F_ROW:F_ROW + HEADS, :], b_in[O_F:O_F + HEADS].unsqueeze(1))
                        load(wsmall[:, :, 0:HEADS], wk[:, :, O_DT:O_DT + HEADS])
                        load(wsmall[:, :, F_ROW:F_ROW + HEADS], wk[:, :, O_F:O_F + HEADS])

                @block.gpsimd
                def _(pool):
                    link = Chain(pool, pool_chain)
                    pool.memset(param_rows, 0.0)
                    pool.memset(sign, -1.0)
                    link(pool.memset(bgate, 0.0))
                    link(pool.memset(sign[0:32, :], 1.0))
                    pool.memset(wsmall, 0.0).then_inc(consts.sem, 1)

                    def select(m, fill, op, base, step, mult):
                        link(pool.affine_select(out=m, in_=m, pattern=[[step, P]], compare_op=op, fill=fill,
                                                base=base, channel_multiplier=mult))

                    for m, v in ((ident, 0.0), (mask_qk, 0.0), (mask_sq, 0.0), (before, 1.0), (ones, 1.0),
                                 (low_ts, 1.0), (low_st, 1.0), (upto_st, 1.0)):
                        pool.memset(m, v)
                    pool.memset(eps_ln, LN_EPS)
                    pool.memset(one_col, 1.0)
                    pool.memset(eps_gn, GN_EPS)
                    link(pool.iota(iota_f, pattern=[[1, BLK]], base=0, channel_multiplier=0,
                                   allow_small_or_imprecise_dtypes=True))
                    select(ident, 1.0, ALU.not_equal, 0, -1, 1)
                    select(mask_qk, NEG, ALU.is_ge, 0, -1, 1)
                    select(mask_sq, NEG, ALU.is_ge, 0, 1, -1)
                    select(before, 0.0, ALU.is_gt, 0, 1, -1)
                    select(low_ts, 0.0, ALU.is_gt, 0, -1, 1)
                    select(low_st, 0.0, ALU.is_gt, 0, 1, -1)
                    select(upto_st, 0.0, ALU.is_ge, 0, 1, -1)
                    for m in (low_st, upto_st):
                        link(pool.memset(m[0:RC, RC:P], 0.0))
                    for r in range(1, P // RB):
                        link(pool.memset(low_ts[r * RB:(r + 1) * RB, 0:r * RB], 0.0))
            transpose_stage(lambda j, k: x_tok[:, j, k * P:(k + 1) * P], xT)

        xbc = view(arena, 0, 8, 516)
        xbc_a = view(arena, 4128, 8, T)
        z_s = view(arena, 8224, NT, T)
        v_tok = view(arena, 10272, NT, T)
        qT = view(arena, 12320, 4, T)
        kT = view(arena, 14368, 4, T)
        gate_u = rows[0:64, 1024:1536]
        gates = rows[:, 1536:2048]
        gate_c = gates[0:64, :]

        def in_proj_stage():
            bcol, convb = param_cols[:, 0:16], param_cols[:, 48:56]
            convw = view(param_cols, 16, CONV_W, 8)
            c0, m0, e0, z0 = consts.take(2), mm.take(25), ev.take(25), dve_a.take(32)
            t0, params = tr.take(1), mixer_params.take(16 * 10) + 16 * 10
            first = mixer_at[0]
            for c in range(6):
                used[first + c] = (mm.sem, m0 + 1 + 4 * (c + 1))
            with nc.Block() as block:
                @block.sync
                def _(sp):
                    sp.wait_ge(mixer_params.sem, params)
                    stream_mixer(sp, first + 1, first + 12)

                @block.gpsimd
                def _(pool):
                    link = Chain(pool, pool_chain)
                    link(pool.memset(xbc[:, :, 0:CONV_W - 1], 0.0))

                    pool.wait_ge(mixer_params.sem, params)
                    pool.tensor_tensor(bgate, bgate, sign, ALU.mult).then_inc(consts.sem, 1)

                def is_tok(c):
                    return c in (0, 5)

                @block.tensor
                def _(pe):
                    pe.wait_ge(mixer_params.sem, params)
                    pe.transpose(ps[:, 7, 0:P], param_rows, ident).then_inc(tr.sem, 1)
                    for n in range(25):
                        if n == 7:
                            pe.wait_ge(consts.sem, c0 + 2)
                        if n >= 8:
                            pe.wait_ge(ev.sem, e0 + n - 7)
                        bank = ps[:, n % 8, :]
                        if n == 0:
                            for k in range(NK):
                                ins = pe.matmul(bank[0:64, :], wsmall[:, k, :], xT[:, k, :],
                                                start=(k == 0), stop=(k == NK - 1))
                            ins.then_inc(mm.sem, 1)
                            continue
                        c, j = (n - 1) // 4, (n - 1) % 4
                        if j == 0:
                            wait_chunk(pe, first + c)
                        w = slot((first + c) % SLOTS).rearrange("p (k n) -> p k n", k=NK)
                        if is_tok(c):
                            pe.matmul(bank, ones[0:1, :], brow[:, (c // 5) * T:(c // 5 + 1) * T], start=True, stop=False)
                        for k in range(NK):
                            if is_tok(c):
                                ins = pe.matmul(bank, xT[:, k, j * P:(j + 1) * P], w[:, k, :],
                                                start=False, stop=(k == NK - 1))
                            else:
                                ins = pe.matmul(bank, w[:, k, j * P:(j + 1) * P], xT[:, k, :],
                                                start=(k == 0), stop=(k == NK - 1))
                        ins.then_inc(mm.sem, 1)

                @block.scalar
                def _(act):
                    act.wait_ge(tr.sem, t0 + 1)
                    act.activation(param_cols, ps[:, 7, 0:56], ACT.Copy).then_inc(consts.sem, 1)
                    act.wait_ge(consts.sem, c0 + 2)
                    for n in range(25):
                        act.wait_ge(mm.sem, m0 + n + 1)
                        bank = ps[:, n % 8, :]
                        c, j = (n - 1) // 4, (n - 1) % 4
                        if n == 0:
                            ins = act.activation(gate_u, bank[0:64, :], ACT.Identity, bias=bgate, scale=sign)
                        elif c == 0:
                            ins = act.activation(z_s[:, j, :], bank, ACT.Silu)
                        elif c == 5:
                            ins = act.activation(v_tok[:, j, :], bank, ACT.Copy)
                        else:
                            dst = (xbc[:, j, 3:515], xbc[:, 4 + j, 3:515], qT[:, j, :], kT[:, j, :])[c - 1]
                            ins = act.activation(dst, bank, ACT.Identity, bias=bcol[:, 4 * (c - 1) + j:4 * (c - 1) + j + 1])
                        ins.then_inc(ev.sem, 1)
                    for c in range(8):
                        act.wait_ge(dve_a.sem, z0 + 25 + c)
                        act.activation(xbc_a[:, c, :], xbc_a[:, c, :], ACT.Silu)

                @block.vector
                def _(dve):
                    dve.wait_ge(consts.sem, c0 + 2)
                    dve.wait_ge(mm.sem, m0 + 1)
                    for k in range(CONV_W):
                        tap = CONV_W - 1 - k
                        for c in range(8):
                            if k == 0:
                                dve.wait_ge(ev.sem, e0 + 5 + c + 1)
                            else:
                                dve.wait_ge(dve_a.sem, z0 + 8 * (k - 1) + c + 1)
                            shifted = xbc[:, c, tap:tap + T]
                            if k == 0:
                                ins = dve.tensor_scalar(xbc_a[:, c, :], shifted, convw[:, tap, c:c + 1],
                                                        convb[:, c:c + 1], ALU.mult, ALU.add)
                            else:
                                ins = dve.scalar_tensor_tensor(xbc_a[:, c, :], shifted, convw[:, tap, c:c + 1],
                                                               xbc_a[:, c, :], ALU.mult, ALU.add)
                            ins.then_inc(dve_a.sem, 1)

        xs_tok = view(arena, 0, NT, T)
        xdt = view(arena, 2048, NT, T)
        merged_s = view(arena, 4128, NT, T)
        merged_a = view(arena, 4128 + 2048, NT, T)
        CB_AT = (0, 512, 896, 1152)
        TRI = 1280
        cb = view(xt_mem, 0, GROUPS, TRI)
        sel = view(rows, 0, HEADS, P)
        gate_c_tok = view(small, 96, NT, 64)
        gate_u_tok = view(small, 96 + 256, NT, 64)
        dskip = view(small, 620, HEADS)
        coef = small[0:64, 628:629]
        neg_c = view(small, 630, NT, HEADS)
        sumsq = view(small, 664, 32)

        def decay_stage():
            tmp = xt_mem[0:64, 3072:3584]
            l0, a0, d0 = loaded.take(32), act_a.take(6), dve_a.take(1)
            t0, b0, e0 = tr.take(5), pe_a.take(8), dve_b.take(8)
            with nc.Block() as block:
                @block.gpsimd
                def _(pool):
                    with nc.allow_non_contiguous_dma("one value per partition"):
                        pool.dma_start(coef[0:HEADS, :], a["a_log"][0].unsqueeze(1)).then_inc(loaded.sem, 16)
                    pool.memset(gates[64:P, :], 0.0)
                    pool.dma_start(dskip, a["d_skip"][0].partition_broadcast(P)).then_inc(loaded.sem, 16)
                    pool.wait_ge(loaded.sem, l0 + 32)

                @block.scalar
                def _(act):
                    link = Chain(act, act_chain)
                    act.wait_ge(loaded.sem, l0 + 32)
                    act.activation(coef[0:HEADS, :], coef[0:HEADS, :], ACT.Exp).then_inc(act_a.sem, 1)
                    link(act.activation(tmp, gate_u, ACT.Abs))
                    link(act.activation(tmp, tmp, ACT.Exp, scale=-1.0))
                    act.activation(tmp, tmp, ACT.Ln, bias=one_col[0:64, :]).then_inc(act_a.sem, 1)
                    for j in range(NT):
                        act.wait_ge(tr.sem, t0 + j + 1)
                        act.activation(xs_tok[:, j, :], ps[:, j, :], ACT.Copy).then_inc(act_a.sem, 1)

                @block.vector
                def _(dve):
                    link = Chain(dve, dve_chain)
                    dve.wait_ge(act_a.sem, a0 + 2)
                    link(dve.tensor_scalar(gate_u, gate_u, 0.0, None, ALU.max))
                    link(dve.tensor_tensor(gate_u, gate_u, tmp, ALU.add))
                    dve.tensor_scalar(tmp[32:64, :], gate_u[32:64, :], -1.0, None, ALU.mult)
                    link(dve.tensor_scalar(tmp[0:32, :], gate_u[0:32, :], -1.0, None, ALU.mult))
                    link(dve.tensor_scalar(tmp[0:HEADS, :], tmp[0:HEADS, :], coef[0:HEADS, :], None, ALU.mult))
                    dve.tensor_tensor_scan(gate_c, ones[0:64, 0:1].to_broadcast([64, T]), tmp, 0.0,
                                           ALU.mult, ALU.add).then_inc(dve_a.sem, 1)
                    dve.tensor_copy(sel, ident[:, 0:HEADS].unsqueeze(2).to_broadcast([P, HEADS, P]))
                    dve.wait_ge(tr.sem, t0 + 5)
                    dve.tensor_copy(gate_c_tok, ps[:, 4, 0:256].rearrange("p (j r) -> p j r", j=NT))
                    link(dve.tensor_copy(gate_u_tok, ps[:, 4, 256:512].rearrange("p (j r) -> p j r", j=NT)))
                    dve.tensor_scalar(neg_c, gate_c_tok[:, :, 0:HEADS], -1.0, None, ALU.mult)
                    for j in range(NT):
                        dve.wait_ge(act_a.sem, a0 + 3 + j)
                        dve.tensor_tensor(xdt[:, j, :].rearrange("p (h d) -> p h d", h=HEADS),
                                          xs_tok[:, j, :].rearrange("p (h d) -> p h d", h=HEADS),
                                          gate_u_tok[:, j, 0:HEADS].unsqueeze(2).to_broadcast([P, HEADS, HD]),
                                          ALU.mult)
                    for n in range(8):
                        g, i = n // 4, n % 4
                        dve.wait_ge(pe_a.sem, b0 + n + 1)
                        dve.tensor_copy(cb[:, g, CB_AT[i]:CB_AT[i] + T - i * P], ps[:, 5 + n % 3, 0:T - i * P])\
                           .then_inc(dve_b.sem, 1)

                @block.tensor
                def _(pe):
                    for j in range(NT):
                        for c in range(4):
                            ins = pe.transpose(ps[:, j, c * P:(c + 1) * P], xbc_a[:, c, j * P:(j + 1) * P], ident)
                        ins.then_inc(tr.sem, 1)
                    pe.wait_ge(dve_a.sem, d0 + 1)
                    for j in range(NT):
                        pe.transpose(ps[:, 4, j * 64:(j + 1) * 64], gate_c[:, j * P:(j + 1) * P], ident[0:64, 0:64])
                        ins = pe.transpose(ps[:, 4, 256 + j * 64:256 + (j + 1) * 64], gate_u[:, j * P:(j + 1) * P],
                                           ident[0:64, 0:64])
                    ins.then_inc(tr.sem, 1)
                    for n in range(8):
                        g, i = n // 4, n % 4
                        if n >= 3:
                            pe.wait_ge(dve_b.sem, e0 + n - 2)
                        pe.matmul(ps[:, 5 + n % 3, 0:T - i * P], xbc_a[:, 4 + g, i * P:(i + 1) * P],
                                  xbc_a[:, 6 + g, i * P:T], start=True, stop=True).then_inc(pe_a.sem, 1)

        def ssd_stage():
            eb = [view(xt_mem, 2 * TRI, TRI), view(arena, 4128 + 2048, TRI)]
            gnorm = rows[:, 2 * T:3 * T]
            l0 = loaded.take(16)
            m0, e0, g0 = pe_a.take(4 * HEADS), act_a.take(4 * HEADS + 2), dve_a.take(4 * HEADS)
            y0, d0 = pe_b.take(HEADS), dve_b.take(HEADS)
            k0 = dve_c.take(2)
            with nc.Block() as block:
                @block.gpsimd
                def _(pool):
                    pool.dma_start(gnorm, a["ssd_norm_g"][0].partition_broadcast(P)).then_inc(loaded.sem, 16)

                @block.tensor
                def _(pe):
                    def decays(h):
                        for i in range(NT):
                            n = 4 * h + i
                            if h >= 1:
                                pe.wait_ge(act_a.sem, e0 + n - 3)
                            w = T - i * P
                            d, row = sel[:, h, :], gates
                            pe.matmul(ps[:, i, 0:P], ident, mask_sq, start=True, stop=False)
                            ins = pe.matmul(ps[:, i, 0:P], d, row[:, i * P:(i + 1) * P], start=False, stop=True)
                            if w > P:
                                ins = pe.matmul(ps[:, i, P:w], d, row[:, (i + 1) * P:T], start=True, stop=True)
                            ins.then_inc(pe_a.sem, 1)

                    decays(0)
                    for h in range(HEADS):
                        if h + 1 < HEADS:
                            decays(h + 1)
                        pe.wait_ge(dve_a.sem, g0 + 4 * h + 4)
                        if h >= 2:
                            pe.wait_ge(dve_b.sem, d0 + h - 1)
                        for j in range(NT):
                            for i in range(j + 1):
                                at = CB_AT[i] + (j - i) * P
                                ins = pe.matmul(ps[:, 4 + h % 2, j * HD:(j + 1) * HD], eb[h % 2][:, at:at + P],
                                                xdt[:, i, h * HD:(h + 1) * HD], start=(i == 0), stop=(i == j))
                        ins.then_inc(pe_b.sem, 1)

                @block.scalar
                def _(act):
                    for h in range(HEADS):
                        if h >= 2:
                            act.wait_ge(pe_b.sem, y0 + h - 1)
                        for i in range(NT):
                            w = T - i * P
                            act.wait_ge(pe_a.sem, m0 + 4 * h + i + 1)
                            act.activation(eb[h % 2][:, CB_AT[i]:CB_AT[i] + w], ps[:, i, 0:w], ACT.Exp,
                                           bias=neg_c[:, i, h:h + 1]).then_inc(act_a.sem, 1)
                    act.wait_ge(dve_c.sem, k0 + 1)
                    for j in range(NT):
                        for g in range(GROUPS):
                            ins = act.activation(xdt[:, j, g * 256:(g + 1) * 256], merged_s[:, j, g * 256:(g + 1) * 256],
                                                 ACT.Square, accum_out=sumsq[:, 2 * j + g:2 * j + g + 1])
                    ins.then_inc(act_a.sem, 1)
                    act.wait_ge(dve_c.sem, k0 + 2)
                    act.activation(sumsq[:, 16:24], sumsq[:, 8:16], ACT.Sqrt).then_inc(act_a.sem, 1)

                @block.vector
                def _(dve):
                    link = Chain(dve, dve_chain)

                    def take_y(h):
                        dve.wait_ge(pe_b.sem, y0 + h + 1)
                        dve.scalar_tensor_tensor(merged_s[:, :, h * HD:(h + 1) * HD], xs_tok[:, :, h * HD:(h + 1) * HD],
                                                 dskip[:, h:h + 1],
                                                 ps[:, 4 + h % 2, 0:4 * HD].rearrange("p (j d) -> p j d", j=NT),
                                                 ALU.mult, ALU.add).then_inc(dve_b.sem, 1)

                    for h in range(HEADS):
                        g = h // (HEADS // GROUPS)
                        for i in range(NT):
                            dve.wait_ge(act_a.sem, e0 + 4 * h + i + 1)
                            e = eb[h % 2][:, CB_AT[i]:CB_AT[i] + T - i * P]
                            dve.tensor_tensor(e, e, cb[:, g, CB_AT[i]:CB_AT[i] + T - i * P], ALU.mult)\
                               .then_inc(dve_a.sem, 1)
                        if h >= 1:
                            take_y(h - 1)
                    take_y(HEADS - 1)
                    dve.wait_ge(dve_b.sem, d0 + HEADS)
                    for j in range(NT):
                        ins = dve.tensor_tensor(merged_s[:, j, :], merged_s[:, j, :], z_s[:, j, :], ALU.mult)
                    ins.then_inc(dve_c.sem, 1)
                    dve.wait_ge(act_a.sem, e0 + 4 * HEADS + 1)
                    dve.tensor_scalar(sumsq[:, 8:16], sumsq[:, 0:8], 1.0 / 256, RMS_EPS, ALU.mult, ALU.add)\
                       .then_inc(dve_c.sem, 1)
                    dve.wait_ge(act_a.sem, e0 + 4 * HEADS + 2)
                    link(dve.reciprocal(sumsq[:, 24:32], sumsq[:, 16:24]))
                    dve.wait_ge(loaded.sem, l0 + 16)
                    for j in range(NT):
                        for g in range(GROUPS):
                            y = merged_s[:, j, g * 256:(g + 1) * 256]
                            dve.scalar_tensor_tensor(y, y, sumsq[:, 24 + 2 * j + g:25 + 2 * j + g],
                                                     gnorm[:, g * 256:(g + 1) * 256], ALU.mult, ALU.mult)

        def attention_stage(n_comp, q, k, v, dv_head, put, lam=None, forget=False):
            jobs = HEADS * NT
            prob = [[view(xt_mem, (2 * b + c) * T, T) for c in range(2)] for b in range(2)]
            turned = [view(xt_mem, (4 + b) * T, T) for b in range(2)]
            DEEP = 8
            st = view(small, 696, DEEP, 8)
            m0, x0, e0 = pe_a.take(jobs * n_comp), dve_a.take(jobs * n_comp), act_a.take(jobs * n_comp)
            t0, c0, o0, d0 = tr.take(jobs), act_b.take(jobs), pe_b.take(jobs), dve_c.take(jobs)
            faded = [view(xt_mem, (2 * b + 1) * T, T) for b in range(2)]
            queries = [view(xt_mem, (6 + b) * T, T) for b in range(2)]
            f0, b0, p0 = (pe_c.take(HEADS), ev.take(HEADS), padded.take(HEADS)) if forget else (0, 0, 0)
            n0 = dve_b.take(jobs) if n_comp == 2 else 0
            s0 = dve_b.take(1) if forget else 0

            def width(n):
                return (n % NT + 1) * P

            def score(n, c):
                return ps[:, n_comp * (n % 2) + c, 0:width(n)]

            with nc.Block() as block:
                if forget:
                    zeros = view(arena, 8224, D)
                    z0 = consts.take(1)

                    @block.gpsimd
                    def _(pool):
                        link = Chain(pool, pool_chain)
                        link(pool.memset(queries[0][HD:P, :], 0.0))
                        for h in range(HEADS):
                            if h >= 2:
                                pool.wait_ge(pe_a.sem, m0 + NT * (h - 1))
                            if h == 1:
                                link(pool.memset(queries[1][0:HD, :], 0.0))
                            at = slice(h % 2 * HD, (h % 2 + 1) * HD)
                            pool.tensor_copy(queries[h % 2][at, :], q(h, 0)).then_inc(padded.sem, 1)
                            pool.wait_ge(padded.sem, p0 + h + 1)
                            if h == 1:
                                pool.memset(zeros, 0.0).then_inc(consts.sem, 1)

                    @block.sync
                    def _(sp):
                        sp.wait_ge(consts.sem, z0 + 1)
                        sp.dma_start(ybuf.rearrange("(r p) d -> p r d", p=P),
                                     zeros.unsqueeze(1).to_broadcast([P, ybuf.shape[0] // P, D])).then_inc(zeroed.sem, 16)
                        sp.wait_ge(zeroed.sem, zeroed.take(16) + 16)

                @block.tensor
                def _(pe):
                    def scores(n):
                        h, j = n // NT, n % NT
                        if n >= 2:
                            pe.wait_ge(act_a.sem, e0 + n_comp * (n - 1))
                        if forget and j == 0:
                            pe.wait_ge(padded.sem, p0 + h + 1)
                        for lo, hi in ((j * P, (j + 1) * P), (0, j * P))[0:1 + (j > 0)]:
                            parts = [score(n, c)[:, lo:hi] for c in range(n_comp)]
                            if lo == j * P:
                                for part in parts:
                                    pe.matmul(part, ident, mask_qk, start=True, stop=False)
                            for c, part in enumerate(parts):
                                qh = queries[h % 2] if forget else q(h, c)
                                ins = pe.matmul(part, qh[:, j * P:(j + 1) * P], k(h, c)[:, lo:hi],
                                                start=(lo != j * P), stop=True)
                                if lo == 0:
                                    ins.then_inc(pe_a.sem, 1)

                    def fade(h):
                        if h >= 2:
                            pe.wait_ge(ev.sem, b0 + h - 1)
                        pe.matmul(ps[:, 2 + h % 2, :], sel[:, h, :], gates, start=True, stop=True).then_inc(pe_c.sem, 1)

                    def turn(n):
                        if n_comp == 1:
                            pe.wait_ge(act_a.sem, e0 + n + 1)
                        else:
                            pe.wait_ge(dve_b.sem, n0 + n + 1)
                        if n >= 2:
                            pe.wait_ge(act_b.sem, c0 + n - 1)
                        for i in range(n % NT + 1):
                            ins = pe.transpose(ps[:, 4 + n % 2, i * P:(i + 1) * P],
                                               prob[n % 2][0][:, i * P:(i + 1) * P], ident)
                        ins.then_inc(tr.sem, 1)

                    def product(n):
                        h = n // NT
                        pe.wait_ge(act_b.sem, c0 + n + 1)
                        if n >= 2:
                            pe.wait_ge(dve_c.sem, d0 + n - 1)
                        for i in range(n % NT + 1):
                            ins = pe.matmul(ps[:, 6 + n % 2, 0:dv_head], turned[n % 2][:, i * P:(i + 1) * P],
                                            v[:, i, h * dv_head:(h + 1) * dv_head],
                                            start=(i == 0), stop=(i == n % NT))
                        ins.then_inc(pe_b.sem, 1)

                    if forget:
                        pe.wait_ge(dve_b.sem, s0 + 1)
                        fade(0)
                    for s in range(jobs + 3):
                        if s < jobs:
                            scores(s)
                            if forget and s % NT == 1 and s // NT + 1 < HEADS:
                                fade(s // NT + 1)
                        if 0 <= s - 2 < jobs:
                            turn(s - 2)
                        if 0 <= s - 3 < jobs:
                            product(s - 3)

                @block.scalar
                def _(act):
                    def take_faded(h):
                        act.wait_ge(pe_c.sem, f0 + h + 1)
                        act.activation(faded[h % 2], ps[:, 2 + h % 2, :], ACT.Copy).then_inc(ev.sem, 1)

                    if forget:
                        take_faded(0)
                    for s in range(jobs + 2):
                        if s < jobs:
                            for c in range(n_comp):
                                act.wait_ge(dve_a.sem, x0 + n_comp * s + c + 1)
                                if s >= 2:
                                    act.wait_ge(tr.sem, t0 + s - 1)
                                act.activation(prob[s % 2][c][:, 0:width(s)], score(s, c), ACT.Exp,
                                               bias=st[:, s % DEEP, 2 + c:3 + c], scale=SCALE,
                                               accum_out=st[:, s % DEEP, 4 + c:5 + c]).then_inc(act_a.sem, 1)
                            if forget and s % NT == 1 and s // NT + 1 < HEADS:
                                take_faded(s // NT + 1)
                        n = s - 2
                        if 0 <= n:
                            act.wait_ge(tr.sem, t0 + n + 1)
                            if n >= 2:
                                act.wait_ge(pe_b.sem, o0 + n - 1)
                            act.activation(turned[n % 2][:, 0:width(n)], ps[:, 4 + n % 2, 0:width(n)], ACT.Copy)\
                               .then_inc(act_b.sem, 1)

                @block.vector
                def _(dve):
                    link = Chain(dve, dve_chain)
                    if forget:
                        dve.tensor_scalar(sel, ident[:, F_ROW:F_ROW + HEADS].unsqueeze(2).to_broadcast([P, HEADS, P]),
                                          -1.0 / SCALE, None, ALU.mult).then_inc(dve_b.sem, 1)

                    def maxima(n):
                        m = st[:, n % DEEP, :]
                        for c in range(n_comp):
                            dve.wait_ge(pe_a.sem, m0 + n_comp * n + c + 1)
                            if forget:
                                if n % NT == 0:
                                    dve.wait_ge(ev.sem, b0 + n // NT + 1)
                                link(dve.tensor_tensor(score(n, c), score(n, c), faded[n // NT % 2][:, 0:width(n)], ALU.add))
                            link(dve.tensor_reduce(m[:, c:c + 1], score(n, c), AX, ALU.max))
                            dve.tensor_scalar(m[:, 2 + c:3 + c], m[:, c:c + 1], -SCALE, None, ALU.mult)\
                               .then_inc(dve_a.sem, 1)

                    def divide(n):
                        m = st[:, n % DEEP, :]
                        dve.wait_ge(act_a.sem, e0 + n_comp * (n + 1))
                        link(dve.reciprocal(m[:, 6:6 + n_comp], m[:, 4:4 + n_comp]))
                        if n_comp == 2:
                            p0, p1 = (p[:, 0:width(n)] for p in prob[n % 2])
                            link(dve.tensor_scalar(m[:, 7:8], m[:, 7:8], m[:, 4:5], lam, ALU.mult, ALU.mult))
                            dve.scalar_tensor_tensor(p0, p1, m[:, 7:8], p0, ALU.mult, ALU.subtract).then_inc(dve_b.sem, 1)

                    for s in range(jobs + 4):
                        if s < jobs:
                            maxima(s)
                        if 0 <= s - 1 < jobs:
                            divide(s - 1)
                        n = s - 4
                        if 0 <= n:
                            dve.wait_ge(pe_b.sem, o0 + n + 1)
                            dve.tensor_scalar(put(n // NT, n % NT), ps[:, 6 + n % 2, 0:dv_head], st[:, n % DEEP, 6:7],
                                              -1.0 if n_comp == 2 else 1.0, ALU.mult, ALU.mult).then_inc(dve_c.sem, 1)

        def moe_stage(l, alpha, g_src, b_src, last):
            E, EPG = n_experts[l], n_experts[l] // 4
            G = 4
            NR = G + E
            MAXB = 2 * T // BLK + E
            at = [0]

            def take(*shape, dt=F32):
                v = view(arena, at[0], *shape)
                at[0] += int(np.prod(shape))
                return v.bitcast(dt) if dt != F32 else v

            logits, expo, pen = take(NT, NR), take(NT, G), take(NT, G)
            gmax, gsum, m1, m2 = take(NT), take(NT), take(NT), take(NT)
            iota_g, iota_e = take(G), take(E)
            first, pick_g = take(NT), take(NT, G)
            es, es2 = take(NT, E), take(NT, E)
            pick1, pick2, pick = take(NT, E), take(NT, E), take(NT, E)
            w1, w2, ratio = take(NT), take(NT), take(NT)
            count_i, count_s = take(E, dt=I32), take(E, dt=I32)
            nblk, ends, starts = take(E), take(E), take(E)
            table = take(E + 3, dt=I32)
            pos = take(NT, E)
            slots = take(2, NT)
            slots_i = take(2, NT, dt=U32)
            slots_now = take(2, NT)
            hit1, hit2, hit = take(NT, BLK), take(NT, BLK), take(NT, BLK)
            x_rows, xg = take(2, P), take(NK, BLK)
            silu_g, hidden, hT = take(P), take(P), take(P)
            y_sb = take(2, D // 4)
            total_i = take(2, dt=I32)
            third = at[0]
            y1, y2 = take(NT, D), take(NT, D)
            assert at[0] <= 16448

            def bc(v, n):
                return v.unsqueeze(2).to_broadcast([P, v.shape[1], n])

            def mid(v, n):
                return v.unsqueeze(1).to_broadcast([P, n, v.shape[1]])

            m0, d0, a0 = mm.take(1), dve_a.take(3), act_a.take(2)
            ready = consts.take(1)
            with nc.Block() as block:
                @block.gpsimd
                def _(pool):
                    pool.iota(iota_g, pattern=[[1, G]], base=0, channel_multiplier=0, allow_small_or_imprecise_dtypes=True)
                    pool.iota(iota_e, pattern=[[1, E]], base=0, channel_multiplier=0, allow_small_or_imprecise_dtypes=True)
                    pool.memset(table, 0).then_inc(consts.sem, 1)

                @block.tensor
                def _(pe):
                    pe.wait_ge(dve_a.sem, d0 + 3)
                    for j in range(NT):
                        for i in range(j + 1):
                            pe.matmul(ps[:, 1, j * E:(j + 1) * E], before if i == j else ones, pick[:, i, :],
                                      start=(i == 0), stop=(i == j))
                    for i in range(NT):
                        ins = pe.matmul(ps[:, 3, 0:E], ones, pick[:, i, :], start=(i == 0), stop=(i == NT - 1))
                    ins.then_inc(mm.sem, 1)

                @block.scalar
                def _(act):
                    act.wait_ge(dve_a.sem, d0 + 1)
                    act.activation(expo, expo, ACT.Exp).then_inc(act_a.sem, 1)
                    act.wait_ge(dve_a.sem, d0 + 2)
                    act.activation(ratio, ratio, ACT.Exp).then_inc(act_a.sem, 1)

                @block.vector
                def _(dve):
                    link = Chain(dve, dve_chain)

                    def pick_max(dst, tmp, x, m, iota, n):
                        link(dve.tensor_reduce(m, x, AX, ALU.max))
                        link(dve.tensor_tensor(tmp, x, bc(m, n), ALU.is_equal))
                        link(dve.scalar_tensor_tensor(tmp, tmp, -1000.0, mid(iota, NT), ALU.mult, ALU.add))
                        link(dve.tensor_reduce(first, tmp, AX, ALU.min))
                        link(dve.tensor_tensor(dst, tmp, bc(first, n), ALU.is_equal))

                    dve.wait_ge(consts.sem, ready + 1)
                    link(dve.tensor_copy(logits, ps[:, 0:2 * NT:2, 0:NR]))
                    gl, el = logits[:, :, 0:G], logits[:, :, G:NR]
                    pick_max(pick_g, pen, gl, gmax, iota_g, G)
                    dve.tensor_tensor(expo, gl, bc(gmax, G), ALU.subtract).then_inc(dve_a.sem, 1)
                    link(dve.tensor_scalar(pen, pick_g, -NEG, NEG, ALU.mult, ALU.add))
                    link(dve.tensor_tensor(es.rearrange("p j (g e) -> p j g e", g=G),
                                           el.rearrange("p j (g e) -> p j g e", g=G),
                                           pen.unsqueeze(3).to_broadcast([P, NT, G, EPG]), ALU.add))
                    pick_max(pick1, es2, es, m1, iota_e, E)
                    link(dve.scalar_tensor_tensor(es, pick1, 2 * NEG, es, ALU.mult, ALU.add))
                    pick_max(pick2, es2, es, m2, iota_e, E)
                    dve.tensor_tensor(ratio, m2, m1, ALU.subtract).then_inc(dve_a.sem, 1)
                    dve.tensor_tensor(pick, pick1, pick2, ALU.add).then_inc(dve_a.sem, 1)
                    dve.wait_ge(act_a.sem, a0 + 2)
                    link(dve.tensor_reduce(gsum, expo, AX, ALU.add))
                    link(dve.tensor_scalar(w2, ratio, 1.0, None, ALU.add))
                    link(dve.tensor_tensor(w1, gsum, w2, ALU.mult))
                    link(dve.reciprocal(w1, w1))
                    dve.tensor_tensor(w2, w1, ratio, ALU.mult)
                    dve.wait_ge(mm.sem, m0 + 1)
                    link(dve.tensor_scalar(count_i, ps[:, 3, 0:E], float(BLK - 1), None, ALU.add))
                    link(dve.tensor_scalar(count_s, count_i, BLK.bit_length() - 1, None, ALU.arith_shift_right))
                    link(dve.tensor_scalar(nblk, count_s, 1.0, None, ALU.max))
                    link(dve.tensor_tensor_scan(ends, ones[:, 0:E], nblk, 0.0, ALU.mult, ALU.add))
                    link(dve.tensor_tensor(starts, ends, nblk, ALU.subtract))
                    link(dve.tensor_scalar(total_i[:, 0:1], ends[:, E - 1:E], 1.0, None, ALU.add))
                    link(dve.tensor_scalar(total_i[:, 1:2], total_i[:, 0:1], 1, None, ALU.arith_shift_right))
                    link(dve.tensor_copy(table[:, 1:E], ends[:, 0:E - 1]))
                    for n in (E, E + 1):
                        dve.tensor_scalar(table[:, n:n + 1], total_i[:, 1:2], 2.0, None, ALU.mult)
                    dve.tensor_copy(table[:, E + 2:E + 3], total_i[:, 1:2])
                    link(dve.scalar_tensor_tensor(pos, mid(starts, NT), float(BLK),
                                                  ps[:, 1, 0:NT * E].rearrange("p (j e) -> p j e", j=NT),
                                                  ALU.mult, ALU.add))
                    for n, pk in enumerate((pick1, pick2)):
                        link(dve.tensor_tensor(es, pos, pk, ALU.mult))
                        link(dve.tensor_reduce(slots[:, n, :], es, AX, ALU.add))
                    dve.tensor_copy(slots_i, slots)
                    dve.tensor_copy(slots_now, slots)
                    dve.memset(y_sb, 0.0)

            s_hit, s_got, s_rows, s_turned, s_xg, s_gu, s_silu, s_h, s_hturned, s_hT, s_down, s_y, s_even, s_odd, s_slots = (
                signal(f"{n}{l}").sem for n in (
                    "selection_ready", "gathered", "rows_taken", "inputs_turned", "inputs_ready", "gate_up_done", "silu_ready",
                    "hidden_ready", "hidden_turned", "hidden_taken", "down_done", "rows_ready", "even_rows_stored", "odd_rows_stored", "slots_moved"))
            s_stored = (s_even, s_odd)
            c0 = moe_at[l]
            quarters = [slice(q * BLK, (q + 1) * BLK) for q in range(4)]
            W = D // 4
            third_at = [arena[:, third:third + NK * CH], arena[:, third + NK * CH:third + 2 * NK * CH], xt_mem[:, :]]

            def value(eng, n, low=1, high=MAXB):
                return eng.value_load(table[0:1, n], min_val=low, max_val=high)

            def rows_at(g):
                return ybuf[bass.ds(g * BLK, BLK), :].rearrange("r (q n) -> q r n", q=4)

            with nc.Block() as block:
                @block.sync
                def _(sp):
                    def load_third(e):
                        for kind in range(3):
                            src = expert_src(l, e, kind)
                            sp.dma_start(third_at[kind].rearrange("p (k n) -> p k n", k=src.shape[1]), src)\
                              .then_inc(arrived_x[kind].sem, 16)

                    def follow(i, q):
                        sp.wait_ge(s_down, value(sp, bass.ds(3 * i + q + 1, 1)))
                        if q == 2:
                            load_third(3 * i + q + 3)
                        else:
                            for j in range(3):
                                load_expert_chunk(sp, l, 3 * i + q + 3, j, c0 + 3 * q + j)

                    load_third(2)
                    with sp.Fori(0, (E - 3) // 3) as i:
                        for q in range(3):
                            follow(i, q)
                    for q in range((E - 3) % 3):
                        follow((E - 3) // 3, q)
                    if l < 2:
                        for n in range(mixer_at[l + 1], mixer_at[l + 1] + 3):
                            k = (n - SLOTS - c0) // 3
                            e = 3 * (k // 2) + k % 2
                            sp.wait_ge(s_down, value(sp, slice(e + 1, e + 2)))
                            load_chunk(sp, n)

                @block.tensor
                def _(pe):
                    def gather():
                        for j in range(NT):
                            for q, at in enumerate(quarters):
                                ins = pe.matmul(ps[at, 0, 0:W], hit[:, j, :],
                                                x_tok[:, j, :].rearrange("p (h q c) -> p h q c", h=2, q=4)[:, :, q, :],
                                                start=(j == 0), stop=(j == NT - 1))
                        ins.then_inc(s_got, 1)

                    def turn_inputs():
                        for h in range(2):
                            ins = pe.transpose(ps[:, 1, h * P:(h + 1) * P], x_rows[:, h, :], ident)
                        ins.then_inc(s_turned, 1)

                    pe.wait_ge(s_hit, 1)
                    gather()
                    pe.wait_ge(s_rows, 1)
                    turn_inputs()
                    def expert(i, q):
                        if q < 2:
                            first_chunk = c0 + 3 * q
                            sg, sd = (first_chunk + kinds(first_chunk).index(kind) for kind in (0, 2))
                            gu_mem = ring[:, sg % SLOTS * NK * CH:(sg % SLOTS + 2) * NK * CH]
                            d_mem = slot(sd % SLOTS)
                            there = [(arrived[n % SLOTS].sem, i * 16 + 16 * (n // SLOTS + 1))
                                     for n in range(first_chunk, first_chunk + 3)]
                        else:
                            gu_mem, d_mem = arena[:, third:third + 2 * NK * CH], third_at[2]
                            there = [(x.sem, i * 16 + 16 * (x.total // 16 + 1)) for x in arrived_x]
                        w_gu = gu_mem.rearrange("p (w k n) -> p w k n", w=2, k=NK)
                        wd = d_mem.rearrange("p (k n) -> p k n", k=NT)
                        start, end = value(pe, bass.ds(3 * i + q, 1), 0), value(pe, bass.ds(3 * i + q + 1, 1))
                        with pe.Fori(start, end) as g:
                            for chunk in there:
                                pe.wait_ge(*chunk)
                            pe.wait_ge(s_xg, g + 1)
                            for k in range(NK):
                                for q, at in enumerate(quarters):
                                    ins = pe.matmul(ps[at, 2, 0:W], xg[:, k, :], w_gu[:, :, k, q * P:(q + 1) * P],
                                                    start=(k == 0), stop=(k == NK - 1))
                            ins.then_inc(s_gu, 1)
                            pe.wait_ge(s_hit, g + 2)
                            gather()
                            pe.wait_ge(s_h, g + 1)
                            pe.transpose(ps[:, 3, 0:P], hidden, ident).then_inc(s_hturned, 1)
                            pe.wait_ge(s_rows, g + 2)
                            turn_inputs()
                            pe.wait_ge(s_hT, g + 1)
                            pe.wait_ge(s_y, g + 1)
                            for f in range(NT):
                                for q, at in enumerate(quarters):
                                    ins = pe.matmul(ps[at, 4, 0:W], hT[:, f * BLK:(f + 1) * BLK], wd[:, f, q * W:(q + 1) * W],
                                                    start=(f == 0), stop=(f == NT - 1))
                            ins.then_inc(s_down, 1)

                    with pe.Fori(0, E // 3) as i:
                        for q in range(3):
                            expert(i, q)
                    for q in range(E % 3):
                        expert(E // 3, q)

                @block.scalar
                def _(act):
                    def take_rows():
                        act.activation(x_rows, ps[:, 0, 0:W].rearrange("p (h c) -> p h c", h=2), ACT.Copy).then_inc(s_rows, 1)

                    for b in range(2):
                        act.dma_start(rows_at(b), y_sb[:, b, :]).then_inc(s_stored[b], 16)
                    pairs = value(act, slice(E + 2, E + 3), high=MAXB // 2)
                    act.wait_ge(s_got, 1)
                    take_rows()
                    with act.Fori(0, pairs) as p:
                        for b in range(2):
                            g = 2 * p + b
                            act.wait_ge(s_gu, g + 1)
                            act.activation(silu_g, ps[:, 2, 0:P], ACT.Silu).then_inc(s_silu, 1)
                            act.wait_ge(s_got, g + 2)
                            take_rows()
                            act.wait_ge(s_y, g + 2)
                            act.dma_start(rows_at(g), y_sb[:, b, :]).then_inc(s_stored[b], 16)
                    for b in range(2):
                        act.wait_ge(s_stored[b], pairs * 16 + 16)
                    act.activation(spot, eps_ln, ACT.Copy)

                @block.vector
                def _(dve):
                    def select(g):
                        dve.tensor_tensor(hit1, mid(iota_f, NT), bc(slots_now[:, 0, :], BLK), ALU.is_equal)
                        dve.tensor_tensor(hit2, mid(iota_f, NT), bc(slots_now[:, 1, :], BLK), ALU.is_equal).then_inc(s_slots, 1)
                        dve.wait_ge(s_slots, g * 2 + 1)
                        dve.tensor_tensor(hit, hit1, hit2, ALU.add).then_inc(s_hit, 1)
                        dve.tensor_scalar(slots_now, slots_now, float(BLK), None, ALU.subtract).then_inc(s_slots, 1)
                        dve.wait_ge(s_slots, g * 2 + 2)

                    def take_inputs():
                        dve.tensor_copy(xg.rearrange("p k s -> p (k s)"), ps[:, 1, 0:W]).then_inc(s_xg, 1)

                    pairs = value(dve, slice(E + 2, E + 3), high=MAXB // 2)
                    dve.memset(spot, 0.0).then_inc(s_y, 1)
                    select(0)
                    dve.wait_ge(s_turned, 1)
                    take_inputs()
                    with dve.Fori(0, pairs) as p:
                        for b in range(2):
                            g = 2 * p + b
                            dve.wait_ge(s_got, g + 1)
                            select(g + 1)
                            dve.wait_ge(s_silu, g + 1)
                            dve.tensor_tensor(hidden, silu_g, ps[:, 2, P:2 * P], ALU.mult).then_inc(s_h, 1)
                            dve.wait_ge(s_hturned, g + 1)
                            dve.tensor_copy(hT, ps[:, 3, 0:P]).then_inc(s_hT, 1)
                            dve.wait_ge(s_turned, g + 2)
                            take_inputs()
                            dve.wait_ge(s_down, g + 1)
                            dve.wait_ge(s_stored[b], p * 16 + 16)
                            dve.tensor_copy(y_sb[:, b, :], ps[:, 4, 0:W]).then_inc(s_y, 1)
            for x in arrived_x:
                x.take(16 * (E // 3))

            r0, l1, x0, n0 = loaded.take(32), [r.take(32) for r in rows_in], act_a.take(NT), norm_bases(not last)
            o0 = stored.take(16 * NT) if last else 0
            with nc.Block() as block:
                @block.sync
                def _(sp):
                    if not last:
                        for j in range(NT):
                            sp.wait_ge(rows_in[j].sem, l1[j] + 32)
                        for n in range(mixer_at[l + 1] + 3, mixer_at[l + 1] + SLOTS):
                            load_chunk(sp, n)
                    else:
                        for j in range(NT):
                            wait_tile(sp, j, n0)
                            sp.dma_start(out[0, j * P:(j + 1) * P, :], x_tok[:, j, :]).then_inc(stored.sem, 16)
                        sp.wait_ge(stored.sem, o0 + 16 * NT)

                @block.gpsimd
                def _(pool):
                    for j in range(NT):
                        for n, y in enumerate((y1, y2)):
                            pool.indirect_dma_start(out=y[:, j, :], out_offset=None, in_=ybuf,
                                                    in_offset=bass.IndirectOffsetOnAxis(ap=slots_i[:, n, j:j + 1], axis=0))\
                                .then_inc(rows_in[j].sem, 16)
                        if j == 0:
                            load_norm_rows(pool, g_src, b_src)
                    shift_tiles(pool, n0)

                @block.scalar
                def _(act):
                    for j in range(NT):
                        act.activation(x_tok[:, j, :], x_tok[:, j, :], ACT.Copy, scale=alpha).then_inc(act_a.sem, 1)
                    for j in range(NT):
                        deviation(act, j, n0)
                        if j >= 2 and not last:
                            take_tile(act, j - 2, n0)
                    if not last:
                        for j in range(NT - 2, NT):
                            take_tile(act, j, n0)

                @block.vector
                def _(dve):
                    link = Chain(dve, dve_chain)

                    def update(j):
                        xj = x_tok[:, j, :]
                        dve.wait_ge(act_a.sem, x0 + j + 1)
                        dve.wait_ge(rows_in[j].sem, l1[j] + 32)
                        link(dve.scalar_tensor_tensor(xj, y1[:, j, :], w1[:, j:j + 1], xj, ALU.mult, ALU.add))
                        link(dve.scalar_tensor_tensor(xj, y2[:, j, :], w2[:, j:j + 1], xj, ALU.mult, ALU.add))
                        if j == 0:
                            dve.wait_ge(loaded.sem, r0 + 32)

                    norm_tiles(dve, link, update, n0)

                if not last:
                    @block.tensor
                    def _(pe):
                        for j in range(NT):
                            turn_tile(pe, j, n0)

        q2 = view(arena, 0, DA_HEADS, T)
        k2 = view(arena, NK * T, DA_HEADS, T)
        v2 = view(arena, 2 * NK * T, NT, D)
        o2 = view(arena, 3 * NK * T, NT, D)
        lam = cols[:, 8:9]
        lam_rows = rows[:, 0:256].rearrange("p (n d) -> p n d", n=4)
        subln = rows[:, 256:256 + P]

        def qkv_stage():
            first = mixer_at[1]
            m0, e0, l0 = mm.take(24), ev.take(24), loaded.take(32)
            for c in range(6):
                used[first + c] = (mm.sem, m0 + 4 * (c + 1))
            prods = view(rows, 512, 2, HD)
            sums = cols[:, 16:18]
            x0, a0 = dve_a.take(1), act_a.take(1)
            with nc.Block() as block:
                @block.sync
                def _(sp):
                    stream_mixer(sp, first + SLOTS, first + 12)

                @block.gpsimd
                def _(pool):
                    pool.dma_start(lam_rows, a["attn_lambda_2"][0].partition_broadcast(P)).then_inc(loaded.sem, 16)
                    pool.dma_start(subln, a["attn_subln_g_2"][0].partition_broadcast(P)).then_inc(loaded.sem, 16)

                @block.tensor
                def _(pe):
                    for n in range(24):
                        c, j = n // 4, n % 4
                        if n >= 8:
                            pe.wait_ge(ev.sem, e0 + n - 7)
                        if j == 0:
                            wait_chunk(pe, first + c)
                        w = slot((first + c) % SLOTS).rearrange("p (k n) -> p k n", k=NK)
                        for k in range(NK):
                            wj, xj = w[:, k, :], xT[:, k, :]
                            if c < 4:
                                wj = w[:, k, j * P:(j + 1) * P]
                            else:
                                xj = xT[:, k, j * P:(j + 1) * P]
                            lhs, rhs = (wj, xj) if c < 4 else (xj, wj)
                            ins = pe.matmul(ps[:, n % 8, :], lhs, rhs, start=(k == 0), stop=(k == NK - 1))
                        ins.then_inc(mm.sem, 1)

                @block.scalar
                def _(act):
                    act.wait_ge(dve_a.sem, x0 + 1)
                    act.activation(sums, sums, ACT.Exp).then_inc(act_a.sem, 1)
                    for n in range(24):
                        c, j = n // 4, n % 4
                        act.wait_ge(mm.sem, m0 + n + 1)
                        dst = (q2, k2)[c // 2][:, 4 * (c % 2) + j, :] if c < 4 else v2[:, j, (c - 4) * CH:(c - 3) * CH]
                        act.activation(dst, ps[:, n % 8, :], ACT.Copy).then_inc(ev.sem, 1)

                @block.vector
                def _(dve):
                    link = Chain(dve, dve_chain)
                    dve.wait_ge(loaded.sem, l0 + 32)
                    link(dve.tensor_tensor(prods, lam_rows[:, 0:4:2, :], lam_rows[:, 1:4:2, :], ALU.mult))
                    dve.tensor_reduce(sums, prods, AX, ALU.add).then_inc(dve_a.sem, 1)
                    dve.wait_ge(act_a.sem, a0 + 1)
                    link(dve.tensor_tensor(lam, sums[:, 0:1], sums[:, 1:2], ALU.subtract))
                    dve.tensor_scalar(lam, lam, LAMBDA_INIT, None, ALU.add)

        def subln_stage():
            squares = view(xt_mem, 0, NT, D)
            ms = cols[:, 16:48]
            x0, a0 = dve_a.take(1), act_a.take(1)
            heads = "p j (h d) -> p (j h) d"
            with nc.Block() as block:
                @block.scalar
                def _(act):
                    act.wait_ge(dve_a.sem, x0 + 1)
                    act.activation(ms, ms, ACT.Sqrt).then_inc(act_a.sem, 1)

                @block.vector
                def _(dve):
                    link = Chain(dve, dve_chain)
                    o = o2.rearrange(heads, h=DA_HEADS)
                    link(dve.tensor_tensor(squares, o2, o2, ALU.mult))
                    link(dve.tensor_reduce(ms, squares.rearrange(heads, h=DA_HEADS), AX, ALU.add))
                    dve.tensor_scalar(ms, ms, 1.0 / P, RMS_EPS, ALU.mult, ALU.add).then_inc(dve_a.sem, 1)
                    link(dve.tensor_scalar(subln, subln, 1.0 - LAMBDA_INIT, None, ALU.mult))
                    dve.wait_ge(act_a.sem, a0 + 1)
                    link(dve.reciprocal(ms, ms))
                    link(dve.tensor_tensor(o, o, ms.unsqueeze(2).to_broadcast([P, 32, P]), ALU.mult))
                    dve.tensor_tensor(o, o, subln.unsqueeze(1).to_broadcast([P, 32, P]), ALU.mult)

        rT = view(arena, 0, NK, T)
        k3 = view(arena, NK * T, NK, T)
        v3 = view(arena, 2 * NK * T, NT, D)
        w2a2 = rows[:, 0:D]
        h_wa = rows[:, D:D + T]
        h_g = rows[:, D + T:D + 2 * T]
        h_g2 = small[0:GATE_LORA - P, 40:40 + T]
        N_PAR = 5
        K_K, K_A, R_K, W0, A0 = range(N_PAR)
        par = view(small, 552, N_PAR, NK)
        same_head = small[:, 592:720]

        def rkv_stage():
            first = mixer_at[2]
            mixes = {"w": 3, "a": 4, "g": 5, "r": 0, "k": 1, "v": 2}
            xx = view(arena, 3 * NK * T, NK, T)
            buf = {"w": view(arena, 2 * NK * T, NK, T), "a": k3}
            buf.update(g=buf["w"], r=buf["a"], k=buf["w"], v=xx)
            w1 = view(arena, 0, NK, DECAY_LORA)
            a1 = view(arena, 512, NK, AAA_LORA)
            g1 = view(arena, 1024, NK, GATE_LORA)
            mu = view(arena, 4 * NK * T, 6, NK)
            jobs = ["w", "a", "g", "g2"] + [(n, c, j) for n in "rkv" for c in range(2) for j in range(4)]
            param_rows = rows[:, D + T:D + T + P]
            m0, e0, l0, t0 = mm.take(28), ev.take(28), mixer_params.take(16 * 11), tr.take(1)
            x0, c0 = dve_a.take(6), consts.take(3)
            for c in range(6):
                used[first + c] = (mm.sem, m0 + 4 + 4 * (c + 1))
            with nc.Block() as block:
                @block.sync
                def _(sp):
                    stream_mixer(sp, first + SLOTS, first + 8)

                @block.gpsimd
                def _(pool):
                    link = Chain(pool, pool_chain)
                    link(pool.memset(param_rows, 0.0))
                    pool.tensor_copy(spot, one_col).then_inc(consts.sem, 1)
                    link(pool.memset(same_head, 0.0))
                    pool.memset(same_head[0:HD, 0:HD], 1.0)
                    pool.memset(same_head[HD:P, HD:P], 1.0).then_inc(consts.sem, 1)

                @block.vector
                def _(dve):
                    link = Chain(dve, dve_chain)
                    dve.tensor_tensor(xx[:, :, 1:T], xT[:, :, 0:T - 1], xT[:, :, 1:T], ALU.subtract)
                    link(dve.tensor_scalar(xx[:, :, 0:1], xT[:, :, 0:1], -1.0, None, ALU.mult))
                    dve.wait_ge(consts.sem, c0 + 3)
                    for n, name in enumerate(mixes):
                        if name in "grk":
                            dve.wait_ge(mm.sem, m0 + {"g": 1, "r": 2, "k": 4}[name])
                        for k in range(NK):
                            ins = dve.scalar_tensor_tensor(buf[name][:, k, :], xx[:, k, :], mu[:, mixes[name], k:k + 1],
                                                           xT[:, k, :], ALU.mult, ALU.add)
                        ins.then_inc(dve_a.sem, 1)

                @block.tensor
                def _(pe):
                    pe.wait_ge(mixer_params.sem, l0 + 16 * 11)
                    pe.transpose(ps[:, 7, 0:P], param_rows, ident).then_inc(tr.sem, 1)
                    order = list(mixes)
                    for n, job in enumerate(jobs):
                        if n >= 8:
                            pe.wait_ge(ev.sem, e0 + n - 7)
                        bank = ps[:, n % 8, :]
                        name = job[0]
                        pe.wait_ge(dve_a.sem, x0 + order.index(name) + 1)
                        xm = buf[name]
                        if n < 4:
                            w, o = ((w1, bank[0:64, :]), (a1, bank[64:128, :]),
                                    (g1[:, :, 0:P], bank), (g1[:, :, P:GATE_LORA], bank[0:GATE_LORA - P, :]))[n]
                            for k in range(NK):
                                ins = pe.matmul(o, w[:, k, :], xm[:, k, :], start=(k == 0), stop=(k == NK - 1))
                        else:
                            _, c, j = job
                            ch = first + 2 * "rkv".index(name) + c
                            if j == 0:
                                wait_chunk(pe, ch)
                            w = slot(ch % SLOTS).rearrange("p (k n) -> p k n", k=NK)
                            for k in range(NK):
                                if name == "v":
                                    ins = pe.matmul(bank, xm[:, k, j * P:(j + 1) * P], w[:, k, :],
                                                    start=(k == 0), stop=(k == NK - 1))
                                else:
                                    ins = pe.matmul(bank, w[:, k, j * P:(j + 1) * P], xm[:, k, :],
                                                    start=(k == 0), stop=(k == NK - 1))
                        ins.then_inc(mm.sem, 1)

                @block.scalar
                def _(act):
                    def load(dst, src):
                        act.dma_start(dst, src).then_inc(mixer_params.sem, 16)

                    act.wait_ge(consts.sem, c0 + 1)
                    load(param_rows[0:6 * NK, :], a["rw_mu_2"][0].rearrange("n (k p) -> (n k) p", p=P))
                    r_k = a["rw_r_k_2"][0].rearrange("h n -> (h n)")
                    for n, src in ((K_K, a["rw_k_k_2"][0]), (K_A, a["rw_k_a_2"][0]), (W0, a["rw_w0_2"][0]),
                                   (A0, a["rw_a0_2"][0]), (R_K, r_k)):
                        load(param_rows[(6 + n) * NK:(7 + n) * NK, :], src.rearrange("(k p) -> k p", p=P))
                    load(w1, a["rw_w1_2"][0].rearrange("(k p) n -> p k n", p=P))
                    load(a1, a["rw_a1_2"][0].rearrange("(k p) n -> p k n", p=P))
                    load(g1, a["rw_g1_2"][0].rearrange("(k p) n -> p k n", p=P))
                    load(w2a2[0:64, :], a["rw_w2_2"][0])
                    load(w2a2[64:128, :], a["rw_a2_2"][0])
                    act.wait_ge(tr.sem, t0 + 1)
                    act.activation(mu, ps[:, 7, 0:6 * NK].rearrange("p (n k) -> p n k", n=6), ACT.Copy)
                    act.activation(par, ps[:, 7, 6 * NK:(6 + N_PAR) * NK].rearrange("p (n k) -> p n k", n=N_PAR), ACT.Copy)\
                       .then_inc(consts.sem, 1)
                    for n, job in enumerate(jobs):
                        act.wait_ge(mm.sem, m0 + n + 1)
                        bank = ps[:, n % 8, :]
                        if n < 4:
                            dst, src, f = ((h_wa[0:64, :], bank[0:64, :], ACT.Tanh), (h_wa[64:128, :], bank[64:128, :], ACT.Copy),
                                           (h_g, bank, ACT.Sigmoid), (h_g2, bank[0:GATE_LORA - P, :], ACT.Sigmoid))[n]
                        else:
                            name, c, j = job
                            src, f = bank, ACT.Copy
                            dst = v3[:, j, c * CH:(c + 1) * CH] if name == "v" else (rT if name == "r" else k3)[:, 4 * c + j, :]
                        act.activation(dst, src, f).then_inc(ev.sem, 1)

        def wkv_stage():
            first = mixer_at[2]
            mem = [slot((first + 2 + n) % SLOTS) for n in range(4)]
            logd, lr, cum, before_d, inv, decay, kk, norm = (view(mem[0], n * T, T) for n in range(8))
            XX = view(mem[1], 0, 8, 2 * P)
            TT = view(mem[1], 16 * P, 8, P)
            QC = view(mem[1], 24 * P, 8, P)
            Z = view(mem[2], 0, 8, P)
            MT = view(mem[2], 8 * P, NC_R, P)
            NN = view(mem[2], 16 * P, NC_R, HD)
            S = view(mem[2], 20 * P, NC_R, HD)
            Y0 = view(mem[2], 24 * P, NT, 2, HD)
            AKM = view(mem[3], 0, 8, 4 * P)
            spare = 3 * NK * T
            keep, rkr, RQ = (view(arena, spare + n * T, T) for n in range(3))
            RH = view(arena, spare + 3 * T, 8, P)
            lora2 = view(arena, spare + 5 * T, 2, P)
            BZ = [view(arena, spare + 5 * T + 2 * P + e * T, T) for e in range(2)]
            KZ = [view(xt_mem, 7 * T, T), view(mem[2], 28 * P, T)]
            tile4 = "p (j t) -> p j t"
            AR = view(xt_mem, 0, NT, 2, P)
            A_T, R_T = AR[:, :, 0, :], AR[:, :, 1, :]
            B_T, K_T = view(xt_mem, 2 * T, T), view(xt_mem, 3 * T, T)
            B_tok, K_tok, V = (view(xt_mem, n * T, NT, P) for n in (4, 5, 6))
            low_st_d = mask_sq
            masks = cst[:, 6 * P:8 * P]
            pcol = cols[:, 16:16 + N_PAR]
            p_end = cols[:, 24:24 + NC_R]
            heads = view(cols, 33, NT, 2)
            TURNED = (0, 2, 6, 7)
            strip = slice(3 * P, 4 * P)
            units = [(e, j) for e in range(2) for j in range(NT)]
            ROUNDS = RB.bit_length() - 2
            assert RC == 2 * RB
            names = ("lora2", "heads_apart", "first_lora", "lora", "par", "sig", "sq", "shift", "first_sums", "ssq", "exp", "inverse",
                     "first_wide", "ops", "turned", "tok", "val", "low", "lowm", "q", "qc", "qc2", "z", "zc", "zc2", "q2", "q2c", "r2", "r2c", "y0", "y0c", "mn", "mnc", "yy", "yc")
            E = {n: signal(f"wkv_{n}").sem for n in names}
            p_akm, d_low, d_akm, p_sq, a_sq, p_tt, d_tt = (signal(f"wkv_{n}").sem for n in (
                "products", "low_masked", "masked", "squared", "squares_taken", "t_products", "t_added"))
            p_s, d_s = signal("wkv_state_product").sem, signal("wkv_state").sem
            chain_v = signal("wkv_dve_chain").sem
            PREPARE_LINKS, TURN_LINKS = 11, 13

            class LoopChain:

                def __init__(self, eng, sem, base, turn, n):
                    self.eng, self.sem, self.base, self.turn, self.n, self.at = eng, sem, base, turn, n, 0

                def __call__(self, ins):
                    self.at += 1
                    ins.then_inc(self.sem, 1)
                    self.eng.wait_ge(self.sem, self.turn * self.n + self.base + self.at)

            def rows_of(e):
                return slice(e * HD, (e + 1) * HD)

            def tile_of(mem3, n):
                return mem3[:, bass.ds(n, 1), :].rearrange("p o t -> p (o t)")

            def turns(eng, turn):
                with eng.Fori(0, NK - 1) as i:
                    turn(i, True)
                turn(NK - 1, False)

            with nc.Block() as block:
                @block.gpsimd
                def _(pool):
                    def take_lora2(n):
                        for e in range(2):
                            ins = pool.tensor_tensor(lora2[:, e, :], w2a2[:, bass.ds(n * P, P)],
                                                     same_head[:, e * HD:e * HD + 1].to_broadcast([P, P]), ALU.mult)
                        ins.then_inc(E["lora2"], 1)

                    def heads_apart(n):
                        pool.wait_ge(E["ops"], n + 1)
                        for src, dst in ((B_T, BZ), (K_T, KZ)):
                            for e in range(2):
                                ins = pool.tensor_tensor(dst[e], src, same_head[:, e * HD:e * HD + 1].to_broadcast([P, T]),
                                                         ALU.mult)
                        ins.then_inc(E["heads_apart"], 1)

                    def turn(i, more):
                        if more:
                            pool.wait_ge(E["lora"], i + 1)
                            take_lora2(i + 1)
                        for u in range(8):
                            pool.wait_ge(d_low, i * 8 + u + 1)
                            pool.tensor_tensor(AKM[:, u, 0:P], AKM[:, u, 0:P], XX[:, u, P:2 * P], ALU.subtract)
                            pool.tensor_tensor(TT[:, u, :], XX[:, u, P:2 * P], ident, ALU.add).then_inc(d_akm, 1)
                        pool.wait_ge(E["yc"], i + 1)
                        pool.tensor_copy(V, v3[:, :, bass.ds(i * P, P)]).then_inc(E["val"], 1)
                        if more:
                            heads_apart(i + 1)

                    link = Chain(pool, pool_chain)
                    link(pool.memset(keep, 1.0))
                    link(pool.memset(keep.rearrange("p (c t) -> p c t", c=NC_R)[:, :, 0:1], 0.0))
                    link(pool.memset(MT, 0.0))
                    link(pool.tensor_copy(low_st_d, low_st))
                    for r in range(P // RB - 1):
                        link(pool.memset(low_st_d[r * RB:(r + 1) * RB, (r + 1) * RB:P], 0.0))
                    pool.tensor_copy(cols[:, 32:33], one_col).then_inc(consts.sem, 1)
                    take_lora2(0)
                    heads_apart(0)
                    turns(pool, turn)

                @block.tensor
                def _(pe):
                    def lora(u):
                        return pe.matmul(ps[:, u, strip], lora2[:, u // NT, :], h_wa[:, u % NT * P:(u % NT + 1) * P],
                                         start=True, stop=True)

                    def head_sums():
                        for j in range(NT):
                            ins = pe.matmul(ps[:, 0, 3 * P + 2 * j:3 * P + 2 * j + 2], norm[:, j * P:(j + 1) * P],
                                            same_head[:, 0:P:HD], start=True, stop=True)
                        return ins

                    def wide(j):
                        return pe.transpose(ps[:, j, strip], norm[:, j * P:(j + 1) * P], ident)

                    def turn_operand(n):
                        for j in range(NT):
                            if n < 3:
                                src = (A_T, B_T.rearrange(tile4, j=NT), K_T.rearrange(tile4, j=NT))[n]
                                pe.transpose(ps[:, TURNED[n], j * P:(j + 1) * P], src[:, j, :], ident)
                            else:
                                ins = pe.matmul(ps[:, TURNED[n], 2 * j:2 * j + 2], rkr[:, j * P:(j + 1) * P],
                                                same_head[:, 0:P:HD], start=True, stop=True)
                        if n == 3:
                            ins.then_inc(E["turned"], 1)

                    def turn(i, more):
                        pe.wait_ge(E["heads_apart"], i + 1)
                        for u, (e, j) in enumerate(units):
                            ins = pe.matmul(ps[:, 4 + e, j * P:(j + 1) * P], A_T[:, j, :],
                                            BZ[e][:, j * P:(j + 1) * P], start=True, stop=True)
                        ins.then_inc(E["low"], 1)
                        for u, (e, j) in enumerate(units):
                            if u == 0:
                                pe.wait_ge(E["tok"], i + 1)
                            if u == 4:
                                pe.wait_ge(E["lowm"], i + 1)
                            if u == 6:
                                pe.wait_ge(E["yc"], i + 1)
                            for n, src in enumerate((BZ, KZ)):
                                ins = pe.matmul(ps[:, u, 2 * n * P:2 * (n + 1) * P], src[e][:, j * P:(j + 1) * P],
                                                AR[:, j, :, :], start=True, stop=True)
                            ins.then_inc(p_akm, 1)
                        for r in range(ROUNDS):
                            for u in range(8):
                                if r == 0:
                                    pe.wait_ge(d_akm, i * 8 + u + 1)
                                else:
                                    pe.wait_ge(a_sq, i * 8 * ROUNDS + 8 * (r - 1) + u + 1)
                                    pe.wait_ge(d_tt, i * 8 * ROUNDS + 8 * (r - 1) + u + 1)
                                x, xt = XX[:, u, 0:P], XX[:, u, P:2 * P]
                                pe.matmul(ps[:, u, 0:P], xt, x, start=True, stop=True)
                                pe.matmul(ps[:, u, P:2 * P], x, xt, start=True, stop=True).then_inc(p_sq, 1)
                            if more and r == 0:
                                pe.wait_ge(E["lora2"], i + 2)
                            if more and r == 1:
                                pe.wait_ge(E["sq"], i + 2)
                            if more and r == 2:
                                pe.wait_ge(E["inverse"], i + 2)
                            if r == 3:
                                pe.wait_ge(E["val"], i + 1)
                            for u in range(8):
                                pe.wait_ge(a_sq, i * 8 * ROUNDS + 8 * r + u + 1)
                                ins = pe.matmul(ps[:, u, 2 * P:3 * P], XX[:, u, 0:P], TT[:, u, :], start=True, stop=True)
                                if more and r == 0:
                                    ins = lora(u)
                                if more and r == 1 and u == 0:
                                    ins = head_sums()
                                if more and r == 2 and u < NT:
                                    ins = wide(u)
                                if r == 3:
                                    e, j = units[u]
                                    ins = pe.matmul(ps[:, u, 3 * P:3 * P + HD], AKM[:, u, 2 * P:3 * P], V[:, j, rows_of(e)],
                                                    start=True, stop=True)
                                ins.then_inc(p_tt, 1)
                        def four(half, bank, lhs, rhs, done):
                            for u in range(4 * half, 4 * half + 4):
                                ins = pe.matmul(ps[:, bank + half, u % 4 * P:(u % 4 + 1) * P], lhs(u), rhs[:, u, :],
                                                start=True, stop=True)
                            ins.then_inc(done, 1)

                        def r2(u):
                            e, j = units[u]
                            return pe.matmul(ps[rows_of(e), 3, j * P:(j + 1) * P], QC[:, u, 0:HD], AKM[:, u, P:2 * P],
                                             start=True, stop=True)

                        pe.wait_ge(d_tt, (i + 1) * (8 * ROUNDS))
                        for half in range(2):
                            four(half, 1, lambda u: TT[:, u, :], RH, E["q"])
                        for half in range(2):
                            pe.wait_ge(E[("qc", "qc2")[half]], i + 1)
                            four(half, 5, lambda u: AKM[:, u, 0:P], QC, E["z"])
                        for half in range(2):
                            pe.wait_ge(E[("zc", "zc2")[half]], i + 1)
                            four(half, 1, lambda u: TT[:, u, :], Z, E["q2"])
                        pe.wait_ge(E["q2c"], 2 * i + 1)
                        for u in range(4):
                            r2(u)
                        pe.wait_ge(E["q2c"], 2 * i + 2)
                        r2(4)
                        for half in range(2):
                            hs = rows_of(half)
                            m = [ps[rows_of(e), 5 + half, j * HD:(j + 1) * HD] for e, j in units]
                            n = [ps[rows_of(e), 7 * (1 - half), j * HD:(j + 1) * HD] for e, j in units]
                            in_turn = [(u, *units[u]) for j in range(NT) for u in (j, NT + j)]
                            for u, e, j in in_turn:
                                pe.matmul(m[u], QC[hs, u, 0:HD], B_tok[hs, j, rows_of(e)], start=True, stop=True)
                            for u, e, j in in_turn:
                                pe.matmul(n[u], B_tok[hs, j, rows_of(e)], QC[hs, u, HD:P], start=True, stop=False)
                                ins = pe.matmul(n[u], K_tok[hs, j, rows_of(e)], V[hs, j, rows_of(e)], start=False, stop=True)
                            ins.then_inc(E["mn"], 1)
                        pe.wait_ge(E["mnc"], i + 1)
                        for c in range(1, NC_R + 1):
                            if 2 <= c < NC_R:
                                pe.wait_ge(d_s, i * (NC_R - 1) + c - 1)
                            if c < NC_R:
                                pe.matmul(ps[:, 1, c * HD:(c + 1) * HD], MT[:, c - 1, :], S[:, c - 1, :],
                                          start=True, stop=True).then_inc(p_s, 1)
                            if c <= 3:
                                ins = r2(c + 4)
                            if c == 3:
                                ins.then_inc(E["r2"], 1)
                            if more and c == 2:
                                pe.wait_ge(E["ops"], i + 2)
                            if more and 2 <= c <= 5:
                                turn_operand(c - 2)
                            e, j = units[c - 1]
                            o = ps[:, 4, (2 * j + e) * HD:(2 * j + e + 1) * HD]
                            pe.matmul(o, AKM[:, c - 1, P:2 * P], QC[:, c - 1, HD:P], start=True, stop=False)
                            ins = pe.matmul(o, AKM[:, c - 1, 3 * P:4 * P], V[:, j, rows_of(e)], start=False, stop=True)
                        ins.then_inc(E["y0"], 1)
                        pe.wait_ge(E["r2c"], i + 1)
                        pe.wait_ge(E["y0c"], i + 1)
                        pe.wait_ge(d_s, (i + 1) * (NC_R - 1))
                        if more:
                            pe.wait_ge(E["tok"], i + 2)
                        for e, j in units:
                            ins = pe.matmul(ps[:, 6 + e, j * P:(j + 1) * P], RQ[rows_of(e), j * P:(j + 1) * P],
                                            S[rows_of(e), 2 * j:2 * j + 2, :], start=True, stop=True)
                        ins.then_inc(E["yy"], 1)

                    pe.wait_ge(E["lora2"], 1)
                    for u in range(8):
                        ins = lora(u)
                    ins.then_inc(E["first_lora"], 1)
                    pe.wait_ge(E["sq"], 1)
                    pe.wait_ge(E["lora"], 1)
                    head_sums().then_inc(E["first_sums"], 1)
                    pe.wait_ge(E["inverse"], 1)
                    for j in range(NT):
                        ins = wide(j)
                    ins.then_inc(E["first_wide"], 1)
                    pe.wait_ge(E["ops"], 1)
                    for n in range(4):
                        turn_operand(n)
                    turns(pe, turn)

                @block.scalar
                def _(act):
                    def sigmoids(n):
                        act.wait_ge(E["lora"], n + 1)
                        act.wait_ge(E["par"], n + 1)
                        act.activation(logd, logd, ACT.Sigmoid, bias=pcol[:, W0:W0 + 1])
                        act.activation(lr, lr, ACT.Sigmoid, bias=pcol[:, A0:A0 + 1]).then_inc(E["sig"], 1)

                    def exponentials(n):
                        act.wait_ge(E["shift"], n + 1)
                        act.activation(decay, cum, ACT.Exp)
                        act.activation(inv, cum, ACT.Exp, scale=-1.0)
                        act.activation(before_d, before_d, ACT.Exp)
                        act.wait_ge(E["ssq"], n + 1)
                        act.activation(heads, heads, ACT.Sqrt).then_inc(E["exp"], 1)

                    def take_operands(n):
                        act.wait_ge(E["turned"], n + 1)
                        act.activation(RH.rearrange("p (e j) c -> p j e c", e=2)[:, :, :, 0:HD],
                                       ps[:, TURNED[0], :].rearrange("p (j e c) -> p j e c", j=NT, e=2), ACT.Copy)
                        for bank, dst in zip(TURNED[1:3], (B_tok, K_tok)):
                            act.activation(dst, ps[:, bank, :].rearrange(tile4, j=NT), ACT.Copy)
                        act.activation(k3[:, bass.ds(n, 1), 0:2 * NT], ps[:, TURNED[3], 0:2 * NT].unsqueeze(1), ACT.Copy)\
                           .then_inc(E["tok"], 1)

                    def turn(i, more):
                        act.wait_ge(E["yc"], i + 1)
                        act.activation(RQ.rearrange(tile4, j=NT), R_T, ACT.Copy)
                        for r in range(ROUNDS):
                            for u in range(8):
                                act.wait_ge(p_sq, i * 8 * ROUNDS + 8 * r + u + 1)
                                act.activation(XX[:, u, :], ps[:, u, 0:2 * P], ACT.Copy).then_inc(a_sq, 1)
                            if more and r == 0:
                                sigmoids(i + 1)
                            if more and r == 1:
                                exponentials(i + 1)
                        for bank, dst, done, taken in ((1, QC, "q", "qc"), (5, Z, "z", "zc")):
                            act.wait_ge(E[done], 2 * i + 1)
                            act.activation(dst[:, 0:4, :], ps[:, bank, :].rearrange("p (u c) -> p u c", u=4), ACT.Copy)\
                               .then_inc(E[taken], 1)
                        if more:
                            take_operands(i + 1)
                        act.wait_ge(E["y0"], i + 1)
                        act.activation(Y0, ps[:, 4, :].rearrange("p (j e c) -> p j e c", j=NT, e=2), ACT.Copy).then_inc(E["y0c"], 1)

                    sigmoids(0)
                    exponentials(0)
                    take_operands(0)
                    turns(act, turn)

                @block.vector
                def _(dve):
                    c0 = consts.total + 1

                    def take_lora(u):
                        return dve.tensor_copy((logd, lr)[u // NT][:, u % NT * P:(u % NT + 1) * P], ps[:, u, strip])

                    def take_sums():
                        return dve.tensor_copy(heads, ps[:, 0, 3 * P:3 * P + 2 * NT].rearrange("p (j e) -> p j e", j=NT))

                    def unit_kk(j):
                        kj = kk[:, j * P:(j + 1) * P]
                        return dve.tensor_tensor(kj, kj, ps[:, j, strip], ALU.mult)

                    def squares(n, link):
                        dve.tensor_copy(pcol, par[:, :, bass.ds(n, 1)].rearrange("p n o -> p (n o)")).then_inc(E["par"], 1)
                        dve.wait_ge(E["par"], n + 1)
                        link(dve.tensor_scalar(kk, tile_of(k3, n), pcol[:, K_K:K_K + 1], None, ALU.mult))
                        dve.tensor_tensor(norm, kk, kk, ALU.mult).then_inc(E["sq"], 1)

                    def log_decays(n, link):
                        dve.wait_ge(E["sig"], n + 1)
                        link(dve.tensor_scalar(logd, logd, -float(np.exp(-0.5)), None, ALU.mult))
                        link(dve.tensor_tensor_scan(cum, keep, logd, 0.0, ALU.mult, ALU.add))
                        dve.tensor_tensor(before_d, cum, logd, ALU.subtract).then_inc(E["shift"], 1)
                        link(dve.tensor_scalar(K_T, lr, 1.0, pcol[:, K_A:K_A + 1], ALU.subtract, ALU.mult))
                        link(dve.scalar_tensor_tensor(K_T, K_T, 1.0, tile_of(k3, n), ALU.add, ALU.mult))

                    def inverse_norms(n, link):
                        dve.wait_ge(E["exp"], n + 1)
                        link(dve.tensor_scalar(heads, heads, 1e-12, None, ALU.max))
                        link(dve.reciprocal(heads, heads))
                        dve.tensor_copy(norm.rearrange("p (j e c) -> p j e c", j=NT, e=2),
                                        heads.unsqueeze(3).to_broadcast([P, NT, 2, HD])).then_inc(E["inverse"], 1)

                    def operands(n, link):
                        dve.scalar_tensor_tensor(A_T, kk.rearrange(tile4, j=NT), -1.0, before_d.rearrange(tile4, j=NT), ALU.mult, ALU.mult)
                        link(dve.tensor_tensor(B_T, kk, lr, ALU.mult))
                        dve.tensor_tensor(B_T, B_T, inv, ALU.mult)
                        dve.tensor_tensor(R_T, tile_of(rT, n).rearrange(tile4, j=NT), decay.rearrange(tile4, j=NT), ALU.mult)
                        link(dve.scalar_tensor_tensor(rkr, tile_of(rT, n), pcol[:, R_K:R_K + 1], K_T, ALU.mult, ALU.mult))
                        link(dve.tensor_tensor(K_T, K_T, inv, ALU.mult))
                        dve.memset(spot, 0.0).then_inc(E["ops"], 1)

                    def turn(i, more):
                        link = LoopChain(dve, chain_v, PREPARE_LINKS, i, TURN_LINKS)
                        link(dve.tensor_copy(p_end, decay[:, RC - 1::RC]))
                        dve.wait_ge(E["low"], i + 1)
                        dve.tensor_tensor(XX[:, :, 0:P], ps[:, 4:6, :].rearrange("p b (u c) -> p (b u) c", u=4),
                                          low_ts.unsqueeze(1).to_broadcast([P, 8, P]), ALU.mult).then_inc(E["lowm"], 1)
                        for u in range(8):
                            dve.wait_ge(p_akm, i * 8 + u + 1)
                            dve.tensor_tensor(XX[:, u, P:2 * P], ps[:, u, 0:P], low_st_d, ALU.mult)
                            dve.tensor_tensor(AKM[:, u, :].rearrange("p (a c) -> p a c", a=2),
                                              ps[:, u, :].rearrange("p (a c) -> p a c", a=2),
                                              masks.unsqueeze(1).to_broadcast([P, 2, 2 * P]), ALU.mult).then_inc(d_low, 1)
                        if more:
                            squares(i + 1, link)
                        for r in range(ROUNDS):
                            for u in range(8):
                                dve.wait_ge(p_tt, i * 8 * ROUNDS + 8 * r + u + 1)
                                ins = dve.tensor_tensor(TT[:, u, :], TT[:, u, :], ps[:, u, 2 * P:3 * P], ALU.add)
                                if more and r == 0:
                                    ins = take_lora(u)
                                if more and r == 1 and u == 0:
                                    ins = take_sums()
                                if more and r == 2 and u < NT:
                                    ins = unit_kk(u)
                                if r == 3:
                                    ins = dve.tensor_copy(RH[:, u, HD:P], ps[:, u, 3 * P:3 * P + HD])
                                ins.then_inc(d_tt, 1)
                            if more and r == 0:
                                dve.memset(spot, 0.0).then_inc(E["lora"], 1)
                            if more and r == 1:
                                dve.memset(spot, 0.0).then_inc(E["ssq"], 1)
                            if more and r == 0:
                                log_decays(i + 1, link)
                            if more and r == 1:
                                inverse_norms(i + 1, link)
                            if more and r == 2:
                                link(dve.memset(spot, 0.0))
                                dve.wait_ge(E["tok"], i + 1)
                                operands(i + 1, link)
                        for bank, dst, done, taken in ((2, QC, "q", "qc2"), (6, Z, "z", "zc2")):
                            dve.wait_ge(E[done], 2 * i + 2)
                            dve.tensor_copy(dst[:, 4:8, :], ps[:, bank, :].rearrange("p (u c) -> p u c", u=4)).then_inc(E[taken], 1)
                        for half in range(2):
                            dve.wait_ge(E["q2"], 2 * i + 1 + half)
                            dve.wait_ge(E[("qc", "qc2")[half]], i + 1)
                            qc = QC[:, 4 * half:4 * half + 4, :]
                            dve.tensor_tensor(qc, qc, ps[:, 1 + half, :].rearrange("p (u c) -> p u c", u=4), ALU.add)\
                               .then_inc(E["q2c"], 1)
                        pe2 = p_end.rearrange("p (j h) -> p j h", h=2)
                        mt, nn = (m.rearrange("p (j h) i -> p j h i", h=2) for m in (MT, NN))
                        for half in range(2):
                            dve.wait_ge(E["mn"], 2 * i + 1 + half)
                            for e in range(2):
                                dve.tensor_tensor(mt[rows_of(e), :, half, e * HD:(e + 1) * HD],
                                                  ps[rows_of(e), 5 + half, 0:NT * HD].rearrange("p (j i) -> p j i", j=NT),
                                                  ident[rows_of(e), rows_of(e)].unsqueeze(1).to_broadcast([HD, NT, HD]), ALU.add)
                            ins = dve.tensor_tensor(nn[:, :, half, :], ps[:, 7 * (1 - half), 0:NT * HD].rearrange("p (j i) -> p j i", j=NT),
                                                    pe2[:, :, half].unsqueeze(2).to_broadcast([P, NT, HD]), ALU.mult)
                        link(ins)
                        dve.memset(S[:, 0, :], 0.0).then_inc(E["mnc"], 1)
                        for c in range(1, NC_R):
                            dve.wait_ge(p_s, i * (NC_R - 1) + c)
                            dve.scalar_tensor_tensor(S[:, c, :], ps[:, 1, c * HD:(c + 1) * HD], p_end[:, c - 1:c],
                                                     NN[:, c - 1, :], ALU.mult, ALU.add).then_inc(d_s, 1)
                            if c == 4:
                                dve.wait_ge(E["r2"], i + 1)
                                dve.tensor_tensor(RQ, RQ, ps[:, 3, :], ALU.add).then_inc(E["r2c"], 1)
                        dve.wait_ge(E["y0c"], i + 1)
                        dve.wait_ge(E["yy"], i + 1)
                        for e in range(2):
                            for h in range(2):
                                ins = dve.tensor_tensor(tile_of(rT, i)[rows_of(h), :].rearrange("p (j e v) -> p j e v", j=NT, e=2)[:, :, e, :],
                                                        ps[rows_of(h), 6 + e, :].rearrange("p (j v) -> p j v", j=NT)[:, :, rows_of(h)],
                                                        Y0[rows_of(h), :, e, :], ALU.add)
                        ins.then_inc(E["yc"], 1)

                    dve.memset(spot, 0.0).then_inc(E["yc"], 1)
                    dve.wait_ge(consts.sem, c0)
                    link = LoopChain(dve, chain_v, 0, 0, 0)
                    squares(0, link)
                    dve.wait_ge(E["first_lora"], 1)
                    for u in range(8):
                        ins = take_lora(u)
                    ins.then_inc(E["lora"], 1)
                    log_decays(0, link)
                    dve.wait_ge(E["first_sums"], 1)
                    take_sums().then_inc(E["ssq"], 1)
                    inverse_norms(0, link)
                    dve.wait_ge(E["first_wide"], 1)
                    for j in range(NT):
                        ins = unit_kk(j)
                    link(ins)
                    operands(0, link)
                    assert link.at == PREPARE_LINKS, link.at
                    turns(dve, turn)
            consts.take(1)

        def wkv_out_stage():
            y = arena[:, 0:NK * T].rearrange("p (n v) -> p n v", v=HD)
            by_tile = "p (c j v) -> p c j v"
            yc = arena[:, 0:NK * T].rearrange(by_tile, c=NK, j=NT)
            squares = arena[:, NK * T:2 * NK * T].rearrange("p (n v) -> p n v", v=HD)
            added = xt_mem[:, :].rearrange("p (n v) -> p n v", v=HD)
            added_c = xt_mem[:, :].rearrange(by_tile, c=NK, j=NT)
            halves = [slice(32 * n, 32 * (n + 1)) for n in range(2)]
            g2a, g2b, ln_g, ln_b = (view(arena, 3 * NK * T + n * D, D) for n in range(4))
            bonus_all = view(rows, 128, NK, NT, 2)
            mean, var = view(rows, 0, 64), view(rows, 64, 64)
            l0, x0, a0, m0, b0 = loaded.take(64), dve_a.take(4), act_a.take(3), mm.take(2 * NT), consts.take(1)

            def by_channel(row):
                return row.rearrange("p (c v) -> p c v", c=NK).unsqueeze(2).to_broadcast([P, NK, NT, P])

            with nc.Block() as block:
                @block.sync
                def _(sp):
                    sp.wait_ge(loaded.sem, l0 + 64)
                    stream_mixer(sp, mixer_at[2] + 8, mixer_at[2] + 12)

                @block.gpsimd
                def _(pool):
                    for dst, src in ((g2a, a["rw_g2_2"][0][0:P]), (g2b[0:GATE_LORA - P, :], a["rw_g2_2"][0][P:GATE_LORA]),
                                     (ln_g, a["rw_lnx_g_2"][0].partition_broadcast(P)),
                                     (ln_b, a["rw_lnx_b_2"][0].partition_broadcast(P))):
                        pool.dma_start(dst, src).then_inc(loaded.sem, 16)
                    link = Chain(pool, pool_chain)
                    pool.wait_ge(dve_a.sem, x0 + 1)
                    for c in range(NK):
                        ins = pool.tensor_tensor(added_c[:, c, :, :].rearrange("p j (e v) -> p j e v", e=2),
                                                 v3[:, :, c * P:(c + 1) * P].rearrange("p j (e v) -> p j e v", e=2),
                                                 bonus_all[:, c, :, :].unsqueeze(3).to_broadcast([P, NT, 2, HD]), ALU.mult)
                    link(ins)
                    pool.wait_ge(loaded.sem, l0 + 64)
                    pool.tensor_tensor(added_c, added_c, by_channel(ln_b), ALU.add).then_inc(consts.sem, 1)

                @block.tensor
                def _(pe):
                    pe.wait_ge(loaded.sem, l0 + 64)
                    for n in range(2 * NT):
                        j, c = n // 2, n % 2
                        pe.matmul(ps[:, n, :], h_g[:, j * P:(j + 1) * P], g2a[:, c * CH:(c + 1) * CH], start=True, stop=False)
                        pe.matmul(ps[:, n, :], h_g2[:, j * P:(j + 1) * P], g2b[0:GATE_LORA - P, c * CH:(c + 1) * CH],
                                  start=False, stop=True).then_inc(mm.sem, 1)

                @block.scalar
                def _(act):
                    for n, half in enumerate(halves):
                        act.wait_ge(dve_a.sem, x0 + 2 + n)
                        act.activation(squares[:, half, :], y[:, half, :], ACT.Square).then_inc(act_a.sem, 1)
                    act.wait_ge(dve_a.sem, x0 + 4)
                    act.activation(var, var, ACT.Sqrt, bias=eps_gn).then_inc(act_a.sem, 1)

                @block.vector
                def _(dve):
                    link = Chain(dve, dve_chain)
                    wide = [P, 32, HD]
                    dve.tensor_copy(bonus_all.rearrange("p c j e -> p c (j e)"), k3[:, :, 0:2 * NT]).then_inc(dve_a.sem, 1)
                    link(dve.tensor_reduce(mean, y, AX, ALU.add))
                    link(dve.tensor_scalar(mean, mean, 1.0 / HD, None, ALU.mult))
                    for half in halves:
                        dve.tensor_tensor(y[:, half, :], y[:, half, :], mean[:, half].unsqueeze(2).to_broadcast(wide), ALU.subtract)\
                           .then_inc(dve_a.sem, 1)
                    for n, half in enumerate(halves):
                        dve.wait_ge(act_a.sem, a0 + n + 1)
                        ins = dve.tensor_reduce(var[:, half], squares[:, half, :], AX, ALU.add)
                    link(ins)
                    dve.tensor_scalar(var, var, 1.0 / HD, None, ALU.mult).then_inc(dve_a.sem, 1)
                    dve.wait_ge(loaded.sem, l0 + 64)
                    link(dve.tensor_tensor(yc, yc, by_channel(ln_g), ALU.mult))
                    dve.wait_ge(act_a.sem, a0 + 3)
                    link(dve.reciprocal(var, var))
                    link(dve.tensor_tensor(y, y, var.unsqueeze(2).to_broadcast([P, 64, HD]), ALU.mult))
                    dve.wait_ge(consts.sem, b0 + 1)
                    link(dve.tensor_tensor(y, y, added, ALU.add))
                    for n in range(2 * NT):
                        j, c = n // 2, n % 2
                        dve.wait_ge(mm.sem, m0 + n + 1)
                        dve.tensor_tensor(yc[:, 4 * c:4 * c + 4, j, :], yc[:, 4 * c:4 * c + 4, j, :],
                                          ps[:, n, :].rearrange("p (c v) -> p c v", c=4), ALU.mult)

        def store_stage():
            o0 = stored.take(16)
            with nc.Block() as block:
                @block.sync
                def _(sp):
                    sp.dma_start(out[0].rearrange("(j p) d -> p j d", p=P), x_tok).then_inc(stored.sem, 16)
                    sp.wait_ge(stored.sem, o0 + 16)

        def program():
            start_stage()
            in_proj_stage()
            decay_stage()
            ssd_stage()
            attention_stage(1, lambda h, c: qT[HD * (h % 2):HD * (h % 2 + 1), h // 2, :],
                            lambda h, c: kT[:, h // 2, :], v_tok, HD,
                            lambda h, j: merged_a[:, j, h * HD:(h + 1) * HD], forget=True)
            mT = view(arena, 0, NK, T)
            transpose_stage(lambda j, k: (merged_s if k < 4 else merged_a)[:, j, (k % 4) * P:(k % 4 + 1) * P], mT)
            project_out_stage(0, ALPHA_1, mT, a["ln1_g"][0], a["ln1_b"][0])
            if stop == "h1":
                return
            moe_stage(0, ALPHA_1, a["ln2_g"][0], a["ln2_b"][0], False)
            if stop == "x1":
                return
            qkv_stage()
            attention_stage(2, lambda h, c: q2[HD * c:HD * (c + 1), h, :], lambda h, c: k2[HD * c:HD * (c + 1), h, :],
                            v2, 2 * HD, lambda h, j: o2[:, j, h * P:(h + 1) * P], lam=lam)
            subln_stage()
            transpose_stage(lambda j, k: o2[:, j, k * P:(k + 1) * P], mT)
            project_out_stage(1, ALPHA_2, mT, a["ln1_g_2"][0], a["ln1_b_2"][0])
            if stop == "h2":
                return
            moe_stage(1, ALPHA_2, a["ln2_g_2"][0], a["ln2_b_2"][0], False)
            if stop == "x2":
                return
            rkv_stage()
            wkv_stage()
            wkv_out_stage()
            mT3 = view(arena, NK * T, NK, T)
            y3 = rT.rearrange("p c (j v) -> p c j v", j=NT)
            transpose_stage(lambda j, k: y3[:, k, j, :], mT3)
            project_out_stage(2, ALPHA_2, mT3, a["ln1_g_2"][1], a["ln1_b_2"][1])
            if stop == "h3":
                return
            moe_stage(2, ALPHA_2, a["ln2_g_2"][1], a["ln2_b_2"][1], True)

        program()
        if stop:
            store_stage()


_INS = ["x", "w_in", "b_in", "conv_w", "conv_b", "a_log", "d_skip", "ssd_norm_g", "w_out", "ln1_g", "ln1_b",
        "router_group_w", "router_group_b", "router_expert_w", "router_expert_b", "w_gate", "w_up", "w_down",
        "ln2_g", "ln2_b", "ln1_g_2", "ln1_b_2", "ln2_g_2", "ln2_b_2", "attn_w_qkv_2", "attn_w_o_2", "attn_lambda_2",
        "attn_subln_g_2", "rw_mu_2", "rw_w_rkv_2", "rw_w_o_2", "rw_w0_2", "rw_w1_2", "rw_w2_2", "rw_a0_2", "rw_a1_2",
        "rw_a2_2", "rw_g1_2", "rw_g2_2", "rw_k_k_2", "rw_k_a_2", "rw_r_k_2", "rw_lnx_g_2", "rw_lnx_b_2",
        "rw_v0_2", "rw_v1_2", "rw_v2_2",
        "moe_rg_w_2", "moe_rg_b_2", "moe_re_w_2", "moe_re_b_2", "moe_w_gu_2", "moe_w_down_2"]
_OUT_SHAPE = (1, T, D)
_STOP = None


def kernel(**inputs):
    import concourse.bacc as bacc
    from concourse.bass_utils import run_bass_kernel_spmd

    nc = bacc.Bacc("TRN2", target_bir_lowering=False, num_devices=1)
    arrays, aps = {}, {}
    for name in _INS:
        arr = np.ascontiguousarray(inputs[name])
        if not arr.size:
            continue
        arrays[f"in_{name}"] = arr
        aps[name] = nc.dram_tensor(f"in_{name}", arr.shape, mybir.dt.from_np(arr.dtype), kind="ExternalInput").ap()
    out = nc.dram_tensor("out", _OUT_SHAPE, F32, kind="ExternalOutput").ap()
    build(nc, aps, out, _STOP)
    r = run_bass_kernel_spmd(nc, [arrays], core_ids=[0])
    return r.results[0]["out"]
```
